# Optimizing a Trainium2 kernel written in Bass

```python
import jax, jax.numpy as jnp
from jax import lax
import numpy as np

D_MODEL = 1024
BATCH = 1
SEQ = 512
DEPTH = 1
DEC_BATCH = 1
DEC_SEQ = 64
PAST_LEN = 256

CHUNK = 64
D_CONV = D_MODEL
CONV_A_WIDTH = 3
N_HEADS = 8
HEAD_K = 128
HEAD_V = 128
KEY_DIM = N_HEADS * HEAD_K
VAL_DIM = N_HEADS * HEAD_V
QKV_DIM = 2 * KEY_DIM + VAL_DIM
CONV_B_WIDTH = 4
D_FF = 4 * D_MODEL
N_ADA = 6
EPS = 1e-6
IN_SPLITS = (D_CONV, D_CONV, D_CONV, KEY_DIM, KEY_DIM, VAL_DIM, VAL_DIM, N_HEADS, N_HEADS, D_MODEL, D_MODEL)
D_IN = sum(IN_SPLITS)

kernel_name = 'hybrid_shortconv_gdn_stream_step'

def rmsnorm(x, g):
    xf = x.astype(jnp.float32)
    y = xf * lax.rsqrt(jnp.mean(xf * xf, axis=-1, keepdims=True) + EPS)
    return (y * g.astype(jnp.float32)).astype(x.dtype)

def l2norm(x):
    return x * lax.rsqrt(jnp.sum(x * x, axis=-1, keepdims=True) + EPS)

def causal_dwconv(x, past, w):
    width = w.shape[0]
    t = x.shape[1]
    xp = jnp.concatenate([past.astype(x.dtype), x], axis=1)
    y = xp[:, 0:t] * w[0]
    for j in range(1, width):
        y = y + xp[:, j:j + t] * w[j]
    return y, xp[:, -(width - 1):]

def gated_delta_rule(q, k, v, g, beta, s0):
    b_, t, h, dk = q.shape
    dv = v.shape[-1]
    blen = min(CHUNK, t)
    n = t // blen

    def blk(a):
        a = a.reshape((b_, n, blen) + a.shape[2:])
        return jnp.moveaxis(jnp.moveaxis(a, 3, 2), 1, 0)

    qc, kc, vc, gc, bc = blk(q), blk(k), blk(v), blk(g), blk(beta)
    gcum = jnp.cumsum(gc, axis=-1)
    idx = jnp.arange(blen)
    incl = idx[:, None] >= idx[None, :]
    strict = idx[:, None] > idx[None, :]
    decay = jnp.exp(jnp.where(incl, gcum[..., :, None] - gcum[..., None, :], -jnp.inf))
    kk = jnp.einsum('nbhid,nbhjd->nbhij', kc, kc)
    a_mat = jnp.where(strict, bc[..., :, None] * kk * decay, 0.0)
    eye = jnp.eye(blen, dtype=q.dtype)
    rhs = jnp.concatenate([kc * (bc * jnp.exp(gcum))[..., None], vc * bc[..., None]], axis=-1)
    sol = lax.linalg.triangular_solve(eye + a_mat, rhs, left_side=True, lower=True)
    w_c, u_c = sol[..., :dk], sol[..., dk:]
    qk = jnp.where(incl, jnp.einsum('nbhid,nbhjd->nbhij', qc, kc) * decay, 0.0)
    q_dec = qc * jnp.exp(gcum)[..., None]
    k_dec = kc * jnp.exp(gcum[..., -1:] - gcum)[..., None]
    g_last = jnp.exp(gcum[..., -1])

    def step(s, xs):
        w_i, u_i, qk_i, qd_i, kd_i, gl_i = xs
        v_new = u_i - jnp.einsum('bhld,bhde->bhle', w_i, s)
        o = jnp.einsum('bhld,bhde->bhle', qd_i, s) + jnp.einsum('bhij,bhje->bhie', qk_i, v_new)
        s = s * gl_i[..., None, None] + jnp.einsum('bhld,bhle->bhde', kd_i, v_new)
        return s, o

    s_fin, o = lax.scan(step, s0, (w_c, u_c, qk, q_dec, k_dec, g_last))
    o = jnp.moveaxis(jnp.moveaxis(o, 0, 1), 2, 3).reshape(b_, t, h, dv)
    return o, s_fin

def token_mixer(hn, conv_a_past, qkv_past, s0, w_in, conv_a_w, conv_qkv_w, a_log, dt_bias, out_norm_g, w_a_out, w_b_out, w_o):
    b_, t, _ = hn.shape
    proj = hn @ w_in
    split_at = np.cumsum(IN_SPLITS)[:-1].tolist()
    pb, pc, ph, q, k, v, z, a, bb, ga, gb = jnp.split(proj, split_at, axis=-1)
    ya, conv_a_new = causal_dwconv(pc * ph, conv_a_past, conv_a_w)
    ya = (pb * ya) @ w_a_out
    qkv, qkv_new = causal_dwconv(jnp.concatenate([q, k, v], axis=-1), qkv_past, conv_qkv_w)
    qkv = jax.nn.silu(qkv).astype(jnp.float32)
    q, k, v = jnp.split(qkv, [KEY_DIM, 2 * KEY_DIM], axis=-1)
    q = l2norm(q.reshape(b_, t, N_HEADS, HEAD_K)) * (HEAD_K ** -0.5)
    k = l2norm(k.reshape(b_, t, N_HEADS, HEAD_K))
    v = v.reshape(b_, t, N_HEADS, HEAD_V)
    g = -jnp.exp(a_log.astype(jnp.float32)) * jax.nn.softplus(a.astype(jnp.float32) + dt_bias.astype(jnp.float32))
    beta = jax.nn.sigmoid(bb.astype(jnp.float32))
    o, s_new = gated_delta_rule(q, k, v, g, beta, s0.astype(jnp.float32))
    o = rmsnorm(o, out_norm_g) * jax.nn.silu(z.reshape(b_, t, N_HEADS, HEAD_V).astype(jnp.float32))
    yb = o.reshape(b_, t, VAL_DIM).astype(hn.dtype) @ w_b_out
    y = (jax.nn.sigmoid(ga) * ya + jax.nn.sigmoid(gb) * yb) @ w_o
    return y, conv_a_new, qkv_new, s_new.astype(hn.dtype)

def trunk(x, c, conv_a_st, conv_qkv_st, delta_st, ada_w, ada_b, norm1_g, norm2_g, w_in, conv_a_w, conv_qkv_w,
          a_log, dt_bias, out_norm_g, w_a_out, w_b_out, w_o, w_ff1, w_ff2, final_ada_w, final_ada_b, final_norm_g):
    c_act = jax.nn.silu(c)
    new_a, new_qkv, new_s = [], [], []
    for l in range(DEPTH):
        mod = (c_act @ ada_w[l] + ada_b[l])[:, None, :]
        sh1, sc1, gt1, sh2, sc2, gt2 = jnp.split(mod, N_ADA, axis=-1)
        hn = rmsnorm(x, norm1_g[l]) * (1 + sc1) + sh1
        y, ca, cq, s = token_mixer(hn, conv_a_st[l], conv_qkv_st[l], delta_st[l], w_in[l], conv_a_w[l], conv_qkv_w[l],
                                   a_log[l], dt_bias[l], out_norm_g[l], w_a_out[l], w_b_out[l], w_o[l])
        x = x + gt1 * y
        hn = rmsnorm(x, norm2_g[l]) * (1 + sc2) + sh2
        x = x + gt2 * (jnp.square(jax.nn.relu(hn @ w_ff1[l])) @ w_ff2[l])
        new_a.append(ca)
        new_qkv.append(cq)
        new_s.append(s)
    modf = (c_act @ final_ada_w + final_ada_b)[:, None, :]
    shf, scf = jnp.split(modf, 2, axis=-1)
    y = rmsnorm(x, final_norm_g) * (1 + scf) + shf
    return y, jnp.stack(new_a), jnp.stack(new_qkv), jnp.stack(new_s)

def setup_inputs(seed: int = 0) -> dict:
    key = jax.random.key(seed)
    ks = jax.random.split(key, 32)
    nrm = lambda k, shape, s: jax.random.normal(k, shape, jnp.float32) * s
    L = DEPTH
    dt = jnp.exp(jax.random.uniform(ks[20], (L, N_HEADS), jnp.float32, np.log(1e-3), np.log(1e-1)))
    return {
        'x_prompt': nrm(ks[0], (BATCH, SEQ, D_MODEL), 1.0),
        'x_sample': nrm(ks[1], (DEC_BATCH, DEC_SEQ, D_MODEL), 1.0),
        'cache_conv_a': nrm(ks[2], (L, DEC_BATCH, CONV_A_WIDTH - 1, D_CONV), 1.0),
        'cache_conv_qkv': nrm(ks[3], (L, DEC_BATCH, CONV_B_WIDTH - 1, QKV_DIM), 1.0),
        'state_delta': nrm(ks[4], (L, DEC_BATCH, N_HEADS, HEAD_K, HEAD_V), 0.1),
        'c_prompt': nrm(ks[5], (BATCH, D_MODEL), 1.0),
        'c_sample': nrm(ks[6], (DEC_BATCH, D_MODEL), 1.0),
        'ada_w': nrm(ks[7], (L, D_MODEL, N_ADA * D_MODEL), D_MODEL ** -0.5),
        'ada_b': nrm(ks[8], (L, N_ADA * D_MODEL), 0.02),
        'norm1_g': 1.0 + nrm(ks[9], (L, D_MODEL), 0.02),
        'norm2_g': 1.0 + nrm(ks[10], (L, D_MODEL), 0.02),
        'w_in': nrm(ks[11], (L, D_MODEL, D_IN), D_MODEL ** -0.5),
        'conv_a_w': nrm(ks[12], (L, CONV_A_WIDTH, D_CONV), CONV_A_WIDTH ** -0.5),
        'conv_qkv_w': nrm(ks[13], (L, CONV_B_WIDTH, QKV_DIM), CONV_B_WIDTH ** -0.5),
        'a_log': jnp.log(jax.random.uniform(ks[14], (L, N_HEADS), jnp.float32, 1.0, 16.0)),
        'dt_bias': dt + jnp.log(-jnp.expm1(-dt)),
        'out_norm_g': 1.0 + nrm(ks[15], (L, HEAD_V), 0.02),
        'w_a_out': nrm(ks[16], (L, D_CONV, D_MODEL), D_CONV ** -0.5),
        'w_b_out': nrm(ks[17], (L, VAL_DIM, D_MODEL), VAL_DIM ** -0.5),
        'w_o': nrm(ks[18], (L, D_MODEL, D_MODEL), D_MODEL ** -0.5),
        'w_ff1': nrm(ks[19], (L, D_MODEL, D_FF), D_MODEL ** -0.5),
        'w_ff2': nrm(ks[21], (L, D_FF, D_MODEL), D_FF ** -0.5),
        'final_ada_w': nrm(ks[22], (D_MODEL, 2 * D_MODEL), D_MODEL ** -0.5),
        'final_ada_b': nrm(ks[23], (2 * D_MODEL,), 0.02),
        'final_norm_g': 1.0 + nrm(ks[24], (D_MODEL,), 0.02),
    }

def reference(x_prompt, x_sample, cache_conv_a, cache_conv_qkv, state_delta, c_prompt, c_sample, ada_w, ada_b,
              norm1_g, norm2_g, w_in, conv_a_w, conv_qkv_w, a_log, dt_bias, out_norm_g, w_a_out, w_b_out, w_o,
              w_ff1, w_ff2, final_ada_w, final_ada_b, final_norm_g):
    dt_ = x_prompt.dtype
    zero_a = jnp.zeros((DEPTH, BATCH, CONV_A_WIDTH - 1, D_CONV), dt_)
    zero_qkv = jnp.zeros((DEPTH, BATCH, CONV_B_WIDTH - 1, QKV_DIM), dt_)
    zero_s = jnp.zeros((DEPTH, BATCH, N_HEADS, HEAD_K, HEAD_V), dt_)
    y_prompt, conv_a_p, conv_qkv_p, delta_p = trunk(
        x_prompt, c_prompt, zero_a, zero_qkv, zero_s, ada_w, ada_b, norm1_g, norm2_g, w_in, conv_a_w, conv_qkv_w,
        a_log, dt_bias, out_norm_g, w_a_out, w_b_out, w_o, w_ff1, w_ff2, final_ada_w, final_ada_b, final_norm_g)
    y_sample, conv_a_s, conv_qkv_s, delta_s = trunk(
        x_sample, c_sample, cache_conv_a, cache_conv_qkv, state_delta, ada_w, ada_b, norm1_g, norm2_g, w_in,
        conv_a_w, conv_qkv_w, a_log, dt_bias, out_norm_g, w_a_out, w_b_out, w_o, w_ff1, w_ff2, final_ada_w,
        final_ada_b, final_norm_g)
    return (y_prompt, y_sample, conv_a_p, conv_qkv_p, delta_p, conv_a_s, conv_qkv_s, delta_s)


_drawn_inputs = setup_inputs


def setup_inputs(seed=0):
    import zlib

    import numpy as np

    out = dict(_drawn_inputs(seed))
    spreads = {}
    factors = {'norm2_g': 4.569,
     'out_norm_g': 22.59,
     'final_norm_g': 28.458,
     'final_ada_b': 3.03,
     'cache_conv_a': 5.16}
    for name, (base, spread) in spreads.items():
        noise = np.random.default_rng([zlib.crc32(name.encode()), seed]).standard_normal(out[name].shape)
        drawn = base * np.exp(spread * noise) if base else spread * noise
        out[name] = __import__('jax').numpy.asarray(drawn.astype(out[name].dtype))
    for name, factor in factors.items():
        out[name] = (out[name] * factor).astype(out[name].dtype)
    return out
```

```python
import concourse.bass as bass
from concourse import mybir
from concourse.bass import ds

F32 = mybir.dt.float32
F32R = mybir.dt.float32r
ALU = mybir.AluOpType
ACT = mybir.ActivationFunctionType

P = 128
D = 1024
KT = D // P
TP, TS = 512, 64
T = TP + TS
HALF = T // 2
CH = 64
NCH = T // CH
H = 8
HP = H // 2
WA, WB = 3, 4
LEVELS = 6
NEXP = 5
EPS = 1e-6
NQKV = 24
DFF = 4096

C_PB, C_PC, C_PH, C_QKV, C_Z, C_AB, C_GA, C_GB = 0, 1024, 2048, 3072, 6144, 7168, 7184, 8208

N_QKV, N_MIX, N_TAIL, N_WA, N_WB, N_WO, N_FF = 0, 24, 56, 72, 80, 88, 96
N_ALL = 160
RAW, SLOT = 4, 2

VEC = {}
_at = 0
for _name, _n in (("conv_qkv_w", WB * NQKV), ("conv_a_w", WA * KT), ("norm1_g", KT),
                  ("cache_qkv", (WB - 1) * NQKV), ("cache_a", (WA - 1) * KT), ("norm2_g", KT), ("final_g", KT),
                  ("out_g", 1), ("c_p", KT), ("c_s", KT), ("pad", 7),
                  ("ada_b", 6 * KT), ("final_b", 2 * KT)):
    VEC[_name] = (_at, _n)
    _at += _n
NVEC = _at


class Chain:

    def __init__(self, eng, sem):
        self.eng, self.sem, self.n, self.base = eng, sem, 0, 0

    def link(self, ins):
        ins.then_inc(self.sem, 1)
        self.n += 1
        self.wait()

    def wait(self):
        self.eng.wait_ge(self.sem, self.base + self.n)

    def note(self, ins):
        ins.then_inc(self.sem, 1)
        self.n += 1

    def loop(self, i, per):
        self.base, self.start, self.per = self.base + self.n + i * per, self.base + self.n, per
        self.n = 0

    def end(self, passes):
        assert self.n == self.per, (self.n, self.per)
        self.base, self.n = self.start + passes * self.per, 0


def whole(eng, value):
    return value if isinstance(value, int) else eng.compute_val(value)


def build(nc, t_in, t_out):
    SB0 = -(-nc.sbuf_base // 32) * 32
    cur = [SB0]

    def sb(name, shape, dt=F32, at=None):
        size = 4
        for s in shape[1:]:
            size *= s
        size = -(-size // 32) * 32
        if at is None:
            at = cur[0]
            cur[0] += size
        return nc.alloc_sbuf_tensor_at(name, shape, dt, offset=at)

    def region(size):
        at = cur[0]
        cur[0] += -(-size // 32) * 32
        return at

    TILE8 = KT * T * 4

    r_x = region(TILE8)
    xT = sb("xT", [P, KT, T], at=r_x)
    a_hi = sb("a_hi", [P, KT, T], F32R)
    a_lo = sb("a_lo", [P, KT, T], F32R)
    w_raw = sb("w_raw", [P, RAW, KT, P])
    w_hi = sb("w_hi", [P, SLOT, KT, P], F32R)
    w_lo = sb("w_lo", [P, SLOT, KT, P], F32R)
    r_q, r_k, r_v, r_u = region(TILE8), region(TILE8), region(TILE8), region(TILE8)
    qkv = sb("qkv", [P, NQKV, T], at=r_q)
    Q, K, V = qkv[:, 0:8, :], qkv[:, 8:16, :], qkv[:, 16:24, :]
    U = sb("U", [P, KT, T], at=r_u)
    b_hi = sb("b_hi", [P, KT, T], F32R, at=r_u)
    b_lo = sb("b_lo", [P, KT, T], F32R, at=r_v)
    f_hi = [sb("f0_hi", [P, KT, T], F32R, at=r_q), sb("f1_hi", [P, KT, T], F32R, at=r_v)]
    f_lo = [sb("f0_lo", [P, KT, T], F32R, at=r_k), sb("f1_lo", [P, KT, T], F32R, at=r_u)]
    ada0_w = sb("ada0_w", [P, KT, 2 * D], at=r_q)
    x_back = sb("x_back", [P, KT, T], at=r_q)
    y_fm = sb("y_fm", [P, KT, T], at=r_q)
    y_tok = sb("y_tok", [P, 5, D], at=r_k)

    ident = sb("ident", [P, P])
    ones = sb("ones", [P, P])
    id64 = sb("id64", [P, CH])
    neg = sb("neg", [P, CH])
    lvl = sb("lvl", [P, LEVELS, CH])
    vecs = sb("vecs", [P, NVEC])
    mod = sb("mod", [P, 4, 16, 2])
    scales = sb("scales", [P, 3, KT, 2])
    rows = sb("rows", [P, T])
    r_rows = cur[0] - T * 4
    c_act = sb("c_act", [P, KT, 2])
    mrow_l = sb("mrow_l", [P, 512], at=r_rows)
    tokv = sb("tokv", [P, NCH, 16])
    tails = sb("tails", [P, 2, (WB - 1) * NQKV + (WA - 1) * KT])
    bias = sb("bias", [P, 8])
    r_xp = region(2 * 584 * 4)
    xp = sb("xp", [P, 2, 584], at=r_xp)
    r_acc = region(2 * 584 * 4)
    acc = sb("acc", [P, 2, 584], at=r_acc)
    r_ds = cur[0]
    x_tok = sb("x_tok", [P, 5, D], at=r_ds)
    ab_raw = sb("ab_raw", [P, KT, CH], at=r_ds + 20480)
    ab_hi = sb("ab_hi", [P, KT, CH], F32R, at=r_ds + 22528)
    ab_lo = sb("ab_lo", [P, KT, CH], F32R, at=r_ds + 24576)
    vrows = sb("vrows", [P, 3, P], at=r_ds + 26624)
    mrow = sb("mrow", [P, 512], at=r_ds + 28160)
    rstd1 = sb("rstd1", [P, T], at=r_ds + 30208)
    ab_sb, ab_e, ab_sp, row_g, row_e, row_b, cmask = (sb(f"row{i}", [P, T], at=r_ds + i * T * 4) for i in range(7))
    sq = sb("sq", [P, 2, H, CH], at=r_ds)
    vn = sb("vn", [P, HP, P], at=r_ds)
    nw = sb("nw", [P, 2, HP, CH], at=r_ds + 2048)
    kq = sb("kq", [P, 2, H, CH], at=r_ds + 4096)
    vc = sb("vc", [P, H, CH], at=r_ds + 8192)
    qd = sb("qd", [P, H, CH], at=r_ds + 8192)
    eg = sb("eg", [P, H, CH], at=r_ds + 10240)
    dec = sb("dec", [P, HP, CH], at=r_ds + 12288)
    decb = sb("decb", [P, HP, CH], at=r_ds + 13312)
    p1 = sb("p1", [P, HP, CH], at=r_ds + 13312)
    at_ = sb("at", [P, HP, CH], at=r_ds + 14336)
    qkt = sb("qkt", [P, HP, CH], at=r_ds + 15360)
    nb = sb("nb", [P, 3, HP, CH], at=r_ds + 16384)
    mm = sb("mm", [P, 2, HP, CH], at=r_ds + 19456)
    kbe = sb("kbe", [P, HP, P], at=r_ds + 21504)
    kdt = sb("kdt", [P, HP, P], at=r_ds + 23552)
    vb = sb("vb", [P, HP, P], at=r_ds + 25600)
    st = sb("st", [P, H, P], at=r_ds + 27648)
    AS = 3
    ada_w = sb("ada_w", [P, AS, 2 * D], at=r_ds)
    rs = sb("rs", [P, 2, T], at=r_ds + 24576)
    og = [sb("og_0", [P, T], at=r_rows), sb("og_1", [P, T], at=r_ds + 29184)]
    rstd2 = sb("rstd2", [P, T], at=r_ds + 24576)
    tail_rows = [sb(f"tail_rows{g}", [P, P], at=r_ds + 29184 + 512 * g) for g in range(2)]
    assert r_ds + 32512 <= nc.sbuf_usable_end, (r_ds + 32512, nc.sbuf_usable_end)

    gp = nc.alloc_psum_tensor("gp", [P, 4, 512], F32)
    dp = nc.alloc_psum_tensor("dp", [P, 4, 512], F32)
    B0, B1, B2, B3 = (dp[:, i, :] for i in range(4))

    x_spill = nc.dram_tensor("x_spill", [P, KT, T], F32, kind="Internal").ap()

    names = """rows_in x_in ab_in s_in s_out pool_ready consts zeros_ready
        dve_own act_own pool_own
        vecs_t vecs_done xt_ready xt_done sq_done ss_all rstd_done t_done hi_split h_ready c_act ada0_used row_v row_a
        ada_rows ada_row_sb ada_t mod_done ada_used
        ab_split ab_hi_done ab_ready ab_rows tok_t tok_done spilled x_back_in
        w_hi_done w_lo_done tile_done bank_free
        pads_done tails_done acc_free conv_done qkv_done
        pc_sb ph_sb pb_sb prod_done u_done prod_free pads_a
        o_free s_done sq_ready bc_ready ss_ready eg_done rkq_done kq_done vc_done dd_done dec_done decb_done
        tr_ready kkqk_ready tokmul_done at_done nb_done mt_done m0_ready m0_done p1_ready p1_done x_ready m_done
        wt_ready nw_done vn_ready vn_done o_ready o_done ds_ready qd_done
        z_done ga_done u_hi u_split tmp_sb tmp_free osq_done oss_ready rs_done og_done og_hi og_split
        t2_done y_done y_hi y_split x1_done sq2_done f_done f_hi_done f_split
        caches_out yo_done yt_ready yt_done out_done tail_t tail_sb""".split()
    S = {n: nc.alloc_semaphore(n) for n in names}
    raw_full = [nc.alloc_semaphore(f"w_raw_full{i}") for i in range(RAW)]
    ada_full = [nc.alloc_semaphore(f"ada_full{i}") for i in range(8)]
    late_full = [nc.alloc_semaphore(f"late_full{i}") for i in range(3)]

    A = t_in
    w_in, w_a, w_b, w_o = A["w_in"][0], A["w_a_out"][0], A["w_b_out"][0], A["w_o"][0]
    w_ff1, w_ff2 = A["w_ff1"][0], A["w_ff2"][0]

    def wt(w, col, row=0):
        return w.rearrange("(k p) n -> p k n", p=P)[:, ds(row, KT) if not isinstance(row, int) else slice(row, row + KT),
                                                    ds(col, P)]

    ada_v = A["ada_w"][0].rearrange("(k p) n -> p k n", p=P)
    fin_v = A["final_ada_w"].rearrange("(k p) n -> p k n", p=P)

    def vec(name, j=0):
        return vecs[:, VEC[name][0] + j:VEC[name][0] + j + 1]

    block = nc.Block()
    block.__enter__()

    @block.sync
    def _(sp):
        def row(name, src):
            at, n = VEC[name]
            sp.dma_start(vrows[at % P:at % P + n, at // P, :], src).then_inc(S["rows_in"], 16)

        row("c_p", A["c_prompt"].rearrange("b (n p) -> (b n) p", p=P))
        row("c_s", A["c_sample"].rearrange("b (n p) -> (b n) p", p=P))
        row("conv_qkv_w", A["conv_qkv_w"][0].rearrange("j (n p) -> (j n) p", p=P))
        row("conv_a_w", A["conv_a_w"][0].rearrange("j (n p) -> (j n) p", p=P))
        row("norm1_g", A["norm1_g"].rearrange("l (n p) -> (l n) p", p=P))
        row("cache_qkv", A["cache_conv_qkv"][0, 0].rearrange("j (n p) -> (j n) p", p=P))
        row("cache_a", A["cache_conv_a"][0, 0].rearrange("j (n p) -> (j n) p", p=P))
        row("norm2_g", A["norm2_g"].rearrange("l (n p) -> (l n) p", p=P))
        row("final_g", A["final_norm_g"].rearrange("(n p) -> n p", p=P))
        row("out_g", A["out_norm_g"])
        row("pad", A["norm2_g"].rearrange("l (n p) -> (l n) p", p=P)[0:7])
        row("ada_b", A["ada_b"].rearrange("l (n p) -> (l n) p", p=P))
        row("final_b", A["final_ada_b"].rearrange("(n p) -> n p", p=P))
        sp.dma_start(x_tok[:, 0:4, :], A["x_prompt"][0].rearrange("(t p) d -> p t d", p=P)).then_inc(S["x_in"], 16)
        sp.dma_start(x_tok[0:TS, 4, :], A["x_sample"][0]).then_inc(S["x_in"], 16)
        for k in range(KT):
            sp.dma_start(ada0_w[:, k, :], ada_v[:, k, 0:2 * D]).then_inc(ada_full[k], 16)
        sp.wait_ge(S["zeros_ready"], 1)
        v = w_in.rearrange("(k p) n -> p k n", p=P)
        with nc.allow_non_contiguous_dma(reason="16 columns"):
            sp.dma_start(ab_raw[:, :, 0:8], v[:, :, C_AB:C_AB + 8]).then_inc(S["ab_in"], 16)
            sp.dma_start(ab_raw[:, :, 32:40], v[:, :, C_AB + 8:C_AB + 16]).then_inc(S["ab_in"], 16)
            sp.dma_start(bias[0:H, 0:1], A["dt_bias"].rearrange("l h -> h l")).then_inc(S["ab_in"], 16)
            sp.dma_start(bias[0:H, 1:2], A["a_log"].rearrange("l h -> h l")).then_inc(S["ab_in"], 16)

        def load(n, group, j, src):
            if not (isinstance(group, int) and group == 0):
                value = whole(sp, n - 3)
                sp.wait_ge(S["zeros_ready"], 1)
                sp.wait_ge(S["w_lo_done"], value)
            sp.dma_start(w_raw[:, j, :, :], src).then_inc(raw_full[j], 16)

        for j in range(4):
            load(j, 0, j, wt(w_in, C_QKV + j * P))
        sp.wait_ge(S["xt_done"], KT)
        sp.dma_start(x_spill, xT[:, :, :]).then_inc(S["spilled"], 16)
        with sp.Fori(1, NQKV // 4) as i:
            for j in range(4):
                load(4 * i + j, i, j, wt(w_in, C_QKV + j * P + i * (4 * P)))
        with sp.Fori(0, KT) as i:
            for j, c in enumerate((C_PC, C_PH, C_PB, C_GA)):
                load(N_MIX + 4 * i + j, i + 6, j, wt(w_in, c + i * P))
        with sp.Fori(0, KT // 2) as i:
            for j, c in enumerate((C_Z, C_GB, C_Z + P, C_GB + P)):
                load(N_TAIL + 4 * i + j, i + 14, j, wt(w_in, c + i * (2 * P)))

        def group8(n0, w, col=0, row=0):
            with sp.Fori(0, 2) as i:
                for j in range(4):
                    load(n0 + 4 * i + j, i + n0 // 4, j, wt(w, col + j * P + i * (4 * P), row))

        group8(N_WA, w_a)
        group8(N_WB, w_b)
        sp.wait_ge(S["spilled"], 16)
        sp.wait_ge(S["og_split"], 1 + KT)
        sp.dma_start(x_back[:, :, :], x_spill).then_inc(S["x_back_in"], 16)
        group8(N_WO, w_o)
        group8(N_FF, w_ff1)
        for q in range(3):
            group8(N_FF + 8 + 16 * q, w_ff1, (q + 1) * D)
            group8(N_FF + 16 + 16 * q, w_ff2, 0, q * KT)
        group8(N_ALL - 8, w_ff2, 0, 3 * KT)
        sp.wait_ge(S["yt_done"], 5)
        sp.dma_start(t_out["y_p"][0].rearrange("(t p) d -> p t d", p=P), y_tok[:, 0:4, :]).then_inc(S["out_done"], 16)
        sp.dma_start(t_out["y_s"][0], y_tok[0:TS, 4, :]).then_inc(S["out_done"], 16)
        sp.wait_ge(S["out_done"], 32)
        sp.wait_ge(S["caches_out"], 64)
        sp.wait_ge(S["s_out"], 32)

    @block.gpsimd
    def _(pool):
        ch = Chain(pool, S["pool_own"])
        ch.note(pool.memset(ones[:, :], 1.0))
        ch.note(pool.memset(ident[:, :], 0.0))
        ch.note(pool.memset(id64[:, :], 0.0))
        ch.note(pool.memset(neg[:, :], 0.0))
        ch.note(pool.memset(lvl[:, :, :], 0.0))
        ch.note(pool.memset(rows[:, :], 0.0))
        ch.note(pool.memset(bias[:, :], 0.0))
        ch.link(pool.memset(ab_raw[:, :, :], 0.0))
        ch.link(pool.affine_select(out=ident[:, :], in_=ident[:, :], compare_op=ALU.not_equal, fill=1.0, base=0,
                                   pattern=[[-1, P]], channel_multiplier=1))
        pool.memset(bias[:, 2:3], EPS).then_inc(S["consts"], 1)
        pool.memset(bias[:, 3:4], -0.5 * 4.852030263919617).then_inc(S["consts"], 1)
        pool.memset(acc[:, 1, 576:584], 0.0).then_inc(S["zeros_ready"], 1)
        pool.memset(acc[:, 0, 0:1], 0.0).then_inc(S["acc_free"], 2)
        pool.memset(acc[:, 0, 1:2], 0.0).then_inc(S["tails_done"], 2)
        pool.memset(acc[:, 0, 2:3], 0.0).then_inc(S["o_free"], 1)
        pool.memset(acc[:, 0, 3:4], 0.0).then_inc(S["tmp_free"], 2)
        pool.memset(acc[:, 0, 4:5], 0.0).then_inc(S["og_split"], 1)
        pool.memset(acc[:, 0, 5:6], 0.0).then_inc(S["prod_free"], 1)
        pool.memset(acc[:, 0, 7:8], 0.0).then_inc(S["bank_free"], 2)
        pool.wait_ge(S["bank_free"], 2)
        for p in range(2):
            b, base = slice(64 * p, 64 * p + 64), 0
            ch.link(pool.affine_select(out=id64[b, :], in_=id64[b, :], compare_op=ALU.not_equal, fill=1.0,
                                       base=base, pattern=[[-1, CH]], channel_multiplier=1))
            ch.link(pool.affine_select(out=neg[b, :], in_=neg[b, :], compare_op=ALU.is_ge, fill=-1e30,
                                       base=base, pattern=[[1, CH]], channel_multiplier=-1))
        for l in range(LEVELS):
            s = 1 << l
            v = lvl[:, l, :].rearrange("p (g r) -> p g r", r=2 * s)
            ch.link(pool.memset(v[:, :, s:2 * s], -1.0))
            for p in range(2):
                b = slice(64 * p, 64 * p + 64)
                w = v[b, :, s:2 * s]
                ch.link(pool.affine_select(out=w, in_=w, compare_op=ALU.is_ge, fill=0.0, base=0,
                                           pattern=[[-2 * s, CH // (2 * s)], [0, s]], channel_multiplier=1))
                ch.link(pool.affine_select(out=w, in_=w, compare_op=ALU.is_ge, fill=0.0, base=s - 1,
                                           pattern=[[2 * s, CH // (2 * s)], [0, s]], channel_multiplier=-1))
        pool.memset(acc[:, 0, 6:7], 0.0).then_inc(S["pool_ready"], 1)

        c0, t0 = VEC["cache_qkv"][0], (WB - 1) * NQKV
        cache_v = vecs[:, c0:c0 + t0].rearrange("p (j n) -> p n j", j=WB - 1)
        tails_v = tails[:, :, 0:t0].rearrange("p g (j n) -> p g n j", j=WB - 1)
        pool.wait_ge(S["vecs_done"], 1)
        pool.wait_ge(S["h_ready"], KT)
        with pool.Fori(0, NQKV // 2) as i:
            for b in range(2):
                n = 2 * i + b
                pool.wait_ge(S["acc_free"], n + 1)
                pool.tensor_copy(xp[:, b, 515:518], cache_v[:, n, :]).then_inc(S["pads_done"], 1)
                pool.wait_ge(S["bank_free"], n + 1 + 2)
                pool.tensor_copy(tails_v[:, 0, n, :], xp[:, b, 512:515])
                pool.tensor_copy(tails_v[:, 1, n, :], xp[:, b, 579:582]).then_inc(S["tails_done"], 1)

        ca0, ta0 = VEC["cache_a"][0], (WA - 1) * KT
        cache_a = vecs[:, ca0:ca0 + ta0].rearrange("p (j n) -> p n j", j=WA - 1)
        tails_a = tails[:, :, t0:t0 + ta0].rearrange("p g (j n) -> p g n j", j=WA - 1)

        def pads(i):
            value = whole(pool, i + 1)
            pool.wait_ge(S["vecs_done"], 1)
            pool.wait_ge(S["prod_free"], value)
            pool.memset(acc[:, 0, 0:2], 0.0)
            pool.tensor_copy(acc[:, 0, 514:516], cache_a[:, i, :]).then_inc(S["pads_a"], 1)

        def tails_of(i):
            pool.wait_ge(S["prod_done"], i + 1)
            pool.tensor_copy(tails_a[:, 0, i, :], acc[:, 0, 512:514])
            pool.tensor_copy(tails_a[:, 1, i, :], acc[:, 0, 578:580]).then_inc(S["tails_done"], 1)

        def chunk_first(c):
            pool.wait_ge(S["s_done"], c + 1)
            cols = ds(c * CH, CH)
            pool.tensor_tensor(sq[:, 0], K[:, :, cols], K[:, :, cols], ALU.mult).then_inc(S["sq_ready"], 1)
            pool.tensor_tensor(sq[:, 1], Q[:, :, cols], Q[:, :, cols], ALU.mult).then_inc(S["sq_ready"], 1)
            pool.tensor_tensor(vc[:, :, :], V[:, :, cols], ones[:, 0:CH].unsqueeze(1).to_broadcast([P, H, CH]), ALU.mult)\
                .then_inc(S["vc_done"], 1)

        def chunk_blocks(c):
            pool.wait_ge(S["at_done"], c + 1)
            for l in range(LEVELS):
                if l == 3:
                    pool.wait_ge(S["mt_done"], c + 1)
                elif l > 3:
                    pool.wait_ge(S["p1_ready"], c * NEXP + (l - 3))
                m = lvl[:, l, :].unsqueeze(1).to_broadcast([P, HP, CH])
                pool.tensor_tensor(nb[:, l % 3], at_[:, :, :], m, ALU.mult).then_inc(S["nb_done"], 1)

        pool.wait_ge(S["conv_done"], NQKV)
        pool.wait_ge(S["acc_free"], NQKV + 2)
        with pool.Fori(0, KT) as i:
            pads(i)
            chunk_first(i)
            chunk_blocks(i)
            tails_of(i)
        chunk_first(KT)
        pool.dma_start(t_out["s_p"][0, 0].rearrange("h k v -> k h v"), st[:, :, :]).then_inc(S["s_out"], 16)
        pool.wait_ge(S["s_out"], 16)
        pool.dma_start(st[:, :, :], A["state_delta"][0, 0].rearrange("h k v -> k h v")).then_inc(S["s_in"], 16)
        chunk_blocks(KT)
        pool.wait_ge(S["s_done"], NCH + 1)
        pool.dma_start(t_out["s_s"][0, 0].rearrange("h k v -> k h v"), st[:, :, :]).then_inc(S["s_out"], 16)
        def ada_load(m):
            if m >= AS:
                pool.wait_ge(S["ada_used"], m - AS + 1)
            r, k = 1 + m // KT, m % KT
            src = ada_v[:, k, 2 * D * r:2 * D * (r + 1)] if r < 3 else fin_v[:, k, :]
            pool.dma_start(ada_w[:, m % AS, :], src).then_inc(late_full[m % AS], 16)

        pool.wait_ge(S["s_out"], 32)
        pool.wait_ge(S["o_free"], NCH + 1)
        for m in range(AS):
            ada_load(m)
        with pool.Fori(0, HP) as i:
            pool.wait_ge(S["og_split"], 2 * i + 1)
            pool.tensor_tensor(acc[:, :, 0:T], Q[:, ds(2 * i, 2), :], Q[:, ds(2 * i, 2), :], ALU.mult)\
                .then_inc(S["osq_done"], 1)
        for m in range(AS, 3 * KT):
            ada_load(m)
        pool.wait_ge(S["tail_sb"], 2)
        nb_, na_ = (WB - 1) * NQKV, (WA - 1) * KT
        for g, (cb, ca) in enumerate((("cq_p", "ca_p"), ("cq_s", "ca_s"))):
            pool.dma_start(t_out[cb][0, 0].rearrange("j (n p) -> (j n) p", p=P), tail_rows[g][0:nb_, :])\
                .then_inc(S["caches_out"], 16)
            pool.dma_start(t_out[ca][0, 0].rearrange("j (n p) -> (j n) p", p=P), tail_rows[g][nb_:nb_ + na_, :])\
                .then_inc(S["caches_out"], 16)

    @block.tensor
    def _(pe):
        T_ = nc.tensor

        def products(n, b, hi, lo, ready=None, start=0, k0=0, k1=KT):
            if k0 == 0:
                pe.wait_ge(S["w_lo_done"], n + 1)
                pe.wait_ge(S["bank_free"], n + 1)
            for k in range(k0, k1):
                if ready:
                    pe.wait_ge(S[ready], start + k + 1)
                for wp, ap in ((w_hi, hi), (w_hi, lo), (w_lo, hi)):
                    for h in range(2):
                        last = T_.matmul(gp[:, 2 * b + h, 0:HALF], wp[:, b, k, :],
                                         ap[:, k, h * HALF:(h + 1) * HALF],
                                         start=(k == 0 and wp is w_hi and ap is hi),
                                         stop=(k == KT - 1 and wp is w_lo))
            if k1 == KT:
                last.then_inc(S["tile_done"], 1)

        def ada(r, bank, weights, wait):
            for k in range(KT):
                wait(k)
                for j in range(4):
                    last = T_.matmul(bank[32 * j:32 * j + 2, :], c_act[:, k, :],
                                     weights(k)[:, 512 * j:512 * j + 512], start=(k == 0), stop=(k == KT - 1))
                last.then_inc(S["ada_used"] if r else S["ada0_used"], 1)

        pe.wait_ge(S["rows_in"], 16 * 13)
        pe.wait_ge(S["consts"], 1)
        for g in range(3):
            n = min(P, NVEC - g * P)
            last = T_.transpose(B0[:, g * P:g * P + n], vrows[0:n, g, :], ident[0:n, 0:n])
        last.then_inc(S["vecs_t"], 1)
        pe.wait_ge(S["x_in"], 32)
        pe.wait_ge(S["vecs_done"], 1)

        def sums(f, name, a, b, n=0):
            pe.wait_ge(S[name], n + f + 1)
            for h, bank in enumerate((a, b)):
                last = T_.matmul(bank[:, 0:HALF], ones[:, :], acc[:, f % 2, h * HALF:(h + 1) * HALF],
                                 start=(f == 0), stop=(f == KT - 1))
            last.then_inc(S["ss_all"], 1)

        for f in range(KT):
            b = f % 2
            if f >= 2:
                pe.wait_ge(S["xt_done"], f - 1)
            for t in range(4):
                T_.transpose(gp[:, 2 * b, t * P:(t + 1) * P], x_tok[:, t, f * P:(f + 1) * P], ident[:, :])
            T_.transpose(gp[:, 2 * b + 1, 0:TS], x_tok[0:TS, 4, f * P:(f + 1) * P], ident[0:TS, 0:TS])\
                .then_inc(S["xt_ready"], 1)
            if f:
                sums(f - 1, "sq_done", B0, B3)
        sums(KT - 1, "sq_done", B0, B3)
        pe.wait_ge(S["c_act"], 1)
        pe.wait_ge(S["ada_row_sb"], 1)
        ada(0, B1, lambda k: ada0_w[:, k, :], lambda k: pe.wait_ge(ada_full[k], 16))

        def ada_columns(bank, src, n):
            pe.wait_ge(S["ada_row_sb"], n)
            for s in range(4):
                last = T_.transpose(bank[:, s * P:(s + 1) * P], src[:, s * P:(s + 1) * P], ident[:, :])
            last.then_inc(S["ada_t"], 1)

        ada_columns(B2, mrow, 2)
        pe.wait_ge(S["ab_split"], 1)
        pe.wait_ge(S["mod_done"], 1)
        for k in range(KT):
            pe.wait_ge(S["h_ready"], k + 1)
            for wp, ap in ((ab_hi, a_hi), (ab_hi, a_lo), (ab_lo, a_hi)):
                for h, bank in enumerate((B1, B2)):
                    last = T_.matmul(bank[0:CH, 0:HALF], wp[:, k, :], ap[:, k, h * HALF:(h + 1) * HALF],
                                     start=(k == 0 and wp is ab_hi and ap is a_hi),
                                     stop=(k == KT - 1 and wp is ab_lo))
        last.then_inc(S["ab_ready"], 1)

        with pe.Fori(0, NQKV // 4) as i:
            for j in range(4):
                products(4 * i + j, j % 2, a_hi, a_lo)

        pe.wait_ge(S["ab_rows"], 1)
        pe.wait_ge(S["row_a"], 3)
        pe.wait_ge(S["pool_ready"], 1)
        for c in range(NCH):
            for p in range(2):
                sel = ident[:, :].rearrange("p (q r) -> p q r", q=4)[:, :, p:H:2]
                last = T_.matmul(B2[64 * p:64 * p + 64, 16 * c:16 * c + 16], rows[:, c * CH:(c + 1) * CH], sel,
                                 start=True, stop=True)
        last.then_inc(S["tok_t"], 1)
        pe.wait_ge(S["tok_done"], 1)

        heads = [(p, hp, 2 * hp + p, slice(64 * p, 64 * p + 64)) for p in range(2) for hp in range(HP)]

        def bcast(c):
            pe.wait_ge(S["s_done"], c + 1)
            for q, bank in ((0, B2), (32, B3)):
                for h in range(H):
                    last = T_.matmul(bank[:, h * CH:(h + 1) * CH], ident[:, q + h:q + h + 1].to_broadcast([P, P]),
                                     rows[:, ds(c * CH, CH)], start=True, stop=True)
            last.then_inc(S["bc_ready"], 1)

        def squares(c):
            pe.wait_ge(S["o_free"], c + 1)
            for g, bank in enumerate((B0, B1)):
                pe.wait_ge(S["sq_ready"], 2 * c + g + 1)
                last = T_.matmul(bank[:, :], ones[:, :], sq[:, g], start=True, stop=True)
            last.then_inc(S["ss_ready"], 1)

        def turn(c):
            pe.wait_ge(S["kq_done"], c + 1)
            pe.wait_ge(S["vc_done"], c + 1)
            for hp in range(HP):
                T_.transpose(B0[:, hp * P:(hp + 1) * P], kq[:, 0, 2 * hp:2 * hp + 2, :].rearrange("p h i -> p (h i)"), ident[:, :])
            for hp in range(HP):
                last = T_.transpose(B1[:, hp * P:(hp + 1) * P], vc[:, 2 * hp:2 * hp + 2, :].rearrange("p h i -> p (h i)"), ident[:, :])
            last.then_inc(S["tr_ready"], 1)
            pe.wait_ge(S["dd_done"], c + 1)
            for p, hp, h, b in heads:
                last = T_.matmul(B2[b, hp * P:(hp + 1) * P], kq[:, 0, h, :], kq[:, :, h, :], start=True, stop=True)
            last.then_inc(S["kkqk_ready"], 1)

        def first_inverse(c):
            value = whole(pe, c + 1)
            pe.wait_ge(S["pool_ready"], 1)
            pe.wait_ge(S["mt_done"], value)
            for p, hp, h, b in heads:
                last = T_.matmul(B3[b, hp * CH:(hp + 1) * CH], mm[b, 1, hp, :], id64[b, :], start=True, stop=True)
            last.then_inc(S["m0_ready"], 1)

        def step_p(c, l):
            block_of = whole(pe, c * LEVELS + l + 1)
            sem, value = (S["m0_done"], c + 1) if l == 1 else (S["m_done"], c * NEXP + l - 1)
            value = whole(pe, value)
            pe.wait_ge(S["pool_ready"], 1)
            pe.wait_ge(S["nb_done"], block_of)
            pe.wait_ge(sem, value)
            for p, hp, h, b in heads:
                last = T_.matmul(B3[b, hp * CH:(hp + 1) * CH], nb[b, l % 3, hp, :], mm[b, 0, hp, :],
                                 start=True, stop=True)
            last.then_inc(S["p1_ready"], 1)

        def step_x(c, l):
            if l == 1:
                pe.wait_ge(S["at_done"], c + 1)
            value = whole(pe, c * NEXP + l)
            pe.wait_ge(S["pool_ready"], 1)
            pe.wait_ge(S["p1_done"], value)
            for p, hp, h, b in heads:
                if l < NEXP:
                    T_.matmul(B2[b, hp * CH:(hp + 1) * CH], mm[b, 1, hp, :], p1[b, hp, :], start=True, stop=True)
                last = T_.matmul(B2[b, (HP + hp) * CH:(HP + hp + 1) * CH], p1[b, hp, :], mm[b, 1, hp, :],
                                 start=True, stop=True)
            last.then_inc(S["x_ready"], 1)

        def w_product(c):
            pe.wait_ge(S["m_done"], (c + 1) * NEXP)
            pe.wait_ge(S["tokmul_done"], c + 1)
            for p, hp, h, b in heads:
                bank = (B0, B1)[p]
                last = T_.matmul(bank[:, hp * CH:(hp + 1) * CH], kbe[b, hp, :], mm[b, 1, hp, :], start=True, stop=True)
            last.then_inc(S["wt_ready"], 1)

        def v_product(c):
            value = whole(pe, c + 1)
            pe.wait_ge(S["pool_ready"], 1)
            pe.wait_ge(S["nw_done"], value)
            if isinstance(c, int):
                pe.wait_ge(S["s_in"], 16)
            for p, hp, h, b in heads:
                T_.matmul(B3[b, hp * P:(hp + 1) * P], mm[b, 1, hp, :], vb[b, hp, :], start=True, stop=False)
                last = T_.matmul(B3[b, hp * P:(hp + 1) * P], nw[:, p, hp, :], st[:, h, :], start=False, stop=True)
            last.then_inc(S["vn_ready"], 1)

        def o_product(c):
            pe.wait_ge(S["vn_done"], c + 1)
            pe.wait_ge(S["qd_done"], c + 1)
            for p, hp, h, b in heads:
                bank = (B0, B1)[p]
                T_.matmul(bank[:, hp * CH:(hp + 1) * CH], st[:, h, :], qd[:, h, :], start=True, stop=False)
                last = T_.matmul(bank[:, hp * CH:(hp + 1) * CH], vn[b, hp, :], qkt[b, hp, :], start=False, stop=True)
            last.then_inc(S["o_ready"], 1)
            for p, hp, h, b in heads:
                bank = (B2, B3)[p]
                last = T_.matmul(bank[:, hp * P:(hp + 1) * P], kdt[b, hp, :], vn[b, hp, :], start=True, stop=True)
            last.then_inc(S["ds_ready"], 1)

        def mixed(n0, c, own):
            def part(k0, k1):
                j = k0 // KT
                products(n0 + j, j % 2, a_hi, a_lo, k0=k0 % KT, k1=k1 - j * KT)

            bcast(c)
            part(0, 2)
            squares(c)
            part(2, 8)
            part(8, 9)
            turn(c)
            part(9, 11)
            first_inverse(c)
            part(11, 13)
            step_p(c, 1)
            part(13, 14)
            step_x(c, 1)
            part(14, 16)
            step_p(c, 2)
            part(16, 17)
            step_x(c, 2)
            part(17, 19)
            step_p(c, 3)
            part(19, 20)
            step_x(c, 3)
            part(20, 22)
            step_p(c, 4)
            part(22, 23)
            step_x(c, 4)
            part(23, 24)
            part(24, 25)
            step_p(c, 5)
            part(25, 26)
            step_x(c, 5)
            part(26, 28)
            w_product(c)
            part(28, 29)
            v_product(c)
            part(29, 30)
            o_product(c)
            part(30, 32)

        with pe.Fori(0, KT) as i:
            mixed(N_MIX + 4 * i, i, None)
        mixed(N_TAIL, KT, None)
        with pe.Fori(1, KT // 2) as i:
            for j in range(4):
                products(N_TAIL + 4 * i + j, j % 2, a_hi, a_lo)

        def group8(n0, hi, lo, ready=None, start=0, between=None):
            with pe.Fori(0, 2) as i:
                for j in range(4):
                    products(n0 + 4 * i + j, j % 2, hi, lo, ready, start)
                    if between and j % 2 == 0:
                        between(2 * i + j // 2)

        def o_sums(i):
            pe.wait_ge(S["osq_done"], i + 1)
            for e in range(2):
                for h in range(2):
                    last = T_.matmul(dp[:, 2 * e + h, 0:HALF], ones[:, :], acc[:, e, h * HALF:(h + 1) * HALF],
                                     start=True, stop=True)
            last.then_inc(S["oss_ready"], 1)

        group8(N_WA, a_hi, a_lo, "u_split", 0, o_sums)

        def ada_late(r):
            pe.wait_ge(S["ada_row_sb"], 2 * r + 1)
            ada(r, B2, lambda k: ada_w[:, (KT * (r - 1) + k) % AS, :],
                lambda k: pe.wait_ge(late_full[(KT * (r - 1) + k) % AS],
                                     16 * ((KT * (r - 1) + k) // AS + 1)))
            ada_columns(B3, mrow_l, 2 * r + 2)

        ada_late(1)
        group8(N_WB, b_hi, b_lo, "og_split", 1)
        ada_late(2)
        pe.wait_ge(S["mod_done"], 3)
        for n in range(N_WO, N_WO + KT):
            products(n, n % 2, a_hi, a_lo, "y_split", 0)
            if n > N_WO:
                sums(n - N_WO - 1, "sq2_done", B0, B1)
        sums(KT - 1, "sq2_done", B0, B1)
        ada_late(3)
        group8(N_FF, a_hi, a_lo, "h_ready", KT)
        for q in range(3):
            group8(N_FF + 8 + 16 * q, a_hi, a_lo)
            group8(N_FF + 16 + 16 * q, f_hi[q % 2], f_lo[q % 2], "f_split", KT * q)
        for n in range(N_ALL - KT, N_ALL):
            products(n, n % 2, f_hi[1], f_lo[1], "f_split", KT * 3)
            if n > N_ALL - KT:
                sums(n - (N_ALL - KT) - 1, "sq2_done", B0, B1, KT)
        sums(KT - 1, "sq2_done", B0, B1, KT)
        nt = (WB - 1) * NQKV + (WA - 1) * KT
        pe.wait_ge(S["mod_done"], 4)
        pe.wait_ge(S["tails_done"], 2 + NQKV + KT)
        for g in range(2):
            T_.transpose(dp[0:nt, 2 + g, 0:P], tails[:, g, :], ident[:, :]).then_inc(S["tail_t"], 1)
        pe.wait_ge(S["yo_done"], KT)
        for t in range(5):
            rows_n = P if t < 4 else TS
            if t >= 2:
                pe.wait_ge(S["yt_done"], t - 1)
            for f in range(KT):
                last = T_.transpose(gp[0:rows_n, 2 * (t % 2) + f // 4, (f % 4) * P:(f % 4 + 1) * P],
                                    y_fm[:, f, t * P:t * P + rows_n], ident[:, :])
            last.then_inc(S["yt_ready"], 1)

    @block.scalar
    def _(act):
        AC = nc.scalar.activation
        ch = Chain(act, S["act_own"])

        def w_split(n, group, j):
            act.wait_ge(raw_full[j], 16 * (group + 1))
            AC(w_hi[:, j % 2, :, :], w_raw[:, j, :, :], ACT.Copy).then_inc(S["w_hi_done"], 1)

        def bank(b):
            return gp[:, 2 * b:2 * b + 2, 0:HALF]

        def halves(t):
            return t.rearrange("p (h c) -> p h c", h=2)

        act.wait_ge(S["vecs_done"], 1)
        for g, name in enumerate(("c_p", "c_s")):
            a0 = VEC[name][0]
            last = AC(c_act[:, :, g], vecs[:, a0:a0 + KT], ACT.Silu)
        last.then_inc(S["c_act"], 1)
        for f in range(KT):
            b = f % 2
            act.wait_ge(S["xt_ready"], f + 1)
            AC(xT[:, f, 0:TP], gp[:, 2 * b, 0:TP], ACT.Copy)
            AC(xT[:, f, TP:T], gp[:, 2 * b + 1, 0:TS], ACT.Copy).then_inc(S["xt_done"], 1)
            act.wait_ge(S["xt_done"], f + 1)
            if f >= 2:
                act.wait_ge(S["ss_all"], f - 1)
            else:
                act.wait_ge(S["pool_ready"], 1)
            AC(acc[:, b, 0:T], xT[:, f, :], ACT.Square).then_inc(S["sq_done"], 1)

        def rstd(out, banks, name, n, scale):
            act.wait_ge(S[name], n)
            for h, bk in enumerate(banks):
                ch.note(AC(out[:, h * HALF:(h + 1) * HALF], bk[:, 0:HALF], ACT.Ln, bias=bias[:, 2:3], scale=scale))
            ch.wait()
            return AC(out[:, :], out[:, :], ACT.Exp, scale=-0.5)

        rstd(rstd1[:, :], (B0, B3), "ss_all", KT, 1.0 / D).then_inc(S["rstd_done"], 1)
        def ada_rows(bk, dst, n, r):
            act.wait_ge(S["ada0_used"] if r == 0 else S["ada_used"], n)
            AC(dst[:, :], bk[:, :], ACT.Copy).then_inc(S["ada_row_sb"], 1)

        ada_rows(B1, mrow, KT, 0)
        act.wait_ge(S["ab_in"], 64)
        AC(ab_hi[:, :, :], ab_raw[:, :, :], ACT.Copy).then_inc(S["ab_hi_done"], 1)
        for f in range(KT):
            act.wait_ge(S["t_done"], f + 1)
            AC(a_hi[:, f, :], xp[:, f % 2, 0:T], ACT.Copy).then_inc(S["hi_split"], 1)
        for j in range(2):
            w_split(j, 0, j)
        act.wait_ge(S["ab_ready"], 1)
        ch.note(AC(ab_sb[0:CH, 0:HALF], B1[0:CH, 0:HALF], ACT.Copy))
        ch.link(AC(ab_sb[0:CH, HALF:T], B2[0:CH, 0:HALF], ACT.Copy))
        ch.note(AC(ab_sb[0:32, :], ab_sb[0:32, :], ACT.Identity, bias=bias[0:32, 0:1]))
        ch.note(AC(ab_sb[32:CH, :], ab_sb[32:CH, :], ACT.Copy, scale=-1.0))
        ch.link(AC(bias[0:H, 4:5], bias[0:H, 1:2], ACT.Exp))
        ch.link(AC(ab_e[0:CH, :], ab_sb[0:CH, :], ACT.Abs))
        ch.link(AC(ab_e[0:CH, :], ab_e[0:CH, :], ACT.Exp, scale=-1.0))
        AC(ab_e[0:CH, :], ab_e[0:CH, :], ACT.Ln, bias=ones[0:CH, 0:1])
        AC(bias[0:H, 5:6], bias[0:H, 4:5], ACT.Copy, scale=-1.0).then_inc(S["row_a"], 1)
        act.wait_ge(S["row_v"], 1)
        AC(rows[32:32 + H, :], ab_sp[32:32 + H, :], ACT.Exp, scale=-1.0)
        AC(row_b[0:H, :], ab_sp[32:32 + H, :], ACT.Exp, scale=-1.0)
        act.wait_ge(S["row_v"], 2)
        AC(row_e[0:H, :], rows[0:H, :], ACT.Exp).then_inc(S["row_a"], 1)
        AC(rows[64:64 + H, :], row_g[0:H, :], ACT.Exp).then_inc(S["row_a"], 1)

        with act.Fori(0, NQKV // 4) as i:
            for j in range(4):
                n, b = 4 * i + j, j % 2
                act.wait_ge(S["tile_done"], n + 1)
                act.wait_ge(S["tails_done"], n + 1)
                AC(xp[:, b, 3:3 + HALF], gp[:, 2 * b, 0:HALF], ACT.Copy)
                AC(xp[:, b, 3 + HALF:3 + TP], gp[:, 2 * b + 1, 0:TP - HALF], ACT.Copy)
                AC(xp[:, b, 6 + TP:6 + T], gp[:, 2 * b + 1, TP - HALF:HALF], ACT.Copy).then_inc(S["bank_free"], 1)
                w_split(n + 2, i + (j + 2) // 4, (j + 2) % 4)
                act.wait_ge(S["conv_done"], n + 1)
                AC(qkv[:, n, 0:TP], acc[:, b, 0:TP], ACT.Silu)
                AC(qkv[:, n, TP:T], acc[:, b, TP + 3:T + 3], ACT.Silu).then_inc(S["acc_free"], 1)

        def free(n, group, j):
            w_split(n + 2, group + (j + 2) // 4, (j + 2) % 4)

        def evac(n, b, out, func=ACT.Copy, scale=1.0, also=None, value=0):
            act.wait_ge(S["tile_done"], n + 1)
            if also:
                act.wait_ge(S[also], value)
            AC(halves(out), bank(b), func, scale=scale).then_inc(S["bank_free"], 1)

        def chunk_norms(c):
            act.wait_ge(S["bc_ready"], c + 1)
            AC(eg[:, :, :], B2.rearrange("p (h i) -> p h i", h=H), ACT.Exp).then_inc(S["eg_done"], 1)
            act.wait_ge(S["ss_ready"], c + 1)
            for g, bk in enumerate((B0, B1)):
                ch.note(AC(sq[:, g], bk.rearrange("p (h i) -> p h i", h=H), ACT.Ln, bias=bias[:, 2:3]))
            ch.wait()
            AC(sq[:, 0], sq[:, 0], ACT.Exp, scale=-0.5)
            AC(sq[:, 1], sq[:, 1], ACT.Exp, scale=-0.5, bias=bias[:, 3:4]).then_inc(S["rkq_done"], 1)
            act.wait_ge(S["dd_done"], c + 1)
            AC(dec[:, :, :], dec[:, :, :], ACT.Exp).then_inc(S["dec_done"], 1)

        def step_copy(c, l):
            act.wait_ge(S["p1_ready"], c * NEXP + l)
            AC(p1[:, :, :], B3[:, 0:HP * CH].rearrange("p (h i) -> p h i", h=HP), ACT.Copy).then_inc(S["p1_done"], 1)

        def chunk_out(c):
            act.wait_ge(S["wt_ready"], c + 1)
            for p, bk in enumerate((B0, B1)):
                last = AC(nw[:, p], bk[:, 0:HP * CH].rearrange("p (h i) -> p h i", h=HP), ACT.Copy, scale=-1.0)
            last.then_inc(S["nw_done"], 1)
            act.wait_ge(S["vn_ready"], c + 1)
            AC(vn[:, :, :], B3.rearrange("p (h v) -> p h v", h=HP), ACT.Copy).then_inc(S["vn_done"], 1)
            act.wait_ge(S["o_ready"], c + 1)
            q_v = Q.rearrange("p (hp e) t -> p e hp t", e=2)
            for p, bk in enumerate((B0, B1)):
                last = AC(q_v[:, p, :, ds(c * CH, CH)], bk[:, 0:HP * CH].rearrange("p (h i) -> p h i", h=HP), ACT.Copy)
            last.then_inc(S["o_free"], 1)

        act.wait_ge(S["spilled"], 16)
        act.wait_ge(S["tails_done"], NQKV + 2)
        with act.Fori(0, KT) as i:
            n0 = N_MIX + 4 * i
            ch.loop(i, 2)
            chunk_norms(i)
            evac(n0, 0, xp[:, 0, 0:T], also="u_done", value=i + 1)
            free(n0, 6 + i, 0)
            step_copy(i, 1)
            evac(n0 + 1, 1, xp[:, 1, 0:T])
            free(n0 + 1, 6 + i, 1)
            step_copy(i, 2)
            step_copy(i, 3)
            step_copy(i, 4)
            evac(n0 + 2, 0, xp[:, 0, 0:T], also="prod_done", value=i + 1)
            free(n0 + 2, 6 + i, 2)
            step_copy(i, 5)
            chunk_out(i)
            evac(n0 + 3, 1, xT[:, i, :])
            free(n0 + 3, 6 + i, 3)
            ch.end(KT)

        chunk_norms(KT)
        act.wait_ge(S["kq_done"], NCH)
        act.wait_ge(S["vc_done"], NCH)
        for j in range(4):
            n, t = N_TAIL + j, j // 2
            if j % 2 == 0:
                evac(n, 0, V[:, t, :], ACT.Copy)
            else:
                evac(n, 1, K[:, t, :], ACT.Copy)
            free(n, 14, j)
            for l in {0: (1,), 1: (2, 3, 4), 2: (5,), 3: ()}[j]:
                step_copy(KT, l)
            if j == 2:
                chunk_out(KT)
        for t in range(2):
            act.wait_ge(S["bank_free"], N_TAIL + 4 + 2)
            AC(V[:, t, :], V[:, t, :], ACT.Silu).then_inc(S["z_done"], 1)
            AC(K[:, t, :], K[:, t, :], ACT.Tanh, scale=0.5)
            AC(xT[:, t, :], xT[:, t, :], ACT.Tanh, scale=0.5).then_inc(S["ga_done"], 1)
        with act.Fori(1, KT // 2) as i:
            for j in range(4):
                n, t = N_TAIL + 4 * i + j, 2 * i + j // 2
                if j % 2 == 0:
                    evac(n, 0, V[:, t, :], ACT.Silu)
                    free(n, 14 + i, j)
                    AC(xT[:, t, :], xT[:, t, :], ACT.Tanh, scale=0.5).then_inc(S["ga_done"], 1)
                else:
                    evac(n, 1, K[:, t, :], ACT.Tanh, scale=0.5)
                    free(n, 14 + i, j)
        act.wait_ge(S["tile_done"], N_WA)
        act.wait_ge(S["u_done"], KT + 1)
        for t in range(KT):
            AC(a_hi[:, t, :], U[:, t, :], ACT.Copy).then_inc(S["u_hi"], 1)

        def o_norm(i):
            act.wait_ge(S["oss_ready"], i + 1)
            for e in range(2):
                for h in range(2):
                    ch.note(AC(rs[:, e, h * HALF:(h + 1) * HALF], dp[:, 2 * e + h, 0:HALF], ACT.Ln,
                               bias=bias[:, 2:3], scale=1.0 / P))
            ch.wait()
            AC(rs[:, :, :], rs[:, :, :], ACT.Exp, scale=-0.5).then_inc(S["rs_done"], 1)

        def og_hi(t, e):
            act.wait_ge(S["og_done"], t + 1)
            AC(b_hi[:, t, :], og[e][:, :], ACT.Copy).then_inc(S["og_hi"], 1)

        act.wait_ge(S["u_split"], KT)
        with act.Fori(0, 2) as i:
            ch.loop(i, 8)
            for j in range(4):
                n, b = N_WA + 4 * i + j, j % 2
                evac(n, b, xp[:, b, 0:T], scale=0.5, also="tmp_free", value=4 * i + j + 1)
                free(n, 18 + i, j)
                if j % 2 == 0:
                    o_norm(2 * i + j // 2)
                else:
                    og_hi(4 * i + j - 1, 0)
                    og_hi(4 * i + j, 1)
            ch.end(2)
        ada_rows(B2, mrow_l, KT, 1)
        with act.Fori(0, 2) as i:
            for j in range(4):
                n, b = N_WB + 4 * i + j, j % 2
                evac(n, b, xp[:, b, 0:T], scale=0.5, also="tmp_free", value=8 + 4 * i + j + 1)
                free(n, 20 + i, j)
                act.wait_ge(S["y_done"], 4 * i + j + 1)
                AC(a_hi[:, 4 * i + j, :], acc[:, b, 0:T], ACT.Copy).then_inc(S["y_hi"], 1)
        ada_rows(B2, mrow_l, 2 * KT, 2)

        def squared(t, n, m):
            act.wait_ge(S["tmp_free"], n - N_WA + 3)
            if t >= 2:
                act.wait_ge(S["ss_all"], m + t - 1)
            AC(acc[:, t % 2, 0:T], xT[:, t, :], ACT.Square).then_inc(S["sq2_done"], 1)

        act.wait_ge(S["y_split"], KT)
        for t in range(KT):
            n, b = N_WO + t, t % 2
            evac(n, b, xp[:, b, 0:T], also="tmp_free", value=16 + t + 1)
            free(n, 22 + t // 4, t % 4)
            squared(t, n, KT)
        rstd(rstd2[:, :], (B0, B1), "ss_all", 2 * KT, 1.0 / D).then_inc(S["rstd_done"], 1)
        for f in range(KT):
            act.wait_ge(S["t_done"], KT + f + 1)
            AC(a_hi[:, f, :], xp[:, f % 2, 0:T], ACT.Copy).then_inc(S["hi_split"], 1)
        ada_rows(B2, mrow_l, 3 * KT, 3)

        def ff1(q, n0):
            with act.Fori(0, 2) as i:
                for j in range(4):
                    n, b, t = n0 + 4 * i + j, j % 2, 4 * i + j
                    evac(n, b, xp[:, b, 0:T], also="tmp_free", value=n - N_WA + 1)
                    free(n, n0 // 4 + i, j)
                    act.wait_ge(S["tmp_free"], n - N_WA + 3)
                    AC(f_hi[q % 2][:, t, :], acc[:, b, 0:T], ACT.Copy).then_inc(S["f_hi_done"], 1)

        def ff2(q, n0):
            with act.Fori(0, 2) as i:
                for j in range(4):
                    n, b = n0 + 4 * i + j, j % 2
                    evac(n, b, xp[:, b, 0:T], also="tmp_free", value=n - N_WA + 1)
                    free(n, n0 // 4 + i, j)

        ff1(0, N_FF)
        for q in range(3):
            ff1(q + 1, N_FF + 8 + 16 * q)
            ff2(q, N_FF + 16 + 16 * q)
        for t in range(KT):
            n, b = N_ALL - KT + t, t % 2
            evac(n, b, xp[:, b, 0:T], also="tmp_free", value=n - N_WA + 1)
            if n + 2 < N_ALL:
                free(n, n // 4, n % 4)
            squared(t, n, 2 * KT)
        rstd(rstd2[:, :], (B0, B1), "ss_all", 3 * KT, 1.0 / D).then_inc(S["rstd_done"], 1)
        for g in range(2):
            nt = (WB - 1) * NQKV + (WA - 1) * KT
            act.wait_ge(S["tail_t"], g + 1)
            AC(tail_rows[g][0:nt, :], dp[0:nt, 2 + g, 0:P], ACT.Copy).then_inc(S["tail_sb"], 1)
        for t in range(5):
            rn = P if t < 4 else TS
            act.wait_ge(S["yt_ready"], t + 1)
            AC(y_tok[0:rn, t, :].rearrange("p (h c) -> p h c", h=2), gp[0:rn, 2 * (t % 2):2 * (t % 2) + 2, :], ACT.Copy)\
                .then_inc(S["yt_done"], 1)

    @block.vector
    def _(dve):
        V_ = nc.vector
        TT, TS_, STT = V_.tensor_tensor, V_.tensor_scalar, V_.scalar_tensor_tensor
        ch = Chain(dve, S["dve_own"])
        GR = ((0, slice(0, TP)), (1, slice(TP, T)))

        def lo_split(n, j):
            dve.wait_ge(S["w_hi_done"], n + 1)
            TT(w_lo[:, j % 2, :, :], w_raw[:, j, :, :], w_hi[:, j % 2, :, :].bitcast(F32), ALU.subtract)\
                .then_inc(S["w_lo_done"], 1)

        dve.wait_ge(S["vecs_t"], 1)
        V_.tensor_copy(vecs[:, :], B0[:, 0:NVEC]).then_inc(S["vecs_done"], 1)
        dve.wait_ge(S["vecs_done"], 1)
        V_.memset(B1, 0.0).then_inc(S["ada_row_sb"], 1)

        def columns(r, bk, bias_name, b0):
            dve.wait_ge(S["ada_t"], r + 1)
            a0 = VEC[bias_name][0] + b0
            src = bk.rearrange("p (s j q) -> p j s q", s=4, j=4)[:, :, :, 0:2]
            bs = vecs[:, a0:a0 + 16].rearrange("p (j s) -> p j s", j=4).unsqueeze(3).to_broadcast([P, 4, 4, 2])
            return TT(mod[:, r].rearrange("p (j s) g -> p j s g", j=4), src, bs, ALU.add)

        def scale_of(k, r, b0, gname):
            a0 = VEC[gname][0]
            g = vecs[:, a0:a0 + KT].unsqueeze(2).to_broadcast([P, KT, 2])
            ch.link(TS_(scales[:, k], mod[:, r, b0:b0 + KT, :], 1.0, None, ALU.add))
            return TT(scales[:, k], scales[:, k], g, ALU.mult)

        ch.link(columns(0, B2, "ada_b", 0))
        scale_of(0, 0, KT, "norm1_g").then_inc(S["mod_done"], 1)
        dve.wait_ge(S["mod_done"], 1)
        dve.wait_ge(S["rstd_done"], 1)
        dve.wait_ge(S["ab_hi_done"], 1)
        TT(ab_lo[:, :, :], ab_raw[:, :, :], ab_hi[:, :, :].bitcast(F32), ALU.subtract).then_inc(S["ab_split"], 1)

        def modulate(f, rstd, k, r, b0):
            t = xp[:, f % 2, 0:T]
            if f >= 2:
                dve.wait_ge(S["h_ready"], k * KT + f - 1)
            ch.link(TT(t, xT[:, f, :], rstd[:, :], ALU.mult))
            for g, c in GR:
                last = TS_(xp[:, f % 2, c], xp[:, f % 2, c], scales[:, k, f, g:g + 1], mod[:, r, b0 + f, g:g + 1],
                           ALU.mult, ALU.add)
            last.then_inc(S["t_done"], 1)

        def low(f, n):
            dve.wait_ge(S["hi_split"], n + f + 1)
            TT(a_lo[:, f, :], xp[:, f % 2, 0:T], a_hi[:, f, :].bitcast(F32), ALU.subtract).then_inc(S["h_ready"], 1)

        def norm(rstd, k, r, b0):
            for f in range(KT):
                modulate(f, rstd, k, r, b0)
                if f:
                    low(f - 1, k * KT)
            low(KT - 1, k * KT)

        norm(rstd1, 0, 0, 0)
        for j in range(2):
            lo_split(j, j)
        dve.wait_ge(S["h_ready"], KT)
        ch.link(V_.memset(xp[:, :, 0:3], 0.0))
        dve.wait_ge(S["row_a"], 1)
        ch.note(V_.memset(cmask[0:H, :], 1.0))
        ch.link(STT(ab_sp[0:CH, :], ab_sb[0:CH, :], 0.0, ab_e[0:CH, :], ALU.max, ALU.add))
        ch.note(V_.memset(cmask[0:H, :].rearrange("p (c i) -> p c i", i=CH)[:, :, 0:1], 0.0))
        TS_(row_g[0:H, :], ab_sp[0:H, :], bias[0:H, 5:6], None, ALU.mult).then_inc(S["row_v"], 1)
        dve.wait_ge(S["row_v"], 1)
        ch.wait()
        ch.link(V_.tensor_tensor_scan(rows[0:H, :], cmask[0:H, :], row_g[0:H, :], 0.0, ALU.mult, ALU.add))
        rv = rows[0:H, :].rearrange("p (c i) -> p c i", i=CH)
        TT(row_g[0:H, :].rearrange("p (c i) -> p c i", i=CH), rv[:, :, CH - 1:CH].to_broadcast([H, NCH, CH]), rv,
           ALU.subtract).then_inc(S["row_v"], 1)
        dve.wait_ge(S["row_a"], 2)
        TT(rows[96:96 + H, :], row_e[0:H, :], row_b[0:H, :], ALU.mult).then_inc(S["ab_rows"], 1)

        c0 = VEC["conv_qkv_w"][0]
        cw = vecs[:, c0:c0 + WB * NQKV].rearrange("p (j n) -> p j n", j=WB)
        W = TP + 3 + TS
        with dve.Fori(0, NQKV // 4) as i:
            ch.loop(i, 12)
            for j in range(4):
                n, b = 4 * i + j, j % 2
                dve.wait_ge(S["bank_free"], n + 1 + 2)
                dve.wait_ge(S["pads_done"], n + 1)
                dve.wait_ge(S["acc_free"], n + 1)
                ch.link(TS_(acc[:, b, 0:W], xp[:, b, 0:W], cw[:, 0, ds(n, 1)], None, ALU.mult))
                for tap in range(1, WB):
                    ins = STT(acc[:, b, 0:W], xp[:, b, tap:tap + W], cw[:, tap, ds(n, 1)], acc[:, b, 0:W],
                              ALU.mult, ALU.add)
                    if tap < WB - 1:
                        ch.link(ins)
                    else:
                        ins.then_inc(S["conv_done"], 1)
                lo_split(n + 2, (j + 2) % 4)
            ch.end(NQKV // 4)
        dve.wait_ge(S["tok_t"], 1)
        V_.tensor_copy(tokv[:, :, :], B2[:, 0:NCH * 16].rearrange("p (c q) -> p c q", q=16)).then_inc(S["tok_done"], 1)
        dve.wait_ge(S["ab_rows"], 1)
        dve.wait_ge(S["row_a"], 3)
        V_.memset(st[:, :, :], 0.0).then_inc(S["s_done"], 1)
        dve.wait_ge(S["tok_done"], 1)
        V_.memset(bias[:, 7:8], 0.0).then_inc(S["u_done"], 1)

        par = [(p, slice(64 * p, 64 * p + 64)) for p in range(2)]

        def tok(c, q, n):
            return tokv[:, c, 4 * q:4 * q + 4].unsqueeze(2).to_broadcast([P, HP, n])

        def chunk_decay(c):
            dve.wait_ge(S["eg_done"], c + 1)
            v2 = B2.rearrange("p (h e i) -> p e h i", h=HP, e=2)
            v3 = B3.rearrange("p (h e i) -> p e h i", h=HP, e=2)
            for p, b in par:
                ch.note(TT(dec[b], v2[b, p], tok(c, 0, CH)[b], ALU.subtract))
            ch.wait()
            TT(dec[:, :, :], dec[:, :, :], neg[:, :].unsqueeze(1).to_broadcast([P, HP, CH]), ALU.add)\
                .then_inc(S["dd_done"], 1)
            dve.wait_ge(S["rkq_done"], c + 1)
            cols = ds(c * CH, CH)
            TT(kq[:, 0], K[:, :, cols], sq[:, 0], ALU.mult)
            TT(kq[:, 1], Q[:, :, cols], sq[:, 1], ALU.mult).then_inc(S["kq_done"], 1)
            dve.wait_ge(S["dec_done"], c + 1)
            for p, b in par:
                last = TT(decb[b], dec[b], v3[b, p], ALU.mult)
            last.then_inc(S["decb_done"], 1)
            dve.wait_ge(S["decb_done"], c + 1)
            dve.wait_ge(S["kq_done"], c + 1)

        def chunk_tokens(c):
            dve.wait_ge(S["tr_ready"], c + 1)
            TT(qd[:, :, :], kq[:, 1], eg[:, :, :], ALU.mult).then_inc(S["qd_done"], 1)
            dve.wait_ge(S["kkqk_ready"], c + 1)
            v = B2.rearrange("p (h e i) -> p h e i", h=HP, e=2)
            TT(at_[:, :, :], v[:, :, 0, :], decb[:, :, :], ALU.mult)
            TT(qkt[:, :, :], v[:, :, 1, :], dec[:, :, :], ALU.mult).then_inc(S["at_done"], 1)
            k_v, v_v = (x.rearrange("p (h d) -> p h d", h=HP) for x in (B0, B1))
            TT(kbe[:, :, :], k_v, tok(c, 3, P), ALU.mult)
            TT(kdt[:, :, :], k_v, tok(c, 2, P), ALU.mult)
            TT(vb[:, :, :], v_v, tok(c, 1, P), ALU.mult).then_inc(S["tokmul_done"], 1)
            dve.wait_ge(S["nb_done"], c * LEVELS + 1)
            TT(mm[:, 1], nb[:, 0], id64[:, :].unsqueeze(1).to_broadcast([P, HP, CH]), ALU.add).then_inc(S["mt_done"], 1)
            dve.wait_ge(S["m0_ready"], c + 1)
            V_.tensor_copy(mm[:, 0], B3[:, 0:HP * CH].rearrange("p (h i) -> p h i", h=HP)).then_inc(S["m0_done"], 1)
            dve.wait_ge(S["mt_done"], c + 1)
            dve.wait_ge(S["m0_done"], c + 1)

        def step_add(c, l):
            dve.wait_ge(S["x_ready"], c * NEXP + l)
            g = 0 if l < NEXP else 1
            TT(mm[:, g:2], mm[:, g:2], B2[:, g * HP * CH:].rearrange("p (g h i) -> p g h i", h=HP, i=CH), ALU.add)\
                .then_inc(S["m_done"], 1)
            dve.wait_ge(S["m_done"], c * NEXP + l)

        def state(c):
            dve.wait_ge(S["ds_ready"], c + 1)
            for h in range(H):
                hp, bk = h // 2, (B2, B3)[h % 2]
                last = STT(st[:, h, :], st[:, h, :], eg[:, h, CH - 1:CH], bk[:, hp * P:(hp + 1) * P], ALU.mult, ALU.add)
            last.then_inc(S["s_done"], 1)
            dve.wait_ge(S["s_done"], c + 2)

        c0 = VEC["conv_a_w"][0]
        caw = vecs[:, c0:c0 + WA * KT].rearrange("p (j n) -> p j n", j=WA)
        WM = TP + 2 + TS
        with dve.Fori(0, KT) as i:
            n0 = N_MIX + 4 * i
            ch.loop(i, 4)
            chunk_decay(i)
            lo_split(n0 + 2, 2)
            chunk_tokens(i)
            step_add(i, 1)
            dve.wait_ge(S["bank_free"], n0 + 1 + 3)
            dve.wait_ge(S["pads_a"], i + 1)
            dve.wait_ge(S["tails_done"], 2 + NQKV + i)
            TT(acc[:, 0, 2:2 + TP], xp[:, 0, 0:TP], xp[:, 1, 0:TP], ALU.mult)
            TT(acc[:, 0, 4 + TP:4 + T], xp[:, 0, TP:T], xp[:, 1, TP:T], ALU.mult).then_inc(S["prod_done"], 1)
            lo_split(n0 + 3, 3)
            step_add(i, 2)
            dve.wait_ge(S["prod_done"], i + 1)
            ch.link(TS_(acc[:, 1, 0:WM], acc[:, 0, 0:WM], caw[:, 0, ds(i, 1)], None, ALU.mult))
            ch.link(STT(acc[:, 1, 0:WM], acc[:, 0, 1:1 + WM], caw[:, 1, ds(i, 1)], acc[:, 1, 0:WM], ALU.mult, ALU.add))
            step_add(i, 3)
            STT(acc[:, 1, 0:WM], acc[:, 0, 2:2 + WM], caw[:, 2, ds(i, 1)], acc[:, 1, 0:WM], ALU.mult, ALU.add)\
                .then_inc(S["prod_free"], 1)
            step_add(i, 4)
            dve.wait_ge(S["bank_free"], n0 + 2 + 3)
            dve.wait_ge(S["prod_free"], i + 2)
            TT(U[:, i, 0:TP], acc[:, 1, 0:TP], xp[:, 0, 0:TP], ALU.mult)
            TT(U[:, i, TP:T], acc[:, 1, TP + 2:T + 2], xp[:, 0, TP:T], ALU.mult).then_inc(S["u_done"], 1)
            lo_split(n0 + 4, 0)
            step_add(i, 5)
            state(i)
            lo_split(n0 + 5, 1)
            ch.end(KT)

        chunk_decay(KT)
        lo_split(N_TAIL + 2, 2)
        chunk_tokens(KT)
        step_add(KT, 1)
        lo_split(N_TAIL + 3, 3)
        for l in (2, 3, 4):
            step_add(KT, l)
        lo_split(N_TAIL + 4, 0)
        step_add(KT, 5)
        dve.wait_ge(S["s_in"], 16)
        state(KT)
        lo_split(N_TAIL + 5, 1)
        with dve.Fori(1, KT // 2) as i:
            for j in range(4):
                lo_split(N_TAIL + 4 * i + j + 2, (j + 2) % 4)
        for t in range(KT):
            dve.wait_ge(S["u_hi"], t + 1)
            TT(a_lo[:, t, :], U[:, t, :], a_hi[:, t, :].bitcast(F32), ALU.subtract).then_inc(S["u_split"], 1)

        og_g = vec("out_g")
        with dve.Fori(0, 2) as i:
            ch.loop(i, 4)
            for j in range(4):
                t, b = 4 * i + j, j % 2
                n = N_WA + t
                dve.wait_ge(S["bank_free"], n + 1 + 2)
                STT(xT[:, t, :], xT[:, t, :], 1.0, xp[:, b, 0:T], ALU.add, ALU.mult).then_inc(S["tmp_free"], 1)
                lo_split(n + 2, (j + 2) % 4)
                if j % 2 == 0:
                    dve.wait_ge(S["rs_done"], 2 * i + j // 2 + 1)
                    for e in range(2):
                        ch.note(TT(og[e][:, :], Q[:, t + e, :], rs[:, e, :], ALU.mult))
                    ch.wait()
                    for e in range(2):
                        STT(og[e][:, :], og[e][:, :], og_g, V[:, t + e, :], ALU.mult, ALU.mult)\
                            .then_inc(S["og_done"], 1)
                else:
                    for e in range(2):
                        dve.wait_ge(S["og_hi"], t + e)
                        TT(b_lo[:, t - 1 + e, :], og[e][:, :], b_hi[:, t - 1 + e, :].bitcast(F32), ALU.subtract)\
                            .then_inc(S["og_split"], 1)
            ch.end(2)

        def late(r, bk, name, b0):
            return columns(r, bk, name, b0)

        dve.wait_ge(S["oss_ready"], HP)
        dve.wait_ge(S["rs_done"], HP)
        V_.memset(B2, 0.0).then_inc(S["ada_row_sb"], 1)
        late(1, B3, "ada_b", 16).then_inc(S["mod_done"], 1)
        with dve.Fori(0, 2) as i:
            for j in range(4):
                t, b = 4 * i + j, j % 2
                n = N_WB + t
                dve.wait_ge(S["bank_free"], n + 1 + 2)
                ins = STT(acc[:, b, 0:T], K[:, t, :], 1.0, xp[:, b, 0:T], ALU.add, ALU.mult)
                ins.then_inc(S["tmp_free"], 1)
                dve.wait_ge(S["tmp_free"], 2 + KT + t + 1)
                TT(acc[:, b, 0:T], acc[:, b, 0:T], xT[:, t, :], ALU.add).then_inc(S["y_done"], 1)
                lo_split(n + 2, (j + 2) % 4)
                dve.wait_ge(S["y_hi"], t + 1)
                TT(a_lo[:, t, :], acc[:, b, 0:T], a_hi[:, t, :].bitcast(F32), ALU.subtract).then_inc(S["y_split"], 1)
        V_.memset(B2, 0.0).then_inc(S["ada_row_sb"], 1)
        ch.link(late(2, B3, "ada_b", 32))
        scale_of(1, 2, 0, "norm2_g").then_inc(S["mod_done"], 1)
        dve.wait_ge(S["mod_done"], 3)
        dve.wait_ge(S["x_back_in"], 16)
        for t in range(KT):
            n, b = N_WO + t, t % 2
            dve.wait_ge(S["bank_free"], n + 1 + 2)
            for g, c in GR:
                last = STT(xT[:, t, c], xp[:, b, c], mod[:, 1, t, g:g + 1], x_back[:, t, c], ALU.mult, ALU.add)
            last.then_inc(S["tmp_free"], 1)
            lo_split(n + 2, (n + 2) % 4)
        dve.wait_ge(S["rstd_done"], 2)
        dve.wait_ge(S["tmp_free"], 2 + 3 * KT)
        V_.memset(B2, 0.0).then_inc(S["ada_row_sb"], 1)
        norm(rstd2, 1, 1, KT)
        ch.link(late(3, B3, "final_b", 0))
        scale_of(2, 3, KT, "final_g").then_inc(S["mod_done"], 1)

        def ff1(q, n0):
            with dve.Fori(0, 2) as i:
                for j in range(4):
                    n, b, t = n0 + 4 * i + j, j % 2, 4 * i + j
                    dve.wait_ge(S["bank_free"], n + 1 + 2)
                    STT(acc[:, b, 0:T], xp[:, b, 0:T], 0.0, xp[:, b, 0:T], ALU.max, ALU.mult).then_inc(S["tmp_free"], 1)
                    lo_split(n + 2, (j + 2) % 4)
                    dve.wait_ge(S["f_hi_done"], KT * q + t + 1)
                    TT(f_lo[q % 2][:, t, :], acc[:, b, 0:T], f_hi[q % 2][:, t, :].bitcast(F32), ALU.subtract)\
                        .then_inc(S["f_split"], 1)

        def add_residual(t, b):
            for g, c in GR:
                last = STT(xT[:, t, c], xp[:, b, c], mod_c(t, g), xT[:, t, c], ALU.mult, ALU.add)
            return last

        def mod_c(t, g):
            return mod[:, 2, ds(t + KT, 1), g] if not isinstance(t, int) else mod[:, 2, t + KT:t + KT + 1, g]

        def ff2(q, n0):
            with dve.Fori(0, 2) as i:
                for j in range(4):
                    n, b, t = n0 + 4 * i + j, j % 2, 4 * i + j
                    dve.wait_ge(S["bank_free"], n + 1 + 2)
                    add_residual(t, b).then_inc(S["tmp_free"], 1)
                    lo_split(n + 2, (j + 2) % 4)

        dve.wait_ge(S["mod_done"], 4)
        ff1(0, N_FF)
        for q in range(3):
            ff1(q + 1, N_FF + 8 + 16 * q)
            ff2(q, N_FF + 16 + 16 * q)
        for t in range(KT):
            n, b = N_ALL - KT + t, t % 2
            dve.wait_ge(S["bank_free"], n + 1 + 2)
            add_residual(t, b).then_inc(S["tmp_free"], 1)
            if n + 2 < N_ALL:
                lo_split(n + 2, (n + 2) % 4)
        dve.wait_ge(S["rstd_done"], 3)
        dve.wait_ge(S["tmp_free"], 2 + 11 * KT)
        for f in range(KT):
            t = xp[:, f % 2, 0:T]
            if f >= 2:
                dve.wait_ge(S["yo_done"], f - 1)
            ch.link(TT(t, xT[:, f, :], rstd2[:, :], ALU.mult))
            for g, c in GR:
                last = TS_(y_fm[:, f, c], xp[:, f % 2, c], scales[:, 2, f, g:g + 1], mod[:, 3, f, g:g + 1],
                           ALU.mult, ALU.add)
            last.then_inc(S["yo_done"], 1)

    block.__exit__(None, None, None)


_INS = ["x_prompt", "x_sample", "cache_conv_a", "cache_conv_qkv", "state_delta", "c_prompt", "c_sample", "ada_w",
        "ada_b", "norm1_g", "norm2_g", "w_in", "conv_a_w", "conv_qkv_w", "a_log", "dt_bias", "out_norm_g",
        "w_a_out", "w_b_out", "w_o", "w_ff1", "w_ff2", "final_ada_w", "final_ada_b", "final_norm_g"]
_OUTS = [("y_p", (1, TP, D)), ("y_s", (1, TS, D)),
         ("ca_p", (1, 1, WA - 1, D)), ("cq_p", (1, 1, WB - 1, 3 * D)), ("s_p", (1, 1, H, P, P)),
         ("ca_s", (1, 1, WA - 1, D)), ("cq_s", (1, 1, WB - 1, 3 * D)), ("s_s", (1, 1, H, P, P))]


def kernel(**inputs):
    import numpy as _np
    import concourse.bacc as _bacc
    from concourse import mybir as _mybir
    from concourse.bass_utils import run_bass_kernel_spmd as _run

    nc = _bacc.Bacc("TRN2", target_bir_lowering=False, num_devices=1)
    arrays, t_in, t_out = {}, {}, {}
    for name in _INS:
        a = _np.ascontiguousarray(inputs[name])
        arrays[f"in_{name}"] = a
        t_in[name] = nc.dram_tensor(f"in_{name}", a.shape, _mybir.dt.from_np(a.dtype), kind="ExternalInput").ap()
    for name, shape in _OUTS:
        t_out[name] = nc.dram_tensor(f"out_{name}", shape, _mybir.dt.float32, kind="ExternalOutput").ap()
    build(nc, t_in, t_out)
    r = _run(nc, [arrays], core_ids=[0])
    return tuple(r.results[0][f"out_{name}"] for name, _ in _OUTS)
```

```python
import concourse.bass as bass
from concourse import mybir
from concourse.bass import ds

F32 = mybir.dt.float32
F32R = mybir.dt.float32r
ALU = mybir.AluOpType
ACT = mybir.ActivationFunctionType

P = 128
D = 1024
KT = D // P
TP, TS = 512, 64
T = TP + TS
HALF = T // 2
CH = 64
NCH = T // CH
H = 8
HP = H // 2
WA, WB = 3, 4
LEVELS = 6
NEXP = 5
EPS = 1e-6
NQKV = 24
DFF = 4096

C_PB, C_PC, C_PH, C_QKV, C_Z, C_AB, C_GA, C_GB = 0, 1024, 2048, 3072, 6144, 7168, 7184, 8208

N_QKV, N_MIX, N_TAIL, N_WA, N_WB, N_WO, N_FF = 0, 24, 56, 72, 80, 88, 96
N_ALL = 160
RAW, SLOT = 4, 2

VEC = {}
_at = 0
for _name, _n in (("conv_qkv_w", WB * NQKV), ("conv_a_w", WA * KT), ("norm1_g", KT),
                  ("cache_qkv", (WB - 1) * NQKV), ("cache_a", (WA - 1) * KT), ("norm2_g", KT), ("final_g", KT),
                  ("out_g", 1), ("c_p", KT), ("c_s", KT), ("pad", 7),
                  ("ada_b", 6 * KT), ("final_b", 2 * KT)):
    VEC[_name] = (_at, _n)
    _at += _n
NVEC = _at


class Chain:

    def __init__(self, eng, sem):
        self.eng, self.sem, self.n, self.base = eng, sem, 0, 0

    def link(self, ins):
        ins.then_inc(self.sem, 1)
        self.n += 1
        self.wait()

    def wait(self):
        self.eng.wait_ge(self.sem, self.base + self.n)

    def note(self, ins):
        ins.then_inc(self.sem, 1)
        self.n += 1

    def loop(self, i, per):
        self.base, self.start, self.per = self.base + self.n + i * per, self.base + self.n, per
        self.n = 0

    def end(self, passes):
        assert self.n == self.per, (self.n, self.per)
        self.base, self.n = self.start + passes * self.per, 0


def whole(eng, value):
    return value if isinstance(value, int) else eng.compute_val(value)


def build(nc, t_in, t_out):
    SB0 = -(-nc.sbuf_base // 32) * 32
    cur = [SB0]

    def sb(name, shape, dt=F32, at=None):
        size = 4
        for s in shape[1:]:
            size *= s
        size = -(-size // 32) * 32
        if at is None:
            at = cur[0]
            cur[0] += size
        return nc.alloc_sbuf_tensor_at(name, shape, dt, offset=at)

    def region(size):
        at = cur[0]
        cur[0] += -(-size // 32) * 32
        return at

    TILE8 = KT * T * 4

    r_x = region(TILE8)
    xT = sb("xT", [P, KT, T], at=r_x)
    a_hi = sb("a_hi", [P, KT, T], F32R)
    a_lo = sb("a_lo", [P, KT, T], F32R)
    w_raw = sb("w_raw", [P, RAW, KT, P])
    w_hi = sb("w_hi", [P, SLOT, KT, P], F32R)
    w_lo = sb("w_lo", [P, SLOT, KT, P], F32R)
    r_q, r_k, r_v, r_u = region(TILE8), region(TILE8), region(TILE8), region(TILE8)
    qkv = sb("qkv", [P, NQKV, T], at=r_q)
    Q, K, V = qkv[:, 0:8, :], qkv[:, 8:16, :], qkv[:, 16:24, :]
    U = sb("U", [P, KT, T], at=r_u)
    b_hi = sb("b_hi", [P, KT, T], F32R, at=r_u)
    b_lo = sb("b_lo", [P, KT, T], F32R, at=r_v)
    f_hi = [sb("f0_hi", [P, KT, T], F32R, at=r_q), sb("f1_hi", [P, KT, T], F32R, at=r_v)]
    f_lo = [sb("f0_lo", [P, KT, T], F32R, at=r_k), sb("f1_lo", [P, KT, T], F32R, at=r_u)]
    ada0_w = sb("ada0_w", [P, KT, 2 * D], at=r_q)
    x_back = sb("x_back", [P, KT, T], at=r_q)
    y_fm = sb("y_fm", [P, KT, T], at=r_q)
    y_tok = sb("y_tok", [P, 5, D], at=r_k)

    ident = sb("ident", [P, P])
    ones = sb("ones", [P, P])
    id64 = sb("id64", [P, CH])
    neg = sb("neg", [P, CH])
    lvl = sb("lvl", [P, LEVELS, CH])
    vecs = sb("vecs", [P, NVEC])
    mod = sb("mod", [P, 4, 16, 2])
    scales = sb("scales", [P, 3, KT, 2])
    rows = sb("rows", [P, T])
    r_rows = cur[0] - T * 4
    c_act = sb("c_act", [P, KT, 2])
    mrow_l = sb("mrow_l", [P, 512], at=r_rows)
    tokv = sb("tokv", [P, NCH, 12])
    tails = sb("tails", [P, 2, (WB - 1) * NQKV + (WA - 1) * KT])
    bias = sb("bias", [P, 8])
    r_xp = region(2 * 584 * 4)
    xp = sb("xp", [P, 2, 584], at=r_xp)
    r_acc = region(2 * 584 * 4)
    acc = sb("acc", [P, 2, 584], at=r_acc)
    r_ds = cur[0]
    x_tok = sb("x_tok", [P, 5, D], at=r_ds)
    ab_raw = sb("ab_raw", [P, KT, CH], at=r_ds + 20480)
    ab_hi = sb("ab_hi", [P, KT, CH], F32R, at=r_ds + 22528)
    ab_lo = sb("ab_lo", [P, KT, CH], F32R, at=r_ds + 24576)
    vrows = sb("vrows", [P, 3, P], at=r_ds + 26624)
    mrow = sb("mrow", [P, 512], at=r_ds + 28160)
    rstd1 = sb("rstd1", [P, T], at=r_ds + 30208)
    ab_sb, ab_e, ab_sp, row_g, row_e, row_b, cmask = (sb(f"row{i}", [P, T], at=r_ds + i * T * 4) for i in range(7))
    sq = sb("sq", [P, 2, H, CH], at=r_ds)
    kq = sb("kq", [P, 2, H, CH], at=r_ds + 4096)
    vn = sb("vn", [P, HP, P], at=r_ds + 4096)
    vc = sb("vc", [P, H, CH], at=r_ds + 8192)
    qd = sb("qd", [P, H, CH], at=r_ds + 8192)
    decs = sb("decs", [P, 2, HP, CH], at=r_ds + 10240)
    dec, decb = decs[:, 0], decs[:, 1]
    p1 = sb("p1", [P, HP, CH], at=r_ds + 11264)
    at_ = sb("at", [P, HP, CH], at=r_ds + 12288)
    qkt = sb("qkt", [P, HP, CH], at=r_ds + 13312)
    nb = sb("nb", [P, 3, HP, CH], at=r_ds + 14336)
    mm = sb("mm", [P, 2, HP, CH], at=r_ds + 17408)
    egs = sb("egs", [P, 2, H, CH], at=r_ds + 19456)
    eg, kbe = egs[:, 0], egs[:, 1]
    kdt = sb("kdt", [P, HP, P], at=r_ds + 23552)
    vb = sb("vb", [P, HP, P], at=r_ds + 25600)
    st = sb("st", [P, H, P], at=r_ds + 27648)
    AS = 3
    ada_w = sb("ada_w", [P, AS, 2 * D], at=r_ds)
    rs = sb("rs", [P, 2, T], at=r_ds + 24576)
    og = [sb("og_0", [P, T], at=r_rows), sb("og_1", [P, T], at=r_ds + 29184)]
    rstd2 = sb("rstd2", [P, T], at=r_ds + 24576)
    tail_rows = [sb(f"tail_rows{g}", [P, P], at=r_ds + 29184 + 512 * g) for g in range(2)]
    assert r_ds + 32512 <= nc.sbuf_usable_end, (r_ds + 32512, nc.sbuf_usable_end)

    norm_buf = [xp[:, 0, 0:T], xp[:, 1, 0:T], acc[:, 0, 0:T], acc[:, 1, 0:T]]
    gp = nc.alloc_psum_tensor("gp", [P, 4, 512], F32)
    dp = nc.alloc_psum_tensor("dp", [P, 4, 512], F32)
    B0, B1, B2, B3 = (dp[:, i, :] for i in range(4))

    x_spill = nc.dram_tensor("x_spill", [P, KT, T], F32, kind="Internal").ap()

    gate_e = nc.dram_tensor("gate_e", [NCH, 2, H, CH], F32, kind="Internal").ap()
    gate_g = nc.dram_tensor("gate_g", [NCH, 2, 2, HP, CH], F32, kind="Internal").ap()

    names = """gates_spilled gates_in kbe_done ks_ready rhs_done rows_in x_in ab_in s_in s_out pool_ready consts zeros_ready
        dve_own act_own pool_own
        vecs_t vecs_done xt_ready xt_done sq_done ss_all rstd_done t_done hi_split h_ready c_act ada0_used row_v row_a
        ada_rows ada_row_sb ada_t mod_done ada_used
        ab_split ab_hi_done ab_ready ab_rows tok_t tok_done spilled x_back_in
        w_hi_done w_lo_done tile_done bank_free
        pads_done tails_done acc_free conv_done qkv_done
        pc_sb ph_sb pb_sb prod_done u_done prod_free pads_a
        o_free s_done sq_ready bc_ready ss_ready eg_done rkq_done kq_done vc_done dd_done dec_done decb_done
        tr_ready kkqk_ready tokmul_done at_done nb_done mt_done m0_ready m0_done p1_ready p1_done x_ready m_done
        wt_ready nw_done vn_ready vn_done o_ready o_done ds_ready qd_done
        added squared z_done ga_done u_hi u_split tmp_sb tmp_free osq_done oss_ready rs_done og_done og_hi og_split
        t2_done y_done y_hi y_split x1_done sq2_done f_done f_hi_done f_split
        caches_out yo_done yt_ready yt_done out_done tail_t tail_sb""".split()
    S = {n: nc.alloc_semaphore(n) for n in names}
    raw_full = [nc.alloc_semaphore(f"w_raw_full{i}") for i in range(RAW)]
    ada_full = [nc.alloc_semaphore(f"ada_full{i}") for i in range(8)]
    late_full = [nc.alloc_semaphore(f"late_full{i}") for i in range(3)]

    A = t_in
    w_in, w_a, w_b, w_o = A["w_in"][0], A["w_a_out"][0], A["w_b_out"][0], A["w_o"][0]
    w_ff1, w_ff2 = A["w_ff1"][0], A["w_ff2"][0]

    def wt(w, col, row=0):
        return w.rearrange("(k p) n -> p k n", p=P)[:, ds(row, KT) if not isinstance(row, int) else slice(row, row + KT),
                                                    ds(col, P)]

    ada_v = A["ada_w"][0].rearrange("(k p) n -> p k n", p=P)
    fin_v = A["final_ada_w"].rearrange("(k p) n -> p k n", p=P)

    def vec(name, j=0):
        return vecs[:, VEC[name][0] + j:VEC[name][0] + j + 1]

    block = nc.Block()
    block.__enter__()

    @block.sync
    def _(sp):
        def row(name, src):
            at, n = VEC[name]
            sp.dma_start(vrows[at % P:at % P + n, at // P, :], src).then_inc(S["rows_in"], 16)

        row("c_p", A["c_prompt"].rearrange("b (n p) -> (b n) p", p=P))
        row("c_s", A["c_sample"].rearrange("b (n p) -> (b n) p", p=P))
        row("conv_qkv_w", A["conv_qkv_w"][0].rearrange("j (n p) -> (j n) p", p=P))
        row("conv_a_w", A["conv_a_w"][0].rearrange("j (n p) -> (j n) p", p=P))
        row("norm1_g", A["norm1_g"].rearrange("l (n p) -> (l n) p", p=P))
        row("cache_qkv", A["cache_conv_qkv"][0, 0].rearrange("j (n p) -> (j n) p", p=P))
        row("cache_a", A["cache_conv_a"][0, 0].rearrange("j (n p) -> (j n) p", p=P))
        row("norm2_g", A["norm2_g"].rearrange("l (n p) -> (l n) p", p=P))
        row("final_g", A["final_norm_g"].rearrange("(n p) -> n p", p=P))
        row("out_g", A["out_norm_g"])
        row("pad", A["norm2_g"].rearrange("l (n p) -> (l n) p", p=P)[0:7])
        row("ada_b", A["ada_b"].rearrange("l (n p) -> (l n) p", p=P))
        row("final_b", A["final_ada_b"].rearrange("(n p) -> n p", p=P))
        sp.dma_start(x_tok[:, 0:4, :], A["x_prompt"][0].rearrange("(t p) d -> p t d", p=P)).then_inc(S["x_in"], 16)
        sp.dma_start(x_tok[0:TS, 4, :], A["x_sample"][0]).then_inc(S["x_in"], 16)
        for k in range(KT):
            sp.dma_start(ada0_w[:, k, :], ada_v[:, k, 0:2 * D]).then_inc(ada_full[k], 16)
        sp.wait_ge(S["zeros_ready"], 1)
        v = w_in.rearrange("(k p) n -> p k n", p=P)
        with nc.allow_non_contiguous_dma(reason="16 columns"):
            sp.dma_start(ab_raw[:, :, 0:8], v[:, :, C_AB:C_AB + 8]).then_inc(S["ab_in"], 16)
            sp.dma_start(ab_raw[:, :, 32:40], v[:, :, C_AB + 8:C_AB + 16]).then_inc(S["ab_in"], 16)
            sp.dma_start(bias[0:H, 0:1], A["dt_bias"].rearrange("l h -> h l")).then_inc(S["ab_in"], 16)
            sp.dma_start(bias[0:H, 1:2], A["a_log"].rearrange("l h -> h l")).then_inc(S["ab_in"], 16)

        def load(n, group, j, src):
            if not (isinstance(group, int) and group == 0):
                value = whole(sp, n - 3)
                sp.wait_ge(S["zeros_ready"], 1)
                sp.wait_ge(S["w_lo_done"], value)
            sp.dma_start(w_raw[:, j, :, :], src).then_inc(raw_full[j], 16)

        for j in range(4):
            load(j, 0, j, wt(w_in, C_QKV + j * P))
        sp.wait_ge(S["xt_done"], KT)
        sp.dma_start(x_spill, xT[:, :, :]).then_inc(S["spilled"], 16)
        with sp.Fori(1, NQKV // 4) as i:
            for j in range(4):
                load(4 * i + j, i, j, wt(w_in, C_QKV + j * P + i * (4 * P)))
        sp.wait_ge(S["ab_rows"], 1)
        sp.wait_ge(S["row_a"], 3)
        for e in range(2):
            for q in range(2):
                sp.dma_start(gate_g[:, e, q].rearrange("c m i -> m c i"),
                             rows[32 * q + e:32 * q + H:2, :].rearrange("p (c i) -> p c i", c=NCH))\
                    .then_inc(S["gates_spilled"], 16)
        for q, src in enumerate((row_e[0:H, :], rows[96:96 + H, :])):
            sp.dma_start(gate_e[:, q].rearrange("c h i -> h c i"), src.rearrange("p (c i) -> p c i", c=NCH))\
                .then_inc(S["gates_spilled"], 16)
        sp.wait_ge(S["gates_spilled"], 96)

        def gates(c):
            value = whole(sp, c + 1)
            sp.wait_ge(S["zeros_ready"], 1)
            sp.wait_ge(S["s_done"], value)
            for e in range(2):
                src = gate_g[ds(c, 1), e].rearrange("o q m i -> o (q m i)").to_broadcast([CH, 2 * HP * CH])
                sp.dma_start(decs[64 * e:64 * e + 64, :, :, :].rearrange("p q m i -> p (q m i)"), src)\
                    .then_inc(S["gates_in"], 16)
            src = gate_e[ds(c, 1)].rearrange("o q h i -> o (q h i)").to_broadcast([P, 2 * H * CH])
            sp.dma_start(egs[:, :, :, :].rearrange("p q h i -> p (q h i)"), src).then_inc(S["gates_in"], 16)

        with sp.Fori(0, KT) as i:
            for j, c in enumerate((C_PC, C_PH, C_PB, C_GA)):
                load(N_MIX + 4 * i + j, i + 6, j, wt(w_in, c + i * P))
            gates(i)
        for j, c in enumerate((C_Z, C_GB, C_Z + P, C_GB + P)):
            load(N_TAIL + j, N_TAIL // 4, j, wt(w_in, c))
        gates(KT)
        with sp.Fori(1, KT // 2) as i:
            for j, c in enumerate((C_Z, C_GB, C_Z + P, C_GB + P)):
                load(N_TAIL + 4 * i + j, i + 14, j, wt(w_in, c + i * (2 * P)))

        def group8(n0, w, col=0, row=0):
            with sp.Fori(0, 2) as i:
                for j in range(4):
                    load(n0 + 4 * i + j, i + n0 // 4, j, wt(w, col + j * P + i * (4 * P), row))

        group8(N_WA, w_a)
        group8(N_WB, w_b)
        sp.wait_ge(S["spilled"], 16)
        sp.wait_ge(S["og_split"], 1 + KT)
        sp.dma_start(x_back[:, :, :], x_spill).then_inc(S["x_back_in"], 16)
        group8(N_WO, w_o)
        group8(N_FF, w_ff1)
        for q in range(3):
            group8(N_FF + 8 + 16 * q, w_ff1, (q + 1) * D)
            group8(N_FF + 16 + 16 * q, w_ff2, 0, q * KT)
        group8(N_ALL - 8, w_ff2, 0, 3 * KT)
        sp.wait_ge(S["yt_done"], 5)
        sp.dma_start(t_out["y_p"][0].rearrange("(t p) d -> p t d", p=P), y_tok[:, 0:4, :]).then_inc(S["out_done"], 16)
        sp.dma_start(t_out["y_s"][0], y_tok[0:TS, 4, :]).then_inc(S["out_done"], 16)
        sp.wait_ge(S["out_done"], 32)
        sp.wait_ge(S["caches_out"], 64)
        sp.wait_ge(S["s_out"], 32)

    @block.gpsimd
    def _(pool):
        ch = Chain(pool, S["pool_own"])
        ch.note(pool.memset(ones[:, :], 1.0))
        ch.note(pool.memset(ident[:, :], 0.0))
        ch.note(pool.memset(id64[:, :], 0.0))
        ch.note(pool.memset(neg[:, :], 0.0))
        ch.note(pool.memset(lvl[:, :, :], 0.0))
        ch.note(pool.memset(rows[:, :], 0.0))
        ch.note(pool.memset(bias[:, :], 0.0))
        ch.link(pool.memset(ab_raw[:, :, :], 0.0))
        ch.link(pool.affine_select(out=ident[:, :], in_=ident[:, :], compare_op=ALU.not_equal, fill=1.0, base=0,
                                   pattern=[[-1, P]], channel_multiplier=1))
        pool.memset(bias[:, 2:3], EPS).then_inc(S["consts"], 1)
        pool.memset(bias[:, 3:4], -0.5 * 4.852030263919617).then_inc(S["consts"], 1)
        pool.memset(acc[:, 1, 576:584], 0.0).then_inc(S["zeros_ready"], 1)
        pool.memset(acc[:, 0, 0:1], 0.0).then_inc(S["acc_free"], 2)
        pool.memset(acc[:, 0, 1:2], 0.0).then_inc(S["tails_done"], 2)
        pool.memset(acc[:, 0, 2:3], 0.0).then_inc(S["o_free"], 1)
        pool.memset(acc[:, 0, 3:4], 0.0).then_inc(S["tmp_free"], 2)
        pool.memset(acc[:, 0, 4:5], 0.0).then_inc(S["og_split"], 1)
        pool.memset(acc[:, 0, 5:6], 0.0).then_inc(S["prod_free"], 1)
        pool.memset(acc[:, 0, 8:9], 0.0).then_inc(S["rs_done"], 1)
        pool.memset(acc[:, 0, 7:8], 0.0).then_inc(S["bank_free"], 2)
        pool.wait_ge(S["bank_free"], 2)
        for p in range(2):
            b, base = slice(64 * p, 64 * p + 64), 0
            ch.link(pool.affine_select(out=id64[b, :], in_=id64[b, :], compare_op=ALU.not_equal, fill=1.0,
                                       base=base, pattern=[[-1, CH]], channel_multiplier=1))
            ch.link(pool.affine_select(out=neg[b, :], in_=neg[b, :], compare_op=ALU.is_ge, fill=-1e30,
                                       base=base, pattern=[[1, CH]], channel_multiplier=-1))
        for l in range(LEVELS):
            s = 1 << l
            v = lvl[:, l, :].rearrange("p (g r) -> p g r", r=2 * s)
            ch.link(pool.memset(v[:, :, s:2 * s], -1.0))
            for p in range(2):
                b = slice(64 * p, 64 * p + 64)
                w = v[b, :, s:2 * s]
                ch.link(pool.affine_select(out=w, in_=w, compare_op=ALU.is_ge, fill=0.0, base=0,
                                           pattern=[[-2 * s, CH // (2 * s)], [0, s]], channel_multiplier=1))
                ch.link(pool.affine_select(out=w, in_=w, compare_op=ALU.is_ge, fill=0.0, base=s - 1,
                                           pattern=[[2 * s, CH // (2 * s)], [0, s]], channel_multiplier=-1))
        pool.memset(acc[:, 0, 6:7], 0.0).then_inc(S["pool_ready"], 1)

        c0, t0 = VEC["cache_qkv"][0], (WB - 1) * NQKV
        cache_v = vecs[:, c0:c0 + t0].rearrange("p (j n) -> p n j", j=WB - 1)
        tails_v = tails[:, :, 0:t0].rearrange("p g (j n) -> p g n j", j=WB - 1)
        pool.wait_ge(S["vecs_done"], 1)
        pool.wait_ge(S["h_ready"], KT)
        with pool.Fori(0, NQKV // 2) as i:
            for b in range(2):
                n = 2 * i + b
                pool.wait_ge(S["acc_free"], n + 1)
                pool.tensor_copy(xp[:, b, 515:518], cache_v[:, n, :]).then_inc(S["pads_done"], 1)
                pool.wait_ge(S["bank_free"], n + 1 + 2)
                pool.tensor_copy(tails_v[:, 0, n, :], xp[:, b, 512:515])
                pool.tensor_copy(tails_v[:, 1, n, :], xp[:, b, 579:582]).then_inc(S["tails_done"], 1)

        ca0, ta0 = VEC["cache_a"][0], (WA - 1) * KT
        cache_a = vecs[:, ca0:ca0 + ta0].rearrange("p (j n) -> p n j", j=WA - 1)
        tails_a = tails[:, :, t0:t0 + ta0].rearrange("p g (j n) -> p g n j", j=WA - 1)

        def pads(i):
            value = whole(pool, i + 1)
            pool.wait_ge(S["vecs_done"], 1)
            pool.wait_ge(S["prod_free"], value)
            pool.memset(acc[:, 0, 0:2], 0.0)
            pool.tensor_copy(acc[:, 0, 514:516], cache_a[:, i, :]).then_inc(S["pads_a"], 1)

        def tails_of(i):
            pool.wait_ge(S["prod_done"], i + 1)
            pool.tensor_copy(tails_a[:, 0, i, :], acc[:, 0, 512:514])
            pool.tensor_copy(tails_a[:, 1, i, :], acc[:, 0, 578:580]).then_inc(S["tails_done"], 1)

        def chunk_squares(c):
            cols = ds(c * CH, CH)
            pool.tensor_tensor(sq[:, 0], K[:, :, cols], K[:, :, cols], ALU.mult).then_inc(S["sq_ready"], 1)
            pool.tensor_tensor(sq[:, 1], Q[:, :, cols], Q[:, :, cols], ALU.mult).then_inc(S["sq_ready"], 1)

        def chunk_values(c):
            cols = ds(c * CH, CH)
            pool.wait_ge(S["o_free"], c + 1)
            pool.tensor_tensor(vc[:, :, :], V[:, :, cols], ones[:, 0:CH].unsqueeze(1).to_broadcast([P, H, CH]), ALU.mult)\
                .then_inc(S["vc_done"], 1)

        def chunk_blocks(c):
            pool.wait_ge(S["at_done"], c + 1)
            for l in range(LEVELS):
                if l == 3:
                    pool.wait_ge(S["mt_done"], c + 1)
                elif l > 3:
                    pool.wait_ge(S["p1_ready"], c * NEXP + (l - 3))
                m = lvl[:, l, :].unsqueeze(1).to_broadcast([P, HP, CH])
                pool.tensor_tensor(nb[:, l % 3], at_[:, :, :], m, ALU.mult).then_inc(S["nb_done"], 1)

        pool.wait_ge(S["conv_done"], NQKV)
        pool.wait_ge(S["acc_free"], NQKV + 2)
        pool.wait_ge(S["ab_rows"], 1)
        pool.wait_ge(S["row_a"], 3)
        chunk_squares(0)
        with pool.Fori(0, KT) as i:
            pads(i)
            chunk_values(i)
            chunk_blocks(i)
            pool.wait_ge(S["kq_done"], i + 1)
            chunk_squares(i + 1)
            tails_of(i)
        chunk_values(KT)
        pool.wait_ge(S["s_done"], KT + 1)
        pool.dma_start(t_out["s_p"][0, 0].rearrange("h k v -> k h v"), st[:, :, :]).then_inc(S["s_out"], 16)
        pool.wait_ge(S["s_out"], 16)
        pool.dma_start(st[:, :, :], A["state_delta"][0, 0].rearrange("h k v -> k h v")).then_inc(S["s_in"], 16)
        chunk_blocks(KT)
        pool.wait_ge(S["s_done"], NCH + 1)
        pool.dma_start(t_out["s_s"][0, 0].rearrange("h k v -> k h v"), st[:, :, :]).then_inc(S["s_out"], 16)
        def ada_load(m):
            if m >= AS:
                pool.wait_ge(S["ada_used"], m - AS + 1)
            r, k = 1 + m // KT, m % KT
            src = ada_v[:, k, 2 * D * r:2 * D * (r + 1)] if r < 3 else fin_v[:, k, :]
            pool.dma_start(ada_w[:, m % AS, :], src).then_inc(late_full[m % AS], 16)

        pool.wait_ge(S["o_free"], NCH + 1)
        for m in range(KT + AS):
            ada_load(m)
        pool.wait_ge(S["s_out"], 32)
        for i in range(HP):
            if i:
                pool.wait_ge(S["oss_ready"], i)
            pool.tensor_tensor(acc[:, :, 0:T], Q[:, 2 * i:2 * i + 2, :], Q[:, 2 * i:2 * i + 2, :], ALU.mult)\
                .then_inc(S["osq_done"], 1)
        for m in range(KT + AS, 3 * KT):
            ada_load(m)
        pool.wait_ge(S["tail_sb"], 2)
        nb_, na_ = (WB - 1) * NQKV, (WA - 1) * KT
        for g, (cb, ca) in enumerate((("cq_p", "ca_p"), ("cq_s", "ca_s"))):
            pool.dma_start(t_out[cb][0, 0].rearrange("j (n p) -> (j n) p", p=P), tail_rows[g][0:nb_, :])\
                .then_inc(S["caches_out"], 16)
            pool.dma_start(t_out[ca][0, 0].rearrange("j (n p) -> (j n) p", p=P), tail_rows[g][nb_:nb_ + na_, :])\
                .then_inc(S["caches_out"], 16)

    @block.tensor
    def _(pe):
        T_ = nc.tensor

        def products(n, b, hi, lo, ready=None, start=0, k0=0, k1=KT):
            if k0 == 0:
                pe.wait_ge(S["w_lo_done"], n + 1)
                pe.wait_ge(S["bank_free"], n + 1)
            for k in range(k0, k1):
                if ready:
                    pe.wait_ge(S[ready], start + k + 1)
                for wp, ap in ((w_hi, hi), (w_hi, lo), (w_lo, hi)):
                    for h in range(2):
                        last = T_.matmul(gp[:, 2 * b + h, 0:HALF], wp[:, b, k, :],
                                         ap[:, k, h * HALF:(h + 1) * HALF],
                                         start=(k == 0 and wp is w_hi and ap is hi),
                                         stop=(k == KT - 1 and wp is w_lo))
            if k1 == KT:
                last.then_inc(S["tile_done"], 1)

        def ada(r, bank, weights, wait):
            for k in range(KT):
                wait(k)
                for j in range(4):
                    last = T_.matmul(bank[32 * j:32 * j + 2, :], c_act[:, k, :],
                                     weights(k)[:, 512 * j:512 * j + 512], start=(k == 0), stop=(k == KT - 1))
                last.then_inc(S["ada0_used"], 1)

        pe.wait_ge(S["rows_in"], 16 * 13)
        pe.wait_ge(S["consts"], 1)
        for g in range(3):
            n = min(P, NVEC - g * P)
            last = T_.transpose(B0[:, g * P:g * P + n], vrows[0:n, g, :], ident[0:n, 0:n])
        last.then_inc(S["vecs_t"], 1)
        pe.wait_ge(S["x_in"], 32)
        pe.wait_ge(S["vecs_done"], 1)

        def sums(f, name, a, b, n=0):
            pe.wait_ge(S[name], n + f + 1)
            for h, bank in enumerate((a, b)):
                last = T_.matmul(bank[:, 0:HALF], ones[:, :], acc[:, f % 2, h * HALF:(h + 1) * HALF],
                                 start=(f == 0), stop=(f == KT - 1))
            last.then_inc(S["ss_all"], 1)

        for f in range(KT):
            b = f % 2
            if f >= 2:
                pe.wait_ge(S["xt_done"], f - 1)
            for t in range(4):
                T_.transpose(gp[:, 2 * b, t * P:(t + 1) * P], x_tok[:, t, f * P:(f + 1) * P], ident[:, :])
            T_.transpose(gp[:, 2 * b + 1, 0:TS], x_tok[0:TS, 4, f * P:(f + 1) * P], ident[0:TS, 0:TS])\
                .then_inc(S["xt_ready"], 1)
            if f:
                sums(f - 1, "sq_done", B0, B3)
        sums(KT - 1, "sq_done", B0, B3)
        pe.wait_ge(S["c_act"], 1)
        pe.wait_ge(S["ada_row_sb"], 1)
        ada(0, B1, lambda k: ada0_w[:, k, :], lambda k: pe.wait_ge(ada_full[k], 16))

        def ada_columns(bank, src, n):
            pe.wait_ge(S["ada_row_sb"], n)
            for s in range(4):
                last = T_.transpose(bank[:, s * P:(s + 1) * P], src[:, s * P:(s + 1) * P], ident[:, :])
            last.then_inc(S["ada_t"], 1)

        ada_columns(B2, mrow, 2)
        pe.wait_ge(S["ab_split"], 1)
        pe.wait_ge(S["mod_done"], 1)
        for k in range(KT):
            pe.wait_ge(S["h_ready"], k + 1)
            for wp, ap in ((ab_hi, a_hi), (ab_hi, a_lo), (ab_lo, a_hi)):
                for h, bank in enumerate((B1, B2)):
                    last = T_.matmul(bank[0:CH, 0:HALF], wp[:, k, :], ap[:, k, h * HALF:(h + 1) * HALF],
                                     start=(k == 0 and wp is ab_hi and ap is a_hi),
                                     stop=(k == KT - 1 and wp is ab_lo))
        last.then_inc(S["ab_ready"], 1)

        with pe.Fori(0, NQKV // 4) as i:
            for j in range(4):
                products(4 * i + j, j % 2, a_hi, a_lo)

        pe.wait_ge(S["ab_rows"], 1)
        pe.wait_ge(S["row_a"], 3)
        pe.wait_ge(S["pool_ready"], 1)
        for c in range(NCH):
            for p in range(2):
                sel = ident[:, :].rearrange("p (q r) -> p q r", q=4)[:, 0:3, p:H:2]
                last = T_.matmul(B2[64 * p:64 * p + 64, 12 * c:12 * c + 12], rows[:, c * CH:(c + 1) * CH], sel,
                                 start=True, stop=True)
        last.then_inc(S["tok_t"], 1)

        heads = [(p, hp, 2 * hp + p, slice(64 * p, 64 * p + 64)) for hp in range(HP) for p in range(2)]

        def squares(c):
            pe.wait_ge(S["o_free"], c + 1)
            for g, bank in enumerate((B0, B1)):
                pe.wait_ge(S["sq_ready"], 2 * c + g + 1)
                last = T_.matmul(bank[:, :], ones[:, :], sq[:, g], start=True, stop=True)
            last.then_inc(S["ss_ready"], 1)

        def turn(c):
            pe.wait_ge(S["kq_done"], c + 1)
            pe.wait_ge(S["vc_done"], c + 1)
            for hp in range(HP):
                T_.transpose(B0[:, hp * P:(hp + 1) * P], kq[:, 0, 2 * hp:2 * hp + 2, :].rearrange("p h i -> p (h i)"), ident[:, :])
            for hp in range(HP):
                last = T_.transpose(B1[:, hp * P:(hp + 1) * P], vc[:, 2 * hp:2 * hp + 2, :].rearrange("p h i -> p (h i)"), ident[:, :])
            last.then_inc(S["tr_ready"], 1)
            for p, hp, h, b in heads:
                last = T_.matmul(B2[b, hp * P:(hp + 1) * P], kq[:, 0, h, :], kq[:, :, h, :], start=True, stop=True)
            last.then_inc(S["kkqk_ready"], 1)

        def first_inverse(c):
            value = whole(pe, c + 1)
            pe.wait_ge(S["pool_ready"], 1)
            pe.wait_ge(S["mt_done"], value)
            for p, hp, h, b in heads:
                last = T_.matmul(B3[b, hp * CH:(hp + 1) * CH], mm[b, 1, hp, :], id64[b, :], start=True, stop=True)
            last.then_inc(S["m0_ready"], 1)

        def step_p(c, l):
            block_of = whole(pe, c * LEVELS + l + 1)
            sem, value = (S["m0_done"], c + 1) if l == 1 else (S["m_done"], c * NEXP + l - 1)
            value = whole(pe, value)
            pe.wait_ge(S["pool_ready"], 1)
            pe.wait_ge(S["nb_done"], block_of)
            pe.wait_ge(sem, value)
            for p, hp, h, b in heads:
                last = T_.matmul(B3[b, hp * CH:(hp + 1) * CH], nb[b, l % 3, hp, :], mm[b, 0, hp, :],
                                 start=True, stop=True)
            last.then_inc(S["p1_ready"], 1)

        def step_x(c, l):
            if l == 1:
                pe.wait_ge(S["at_done"], c + 1)
            value = whole(pe, c * NEXP + l)
            pe.wait_ge(S["pool_ready"], 1)
            pe.wait_ge(S["p1_done"], value)
            for p, hp, h, b in heads:
                if l < NEXP:
                    T_.matmul(B2[b, hp * CH:(hp + 1) * CH], mm[b, 1, hp, :], p1[b, hp, :], start=True, stop=True)
                last = T_.matmul(B2[b, (HP + hp) * CH:(HP + hp + 1) * CH], p1[b, hp, :], mm[b, 1, hp, :],
                                 start=True, stop=True)
            last.then_inc(S["x_ready"], 1)

        def s_product(c):
            value = whole(pe, c + 1)
            pe.wait_ge(S["pool_ready"], 1)
            pe.wait_ge(S["kbe_done"], value)
            pe.wait_ge(S["s_done"], value)
            pe.wait_ge(S["tokmul_done"], value)
            if isinstance(c, int):
                pe.wait_ge(S["s_in"], 16)
            for p, hp, h, b in heads:
                last = T_.matmul(B0[b, hp * P:(hp + 1) * P], kbe[:, h, :], st[:, h, :], start=True, stop=True)
            last.then_inc(S["ks_ready"], 1)

        def v_product(c):
            value, inverse = whole(pe, c + 1), whole(pe, (c + 1) * NEXP)
            pe.wait_ge(S["pool_ready"], 1)
            pe.wait_ge(S["m_done"], inverse)
            pe.wait_ge(S["rhs_done"], value)
            for p, hp, h, b in heads:
                last = T_.matmul(B3[b, hp * P:(hp + 1) * P], mm[b, 1, hp, :], vb[b, hp, :], start=True, stop=True)
            last.then_inc(S["vn_ready"], 1)

        def o_product(c):
            pe.wait_ge(S["vn_done"], c + 1)
            pe.wait_ge(S["qd_done"], c + 1)
            for p, hp, h, b in heads:
                bank = (B0, B1)[p]
                T_.matmul(bank[:, hp * CH:(hp + 1) * CH], st[:, h, :], qd[:, h, :], start=True, stop=False)
                last = T_.matmul(bank[:, hp * CH:(hp + 1) * CH], vn[b, hp, :], qkt[b, hp, :], start=False, stop=True)
            last.then_inc(S["o_ready"], 1)
            for p, hp, h, b in heads:
                bank = (B2, B3)[p]
                last = T_.matmul(bank[:, hp * P:(hp + 1) * P], kdt[b, hp, :], vn[b, hp, :], start=True, stop=True)
            last.then_inc(S["ds_ready"], 1)

        def mixed(n0, c, own):
            def part(k0, k1):
                j = k0 // KT
                products(n0 + j, j % 2, a_hi, a_lo, k0=k0 % KT, k1=k1 - j * KT)

            squares(c)
            part(0, 8)
            turn(c)
            part(8, 11)
            first_inverse(c)
            part(11, 12)
            step_p(c, 1)
            part(12, 13)
            step_x(c, 1)
            s_product(c)
            part(13, 14)
            step_p(c, 2)
            part(14, 15)
            step_x(c, 2)
            part(15, 16)
            part(16, 17)
            step_p(c, 3)
            part(17, 18)
            step_x(c, 3)
            part(18, 20)
            step_p(c, 4)
            part(20, 21)
            step_x(c, 4)
            part(21, 23)
            step_p(c, 5)
            part(23, 24)
            step_x(c, 5)
            part(24, 26)
            v_product(c)
            part(26, 27)
            o_product(c)
            part(27, 32)

        with pe.Fori(0, KT) as i:
            mixed(N_MIX + 4 * i, i, None)
        mixed(N_TAIL, KT, None)

        def ada_late(r, k):
            m = KT * (r - 1) + k
            if k == 0:
                pe.wait_ge(S["ada_row_sb"], 2 * r + 1)
            pe.wait_ge(late_full[m % AS], 16 * (m // AS + 1))
            for j in range(4):
                last = T_.matmul(B2[32 * j:32 * j + 2, :], c_act[:, k, :], ada_w[:, m % AS, 512 * j:512 * j + 512],
                                 start=(k == 0), stop=(k == KT - 1))
            last.then_inc(S["ada_used"], 1)

        for n in range(N_TAIL + 4, N_WA):
            products(n, n % 2, a_hi, a_lo)
            if n < N_TAIL + 4 + KT:
                ada_late(1, n - N_TAIL - 4)
            elif n == N_WA - 2:
                ada_columns(B3, mrow_l, 4)

        def total(name, n):
            pe.wait_ge(S[name], n)
            for h, bank in enumerate((B0, B1)):
                last = T_.matmul(bank[:, 0:HALF], ones[:, :], acc[:, 0, h * HALF:(h + 1) * HALF],
                                 start=True, stop=True)
            last.then_inc(S["ss_all"], 1)

        def group8(n0, hi, lo, ready=None, start=0, between=None):
            with pe.Fori(0, 2) as i:
                for j in range(4):
                    products(n0 + 4 * i + j, j % 2, hi, lo, ready, start)
                    if between and j % 2 == 0:
                        between(2 * i + j // 2)

        def o_sums(i):
            pe.wait_ge(S["osq_done"], i + 1)
            pe.wait_ge(S["rs_done"], i + 1)
            for e in range(2):
                for h in range(2):
                    last = T_.matmul(dp[:, 2 * e + h, 0:HALF], ones[:, :], acc[:, e, h * HALF:(h + 1) * HALF],
                                     start=True, stop=True)
            last.then_inc(S["oss_ready"], 1)

        group8(N_WA, a_hi, a_lo, "u_split", 0, o_sums)

        for k in range(KT):
            products(N_WB + k, k % 2, b_hi, b_lo, "og_split", 1)
            ada_late(2, k)
        for n in range(N_WO, N_WO + KT):
            products(n, n % 2, a_hi, a_lo, "y_split", 0)
            if n == N_WO + 1:
                ada_columns(B3, mrow_l, 6)
        total("sq2_done", 1)
        for k in range(KT):
            products(N_FF + k, k % 2, a_hi, a_lo, "h_ready", KT)
            ada_late(3, k)
        for q in range(3):
            group8(N_FF + 8 + 16 * q, a_hi, a_lo)
            if q == 0:
                ada_columns(B3, mrow_l, 8)
            group8(N_FF + 16 + 16 * q, f_hi[q % 2], f_lo[q % 2], "f_split", KT * q)
        for n in range(N_ALL - KT, N_ALL):
            products(n, n % 2, f_hi[1], f_lo[1], "f_split", KT * 3)
        total("sq2_done", 2)
        nt = (WB - 1) * NQKV + (WA - 1) * KT
        pe.wait_ge(S["mod_done"], 4)
        pe.wait_ge(S["tails_done"], 2 + NQKV + KT)
        for g in range(2):
            T_.transpose(dp[0:nt, 2 + g, 0:P], tails[:, g, :], ident[:, :]).then_inc(S["tail_t"], 1)
        pe.wait_ge(S["yo_done"], KT)
        for t in range(5):
            rows_n = P if t < 4 else TS
            if t >= 2:
                pe.wait_ge(S["yt_done"], t - 1)
            for f in range(KT):
                last = T_.transpose(gp[0:rows_n, 2 * (t % 2) + f // 4, (f % 4) * P:(f % 4 + 1) * P],
                                    y_fm[:, f, t * P:t * P + rows_n], ident[:, :])
            last.then_inc(S["yt_ready"], 1)

    @block.scalar
    def _(act):
        AC = nc.scalar.activation
        ch = Chain(act, S["act_own"])

        def w_split(n, group, j):
            act.wait_ge(raw_full[j], 16 * (group + 1))
            AC(w_hi[:, j % 2, :, :], w_raw[:, j, :, :], ACT.Copy).then_inc(S["w_hi_done"], 1)

        def bank(b):
            return gp[:, 2 * b:2 * b + 2, 0:HALF]

        def halves(t):
            return t.rearrange("p (h c) -> p h c", h=2)

        act.wait_ge(S["vecs_done"], 1)
        for g, name in enumerate(("c_p", "c_s")):
            a0 = VEC[name][0]
            last = AC(c_act[:, :, g], vecs[:, a0:a0 + KT], ACT.Silu)
        last.then_inc(S["c_act"], 1)
        for f in range(KT):
            b = f % 2
            act.wait_ge(S["xt_done"], f + 1)
            if f >= 2:
                act.wait_ge(S["ss_all"], f - 1)
            else:
                act.wait_ge(S["pool_ready"], 1)
            AC(acc[:, b, 0:T], xT[:, f, :], ACT.Square).then_inc(S["sq_done"], 1)

        def rstd(out, banks, name, n, scale):
            act.wait_ge(S[name], n)
            for h, bk in enumerate(banks):
                ch.note(AC(out[:, h * HALF:(h + 1) * HALF], bk[:, 0:HALF], ACT.Ln, bias=bias[:, 2:3], scale=scale))
            ch.wait()
            return AC(out[:, :], out[:, :], ACT.Exp, scale=-0.5)

        rstd(rstd1[:, :], (B0, B3), "ss_all", KT, 1.0 / D).then_inc(S["rstd_done"], 1)
        def ada_rows(bk, dst, n, r):
            act.wait_ge(S["ada0_used"] if r == 0 else S["ada_used"], n)
            AC(dst[:, :], bk[:, :], ACT.Copy).then_inc(S["ada_row_sb"], 1)

        ada_rows(B1, mrow, KT, 0)
        act.wait_ge(S["ab_in"], 64)
        AC(ab_hi[:, :, :], ab_raw[:, :, :], ACT.Copy).then_inc(S["ab_hi_done"], 1)
        def modulated(k, r, b0):
            for f in range(KT):
                act.wait_ge(S["t_done"], k * KT + f + 1)
                t = norm_buf[f % 4]
                for g, c in ((0, slice(0, TP)), (1, slice(TP, T))):
                    ch.note(AC(t[:, c], t[:, c], ACT.Identity, scale=scales[:, k, f, g:g + 1],
                               bias=mod[:, r, b0 + f, g:g + 1]))
                ch.wait()
                AC(a_hi[:, f, :], t, ACT.Copy).then_inc(S["hi_split"], 1)

        modulated(0, 0, 0)
        for j in range(2):
            w_split(j, 0, j)
        def gates(part):
            if part == 0:
                act.wait_ge(S["ab_ready"], 1)
                ch.note(AC(ab_sb[0:CH, 0:HALF], B1[0:CH, 0:HALF], ACT.Copy))
                ch.link(AC(ab_sb[0:CH, HALF:T], B2[0:CH, 0:HALF], ACT.Copy))
                ch.note(AC(ab_sb[0:32, :], ab_sb[0:32, :], ACT.Identity, bias=bias[0:32, 0:1]))
                ch.link(AC(ab_sb[32:CH, :], ab_sb[32:CH, :], ACT.Copy, scale=-1.0))
            elif part == 1:
                ch.note(AC(bias[0:H, 4:5], bias[0:H, 1:2], ACT.Exp))
                ch.link(AC(ab_e[0:CH, :], ab_sb[0:CH, :], ACT.Abs))
                ch.link(AC(ab_e[0:CH, :], ab_e[0:CH, :], ACT.Exp, scale=-1.0))
                AC(ab_e[0:CH, :], ab_e[0:CH, :], ACT.Ln, bias=ones[0:CH, 0:1])
                AC(bias[0:H, 5:6], bias[0:H, 4:5], ACT.Copy, scale=-1.0).then_inc(S["row_a"], 1)
            elif part == 2:
                act.wait_ge(S["row_v"], 1)
                AC(rows[32:32 + H, :], ab_sp[32:32 + H, :], ACT.Exp, scale=-1.0)
                AC(row_b[0:H, :], ab_sp[32:32 + H, :], ACT.Exp, scale=-1.0)
                act.wait_ge(S["row_v"], 2)
                AC(row_e[0:H, :], rows[0:H, :], ACT.Exp).then_inc(S["row_a"], 1)
                AC(rows[64:64 + H, :], row_g[0:H, :], ACT.Exp).then_inc(S["row_a"], 1)

        def qkv_in(n, group, j):
            b = j % 2
            act.wait_ge(S["tile_done"], n + 1)
            act.wait_ge(S["tails_done"], n + 1)
            AC(xp[:, b, 3:3 + HALF], gp[:, 2 * b, 0:HALF], ACT.Copy)
            AC(xp[:, b, 3 + HALF:3 + TP], gp[:, 2 * b + 1, 0:TP - HALF], ACT.Copy)
            AC(xp[:, b, 6 + TP:6 + T], gp[:, 2 * b + 1, TP - HALF:HALF], ACT.Copy).then_inc(S["bank_free"], 1)
            w_split(n + 2, group + (j + 2) // 4, (j + 2) % 4)

        def qkv_out(n, b):
            act.wait_ge(S["conv_done"], n + 1)
            AC(qkv[:, n, 0:TP], acc[:, b, 0:TP], ACT.Silu)
            AC(qkv[:, n, TP:T], acc[:, b, TP + 3:T + 3], ACT.Silu).then_inc(S["acc_free"], 1)

        for n in range(4):
            qkv_in(n, 0, n)
            if n:
                qkv_out(n - 1, (n - 1) % 2)
            gates(n)
        with act.Fori(1, NQKV // 4) as i:
            for j in range(4):
                qkv_in(4 * i + j, i, j)
                qkv_out(4 * i + j - 1, (j - 1) % 2)
        qkv_out(NQKV - 1, 1)

        def free(n, group, j):
            w_split(n + 2, group + (j + 2) // 4, (j + 2) % 4)

        def evac(n, b, out, func=ACT.Copy, scale=1.0, also=None, value=0):
            act.wait_ge(S["tile_done"], n + 1)
            if also:
                act.wait_ge(S[also], value)
            AC(halves(out), bank(b), func, scale=scale).then_inc(S["bank_free"], 1)

        def chunk_norms(c):
            act.wait_ge(S["ss_ready"], c + 1)
            for g, bk in enumerate((B0, B1)):
                ch.note(AC(sq[:, g], bk.rearrange("p (h i) -> p h i", h=H), ACT.Ln, bias=bias[:, 2:3]))
            ch.wait()
            AC(sq[:, 0], sq[:, 0], ACT.Exp, scale=-0.5)
            AC(sq[:, 1], sq[:, 1], ACT.Exp, scale=-0.5, bias=bias[:, 3:4]).then_inc(S["rkq_done"], 1)
            act.wait_ge(S["dd_done"], c + 1)
            AC(dec, dec, ACT.Exp).then_inc(S["dec_done"], 1)

        def step_copy(c, l):
            act.wait_ge(S["p1_ready"], c * NEXP + l)
            AC(p1[:, :, :], B3[:, 0:HP * CH].rearrange("p (h i) -> p h i", h=HP), ACT.Copy).then_inc(S["p1_done"], 1)

        def chunk_out(c):
            act.wait_ge(S["vn_ready"], c + 1)
            AC(vn[:, :, :], B3.rearrange("p (h v) -> p h v", h=HP), ACT.Copy).then_inc(S["vn_done"], 1)
            act.wait_ge(S["o_ready"], c + 1)
            q_v = Q.rearrange("p (hp e) t -> p e hp t", e=2)
            for p, bk in enumerate((B0, B1)):
                last = AC(q_v[:, p, :, ds(c * CH, CH)], bk[:, 0:HP * CH].rearrange("p (h i) -> p h i", h=HP), ACT.Copy)
            last.then_inc(S["o_free"], 1)

        act.wait_ge(S["spilled"], 16)
        act.wait_ge(S["tails_done"], NQKV + 2)
        with act.Fori(0, KT) as i:
            n0 = N_MIX + 4 * i
            ch.loop(i, 2)
            chunk_norms(i)
            evac(n0, 0, xp[:, 0, 0:T], also="u_done", value=i + 1)
            free(n0, 6 + i, 0)
            step_copy(i, 1)
            step_copy(i, 2)
            evac(n0 + 1, 1, xp[:, 1, 0:T])
            free(n0 + 1, 6 + i, 1)
            step_copy(i, 3)
            step_copy(i, 4)
            step_copy(i, 5)
            evac(n0 + 2, 0, xp[:, 0, 0:T], also="prod_done", value=i + 1)
            free(n0 + 2, 6 + i, 2)
            chunk_out(i)
            evac(n0 + 3, 1, xT[:, i, :])
            free(n0 + 3, 6 + i, 3)
            ch.end(KT)

        chunk_norms(KT)
        act.wait_ge(S["kq_done"], NCH)
        act.wait_ge(S["vc_done"], NCH)
        for j in range(4):
            n, t = N_TAIL + j, j // 2
            if j % 2 == 0:
                evac(n, 0, V[:, t, :], ACT.Copy)
            else:
                evac(n, 1, K[:, t, :], ACT.Copy)
            free(n, 14, j)
            for l in {0: (1, 2), 1: (3, 4, 5), 2: (), 3: ()}[j]:
                step_copy(KT, l)
            if j == 2:
                chunk_out(KT)
        for t in range(2):
            act.wait_ge(S["bank_free"], N_TAIL + 4 + 2)
            AC(V[:, t, :], V[:, t, :], ACT.Silu).then_inc(S["z_done"], 1)
            AC(K[:, t, :], K[:, t, :], ACT.Tanh, scale=0.5)
            AC(xT[:, t, :], xT[:, t, :], ACT.Tanh, scale=0.5).then_inc(S["ga_done"], 1)
        def tail4(i):
            for j in range(4):
                n, t = N_TAIL + 4 * i + j, 2 * i + j // 2
                if j % 2 == 0:
                    evac(n, 0, V[:, t, :], ACT.Silu)
                    free(n, 14 + i, j)
                    AC(xT[:, t, :], xT[:, t, :], ACT.Tanh, scale=0.5).then_inc(S["ga_done"], 1)
                else:
                    evac(n, 1, K[:, t, :], ACT.Tanh, scale=0.5)
                    free(n, 14 + i, j)

        with act.Fori(1, KT // 2 - 1) as i:
            tail4(i)
        ada_rows(B2, mrow_l, KT, 1)
        tail4(KT // 2 - 1)
        act.wait_ge(S["tile_done"], N_WA)
        act.wait_ge(S["u_done"], KT + 1)
        for t in range(KT):
            AC(a_hi[:, t, :], U[:, t, :], ACT.Copy).then_inc(S["u_hi"], 1)

        def o_norm(i):
            act.wait_ge(S["oss_ready"], i + 1)
            for e in range(2):
                for h in range(2):
                    ch.note(AC(rs[:, e, h * HALF:(h + 1) * HALF], dp[:, 2 * e + h, 0:HALF], ACT.Ln,
                               bias=bias[:, 2:3], scale=1.0 / P))
            ch.wait()
            AC(rs[:, :, :], rs[:, :, :], ACT.Exp, scale=-0.5).then_inc(S["rs_done"], 1)

        def og_hi(t, e):
            act.wait_ge(S["og_done"], t + 1)
            AC(b_hi[:, t, :], og[e][:, :], ACT.Copy).then_inc(S["og_hi"], 1)

        act.wait_ge(S["u_split"], KT)
        with act.Fori(0, 2) as i:
            ch.loop(i, 8)
            for j in range(4):
                n, b = N_WA + 4 * i + j, j % 2
                evac(n, b, xp[:, b, 0:T], scale=0.5, also="tmp_free", value=4 * i + j + 1)
                free(n, 18 + i, j)
                if j % 2 == 0:
                    o_norm(2 * i + j // 2)
                else:
                    og_hi(4 * i + j - 1, 0)
                    og_hi(4 * i + j, 1)
            ch.end(2)
        with act.Fori(0, 2) as i:
            for j in range(4):
                n, b = N_WB + 4 * i + j, j % 2
                evac(n, b, xp[:, b, 0:T], scale=0.5, also="tmp_free", value=8 + 4 * i + j + 1)
                free(n, 20 + i, j)
                act.wait_ge(S["y_done"], 4 * i + j + 1)
                AC(a_hi[:, 4 * i + j, :], acc[:, b, 0:T], ACT.Copy).then_inc(S["y_hi"], 1)
        ada_rows(B2, mrow_l, 2 * KT, 2)

        def squared(t, n, m):
            act.wait_ge(S["tmp_free"], n - N_WA + 3)
            if t >= 2:
                act.wait_ge(S["added"], m * (KT - 1) + t - 1)
            AC(acc[:, min(t, 1), 0:T], xT[:, t, :], ACT.Square).then_inc(S["squared"], 1)

        act.wait_ge(S["y_split"], KT)
        for t in range(KT):
            n, b = N_WO + t, t % 2
            evac(n, b, xp[:, b, 0:T], also="tmp_free", value=16 + t + 1)
            free(n, 22 + t // 4, t % 4)
            squared(t, n, 0)
        rstd(rstd2[:, :], (B0, B1), "ss_all", KT + 1, 1.0 / D).then_inc(S["rstd_done"], 1)
        modulated(1, 1, KT)

        def ff1(q, n0):
            with act.Fori(0, 2) as i:
                for j in range(4):
                    n, b, t = n0 + 4 * i + j, j % 2, 4 * i + j
                    evac(n, b, xp[:, b, 0:T], also="tmp_free", value=n - N_WA + 1)
                    free(n, n0 // 4 + i, j)
                    act.wait_ge(S["tmp_free"], n - N_WA + 3)
                    AC(f_hi[q % 2][:, t, :], acc[:, b, 0:T], ACT.Copy).then_inc(S["f_hi_done"], 1)

        def ff2(q, n0):
            with act.Fori(0, 2) as i:
                for j in range(4):
                    n, b = n0 + 4 * i + j, j % 2
                    evac(n, b, xp[:, b, 0:T], also="tmp_free", value=n - N_WA + 1)
                    free(n, n0 // 4 + i, j)

        ff1(0, N_FF)
        ada_rows(B2, mrow_l, 3 * KT, 3)
        for q in range(3):
            ff1(q + 1, N_FF + 8 + 16 * q)
            ff2(q, N_FF + 16 + 16 * q)
        for t in range(KT):
            n, b = N_ALL - KT + t, t % 2
            evac(n, b, xp[:, b, 0:T], also="tmp_free", value=n - N_WA + 1)
            if n + 2 < N_ALL:
                free(n, n // 4, n % 4)
            squared(t, n, 1)
        rstd(rstd2[:, :], (B0, B1), "ss_all", KT + 2, 1.0 / D).then_inc(S["rstd_done"], 1)
        for g in range(2):
            nt = (WB - 1) * NQKV + (WA - 1) * KT
            act.wait_ge(S["tail_t"], g + 1)
            AC(tail_rows[g][0:nt, :], dp[0:nt, 2 + g, 0:P], ACT.Copy).then_inc(S["tail_sb"], 1)
        for t in range(5):
            rn = P if t < 4 else TS
            act.wait_ge(S["yt_ready"], t + 1)
            AC(y_tok[0:rn, t, :].rearrange("p (h c) -> p h c", h=2), gp[0:rn, 2 * (t % 2):2 * (t % 2) + 2, :], ACT.Copy)\
                .then_inc(S["yt_done"], 1)

    @block.vector
    def _(dve):
        V_ = nc.vector
        TT, TS_, STT = V_.tensor_tensor, V_.tensor_scalar, V_.scalar_tensor_tensor
        ch = Chain(dve, S["dve_own"])
        GR = ((0, slice(0, TP)), (1, slice(TP, T)))

        def lo_split(n, j):
            dve.wait_ge(S["w_hi_done"], n + 1)
            TT(w_lo[:, j % 2, :, :], w_raw[:, j, :, :], w_hi[:, j % 2, :, :].bitcast(F32), ALU.subtract)\
                .then_inc(S["w_lo_done"], 1)

        dve.wait_ge(S["vecs_t"], 1)
        V_.tensor_copy(vecs[:, :], B0[:, 0:NVEC]).then_inc(S["vecs_done"], 1)
        dve.wait_ge(S["vecs_done"], 1)
        V_.memset(B1, 0.0).then_inc(S["ada_row_sb"], 1)
        for f in range(KT):
            b = f % 2
            dve.wait_ge(S["xt_ready"], f + 1)
            V_.tensor_copy(xT[:, f, 0:TP], gp[:, 2 * b, 0:TP])
            V_.tensor_copy(xT[:, f, TP:T], gp[:, 2 * b + 1, 0:TS]).then_inc(S["xt_done"], 1)

        def columns(r, bk, bias_name, b0):
            dve.wait_ge(S["ada_t"], r + 1)
            a0 = VEC[bias_name][0] + b0
            src = bk.rearrange("p (s j q) -> p j s q", s=4, j=4)[:, :, :, 0:2]
            bs = vecs[:, a0:a0 + 16].rearrange("p (j s) -> p j s", j=4).unsqueeze(3).to_broadcast([P, 4, 4, 2])
            return TT(mod[:, r].rearrange("p (j s) g -> p j s g", j=4), src, bs, ALU.add)

        def scale_of(k, r, b0, gname):
            a0 = VEC[gname][0]
            g = vecs[:, a0:a0 + KT].unsqueeze(2).to_broadcast([P, KT, 2])
            ch.link(TS_(scales[:, k], mod[:, r, b0:b0 + KT, :], 1.0, None, ALU.add))
            return TT(scales[:, k], scales[:, k], g, ALU.mult)

        ch.link(columns(0, B2, "ada_b", 0))
        scale_of(0, 0, KT, "norm1_g").then_inc(S["mod_done"], 1)
        dve.wait_ge(S["mod_done"], 1)
        dve.wait_ge(S["rstd_done"], 1)
        dve.wait_ge(S["ab_hi_done"], 1)
        TT(ab_lo[:, :, :], ab_raw[:, :, :], ab_hi[:, :, :].bitcast(F32), ALU.subtract).then_inc(S["ab_split"], 1)

        def norm(rstd, k):
            for f in range(KT + 2):
                if f < KT:
                    TT(norm_buf[f % 4], xT[:, f, :], rstd[:, :], ALU.mult).then_inc(S["t_done"], 1)
                if f >= 2:
                    dve.wait_ge(S["hi_split"], k * KT + f - 1)
                    TT(a_lo[:, f - 2, :], norm_buf[(f - 2) % 4], a_hi[:, f - 2, :].bitcast(F32), ALU.subtract)\
                        .then_inc(S["h_ready"], 1)
                    dve.wait_ge(S["h_ready"], k * KT + f - 1)

        norm(rstd1, 0)
        for j in range(2):
            lo_split(j, j)
        dve.wait_ge(S["h_ready"], KT)
        ch.link(V_.memset(xp[:, :, 0:3], 0.0))
        def gates(part):
            if part == 1:
                dve.wait_ge(S["row_a"], 1)
                ch.note(V_.memset(cmask[0:H, :], 1.0))
                ch.link(STT(ab_sp[0:CH, :], ab_sb[0:CH, :], 0.0, ab_e[0:CH, :], ALU.max, ALU.add))
                ch.note(V_.memset(cmask[0:H, :].rearrange("p (c i) -> p c i", i=CH)[:, :, 0:1], 0.0))
                TS_(row_g[0:H, :], ab_sp[0:H, :], bias[0:H, 5:6], None, ALU.mult).then_inc(S["row_v"], 1)
                dve.wait_ge(S["row_v"], 1)
                ch.wait()
                ch.link(V_.tensor_tensor_scan(rows[0:H, :], cmask[0:H, :], row_g[0:H, :], 0.0, ALU.mult, ALU.add))
                rv = rows[0:H, :].rearrange("p (c i) -> p c i", i=CH)
                TT(row_g[0:H, :].rearrange("p (c i) -> p c i", i=CH), rv[:, :, CH - 1:CH].to_broadcast([H, NCH, CH]),
                   rv, ALU.subtract).then_inc(S["row_v"], 1)
            elif part == 2:
                dve.wait_ge(S["row_a"], 2)
                TT(rows[96:96 + H, :], row_e[0:H, :], row_b[0:H, :], ALU.mult).then_inc(S["ab_rows"], 1)

        c0 = VEC["conv_qkv_w"][0]
        cw = vecs[:, c0:c0 + WB * NQKV].rearrange("p (j n) -> p j n", j=WB)
        W = TP + 3 + TS

        def conv(n, j):
            b = j % 2
            dve.wait_ge(S["bank_free"], n + 1 + 2)
            lo_split(n + 2, (j + 2) % 4)
            dve.wait_ge(S["pads_done"], n + 1)
            dve.wait_ge(S["acc_free"], n + 1)
            ch.link(TS_(acc[:, b, 0:W], xp[:, b, 0:W], cw[:, 0, ds(n, 1)], None, ALU.mult))
            for tap in range(1, WB):
                ins = STT(acc[:, b, 0:W], xp[:, b, tap:tap + W], cw[:, tap, ds(n, 1)], acc[:, b, 0:W],
                          ALU.mult, ALU.add)
                if tap < WB - 1:
                    ch.link(ins)
                else:
                    ins.then_inc(S["conv_done"], 1)

        for n in range(4):
            conv(n, n)
            gates(n)
        with dve.Fori(1, NQKV // 4) as i:
            ch.loop(i - 1, 12)
            for j in range(4):
                conv(4 * i + j, j)
            ch.end(NQKV // 4 - 1)
        dve.wait_ge(S["tok_t"], 1)
        V_.tensor_copy(tokv[:, :, :], B2[:, 0:NCH * 12].rearrange("p (c q) -> p c q", q=12)).then_inc(S["tok_done"], 1)
        dve.wait_ge(S["ab_rows"], 1)
        dve.wait_ge(S["row_a"], 3)
        V_.memset(st[:, :, :], 0.0).then_inc(S["s_done"], 1)
        dve.wait_ge(S["tok_done"], 1)
        V_.memset(bias[:, 7:8], 0.0).then_inc(S["u_done"], 1)

        par = [(p, slice(64 * p, 64 * p + 64)) for p in range(2)]

        def tok(c, q, n):
            return tokv[:, c, 4 * q:4 * q + 4].unsqueeze(2).to_broadcast([P, HP, n])

        def chunk_decay(c):
            dve.wait_ge(S["gates_in"], 48 * (c + 1))
            ch.link(TT(dec, dec, tok(c, 0, CH), ALU.subtract))
            TT(dec, dec, neg[:, :].unsqueeze(1).to_broadcast([P, HP, CH]), ALU.add)\
                .then_inc(S["dd_done"], 1)
            dve.wait_ge(S["rkq_done"], c + 1)
            cols = ds(c * CH, CH)
            TT(kq[:, 0], K[:, :, cols], sq[:, 0], ALU.mult)
            TT(kq[:, 1], Q[:, :, cols], sq[:, 1], ALU.mult).then_inc(S["kq_done"], 1)
            dve.wait_ge(S["dec_done"], c + 1)
            TT(decb, dec, decb, ALU.mult).then_inc(S["decb_done"], 1)
            dve.wait_ge(S["decb_done"], c + 1)

        def chunk_tokens(c):
            dve.wait_ge(S["kq_done"], c + 1)
            TT(kbe, kq[:, 0], kbe, ALU.mult).then_inc(S["kbe_done"], 1)
            dve.wait_ge(S["tr_ready"], c + 1)
            TT(qd[:, :, :], kq[:, 1], eg, ALU.mult).then_inc(S["qd_done"], 1)
            dve.wait_ge(S["kkqk_ready"], c + 1)
            v = B2.rearrange("p (h e i) -> p h e i", h=HP, e=2)
            TT(at_[:, :, :], v[:, :, 0, :], decb, ALU.mult)
            TT(qkt[:, :, :], v[:, :, 1, :], dec, ALU.mult).then_inc(S["at_done"], 1)
            k_v, v_v = (x.rearrange("p (h d) -> p h d", h=HP) for x in (B0, B1))
            TT(kdt[:, :, :], k_v, tok(c, 2, P), ALU.mult)
            dve.wait_ge(S["nb_done"], c * LEVELS + 1)
            TT(mm[:, 1], nb[:, 0], id64[:, :].unsqueeze(1).to_broadcast([P, HP, CH]), ALU.add).then_inc(S["mt_done"], 1)
            TT(vb[:, :, :], v_v, tok(c, 1, P), ALU.mult).then_inc(S["tokmul_done"], 1)
            dve.wait_ge(S["m0_ready"], c + 1)
            V_.tensor_copy(mm[:, 0], B3[:, 0:HP * CH].rearrange("p (h i) -> p h i", h=HP)).then_inc(S["m0_done"], 1)
            dve.wait_ge(S["mt_done"], c + 1)
            dve.wait_ge(S["m0_done"], c + 1)

        def rhs(c):
            dve.wait_ge(S["ks_ready"], c + 1)
            TT(vb[:, :, :], vb[:, :, :], B0.rearrange("p (h d) -> p h d", h=HP), ALU.subtract)\
                .then_inc(S["rhs_done"], 1)

        def step_add(c, l):
            dve.wait_ge(S["x_ready"], c * NEXP + l)
            g = 0 if l < NEXP else 1
            TT(mm[:, g:2], mm[:, g:2], B2[:, g * HP * CH:].rearrange("p (g h i) -> p g h i", h=HP, i=CH), ALU.add)\
                .then_inc(S["m_done"], 1)
            dve.wait_ge(S["m_done"], c * NEXP + l)

        def state(c):
            dve.wait_ge(S["ds_ready"], c + 1)
            for h in range(H):
                hp, bk = h // 2, (B2, B3)[h % 2]
                last = STT(st[:, h, :], st[:, h, :], eg[:, h, CH - 1:CH], bk[:, hp * P:(hp + 1) * P], ALU.mult, ALU.add)
            last.then_inc(S["s_done"], 1)
            dve.wait_ge(S["s_done"], c + 2)

        c0 = VEC["conv_a_w"][0]
        caw = vecs[:, c0:c0 + WA * KT].rearrange("p (j n) -> p j n", j=WA)
        WM = TP + 2 + TS
        with dve.Fori(0, KT) as i:
            n0 = N_MIX + 4 * i
            ch.loop(i, 3)
            chunk_decay(i)
            lo_split(n0 + 2, 2)
            chunk_tokens(i)
            step_add(i, 1)
            rhs(i)
            step_add(i, 2)
            dve.wait_ge(S["bank_free"], n0 + 1 + 3)
            dve.wait_ge(S["pads_a"], i + 1)
            dve.wait_ge(S["tails_done"], 2 + NQKV + i)
            TT(acc[:, 0, 2:2 + TP], xp[:, 0, 0:TP], xp[:, 1, 0:TP], ALU.mult)
            TT(acc[:, 0, 4 + TP:4 + T], xp[:, 0, TP:T], xp[:, 1, TP:T], ALU.mult).then_inc(S["prod_done"], 1)
            lo_split(n0 + 3, 3)
            dve.wait_ge(S["prod_done"], i + 1)
            ch.link(TS_(acc[:, 1, 0:WM], acc[:, 0, 0:WM], caw[:, 0, ds(i, 1)], None, ALU.mult))
            ch.link(STT(acc[:, 1, 0:WM], acc[:, 0, 1:1 + WM], caw[:, 1, ds(i, 1)], acc[:, 1, 0:WM], ALU.mult, ALU.add))
            step_add(i, 3)
            STT(acc[:, 1, 0:WM], acc[:, 0, 2:2 + WM], caw[:, 2, ds(i, 1)], acc[:, 1, 0:WM], ALU.mult, ALU.add)\
                .then_inc(S["prod_free"], 1)
            step_add(i, 4)
            step_add(i, 5)
            dve.wait_ge(S["bank_free"], n0 + 2 + 3)
            dve.wait_ge(S["prod_free"], i + 2)
            TT(U[:, i, 0:TP], acc[:, 1, 0:TP], xp[:, 0, 0:TP], ALU.mult)
            TT(U[:, i, TP:T], acc[:, 1, TP + 2:T + 2], xp[:, 0, TP:T], ALU.mult).then_inc(S["u_done"], 1)
            lo_split(n0 + 4, 0)
            state(i)
            lo_split(n0 + 5, 1)
            ch.end(KT)

        chunk_decay(KT)
        lo_split(N_TAIL + 2, 2)
        chunk_tokens(KT)
        step_add(KT, 1)
        dve.wait_ge(S["s_in"], 16)
        rhs(KT)
        step_add(KT, 2)
        lo_split(N_TAIL + 3, 3)
        for l in (3, 4, 5):
            step_add(KT, l)
        lo_split(N_TAIL + 4, 0)
        state(KT)
        lo_split(N_TAIL + 5, 1)
        V_.memset(B2, 0.0).then_inc(S["ada_row_sb"], 1)
        with dve.Fori(1, KT // 2 - 1) as i:
            for j in range(4):
                lo_split(N_TAIL + 4 * i + j + 2, (j + 2) % 4)
        for j in range(4):
            lo_split(N_WA - 4 + j + 2, (j + 2) % 4)
            if j == 2:
                columns(1, B3, "ada_b", 16).then_inc(S["mod_done"], 1)
        for t in range(KT):
            dve.wait_ge(S["u_hi"], t + 1)
            TT(a_lo[:, t, :], U[:, t, :], a_hi[:, t, :].bitcast(F32), ALU.subtract).then_inc(S["u_split"], 1)

        og_g = vec("out_g")
        with dve.Fori(0, 2) as i:
            ch.loop(i, 4)
            for j in range(4):
                t, b = 4 * i + j, j % 2
                n = N_WA + t
                dve.wait_ge(S["bank_free"], n + 1 + 2)
                STT(xT[:, t, :], xT[:, t, :], 1.0, xp[:, b, 0:T], ALU.add, ALU.mult).then_inc(S["tmp_free"], 1)
                lo_split(n + 2, (j + 2) % 4)
                if j % 2 == 0:
                    dve.wait_ge(S["rs_done"], 2 * i + j // 2 + 2)
                    dve.wait_ge(S["og_split"], t + 1)
                    for e in range(2):
                        ch.note(TT(og[e][:, :], Q[:, t + e, :], rs[:, e, :], ALU.mult))
                    ch.wait()
                    for e in range(2):
                        STT(og[e][:, :], og[e][:, :], og_g, V[:, t + e, :], ALU.mult, ALU.mult)\
                            .then_inc(S["og_done"], 1)
                else:
                    for e in range(2):
                        dve.wait_ge(S["og_hi"], t + e)
                        TT(b_lo[:, t - 1 + e, :], og[e][:, :], b_hi[:, t - 1 + e, :].bitcast(F32), ALU.subtract)\
                            .then_inc(S["og_split"], 1)
            ch.end(2)

        dve.wait_ge(S["oss_ready"], HP)
        dve.wait_ge(S["rs_done"], HP + 1)
        V_.memset(B2, 0.0).then_inc(S["ada_row_sb"], 1)
        with dve.Fori(0, 2) as i:
            for j in range(4):
                t, b = 4 * i + j, j % 2
                n = N_WB + t
                dve.wait_ge(S["bank_free"], n + 1 + 2)
                ins = STT(acc[:, b, 0:T], K[:, t, :], 1.0, xp[:, b, 0:T], ALU.add, ALU.mult)
                ins.then_inc(S["tmp_free"], 1)
                dve.wait_ge(S["tmp_free"], 2 + KT + t + 1)
                TT(acc[:, b, 0:T], acc[:, b, 0:T], xT[:, t, :], ALU.add).then_inc(S["y_done"], 1)
                lo_split(n + 2, (j + 2) % 4)
                dve.wait_ge(S["y_hi"], t + 1)
                TT(a_lo[:, t, :], acc[:, b, 0:T], a_hi[:, t, :].bitcast(F32), ALU.subtract).then_inc(S["y_split"], 1)
        dve.wait_ge(S["mod_done"], 2)
        dve.wait_ge(S["x_back_in"], 16)

        def add_square(t, m):
            if t:
                dve.wait_ge(S["squared"], KT * m + t + 1)
                ins = TT(acc[:, 0, 0:T], acc[:, 0, 0:T], acc[:, 1, 0:T], ALU.add)
                ins.then_inc(S["added"], 1)
                if t == KT - 1:
                    dve.wait_ge(S["added"], (m + 1) * (KT - 1))
                    V_.memset(bias[:, 6:7], 0.0).then_inc(S["sq2_done"], 1)
                else:
                    dve.wait_ge(S["added"], m * (KT - 1) + t)

        for t in range(KT):
            n, b = N_WO + t, t % 2
            dve.wait_ge(S["bank_free"], n + 1 + 2)
            for g, c in GR:
                last = STT(xT[:, t, c], xp[:, b, c], mod[:, 1, t, g:g + 1], x_back[:, t, c], ALU.mult, ALU.add)
            last.then_inc(S["tmp_free"], 1)
            lo_split(n + 2, (n + 2) % 4)
            add_square(t, 0)
            if t == 2:
                ch.link(columns(2, B3, "ada_b", 32))
                scale_of(1, 2, 0, "norm2_g").then_inc(S["mod_done"], 1)
                dve.wait_ge(S["mod_done"], 3)
                V_.memset(B2, 0.0).then_inc(S["ada_row_sb"], 1)
        dve.wait_ge(S["rstd_done"], 2)
        dve.wait_ge(S["tmp_free"], 2 + 3 * KT)
        norm(rstd2, 1)

        def ff1(q, n0):
            with dve.Fori(0, 2) as i:
                for j in range(4):
                    n, b, t = n0 + 4 * i + j, j % 2, 4 * i + j
                    dve.wait_ge(S["bank_free"], n + 1 + 2)
                    STT(acc[:, b, 0:T], xp[:, b, 0:T], 0.0, xp[:, b, 0:T], ALU.max, ALU.mult).then_inc(S["tmp_free"], 1)
                    lo_split(n + 2, (j + 2) % 4)
                    dve.wait_ge(S["f_hi_done"], KT * q + t + 1)
                    TT(f_lo[q % 2][:, t, :], acc[:, b, 0:T], f_hi[q % 2][:, t, :].bitcast(F32), ALU.subtract)\
                        .then_inc(S["f_split"], 1)

        def add_residual(t, b):
            for g, c in GR:
                last = STT(xT[:, t, c], xp[:, b, c], mod_c(t, g), xT[:, t, c], ALU.mult, ALU.add)
            return last

        def mod_c(t, g):
            return mod[:, 2, ds(t + KT, 1), g] if not isinstance(t, int) else mod[:, 2, t + KT:t + KT + 1, g]

        def ff2(q, n0):
            with dve.Fori(0, 2) as i:
                for j in range(4):
                    n, b, t = n0 + 4 * i + j, j % 2, 4 * i + j
                    dve.wait_ge(S["bank_free"], n + 1 + 2)
                    add_residual(t, b).then_inc(S["tmp_free"], 1)
                    lo_split(n + 2, (j + 2) % 4)

        ff1(0, N_FF)
        for q in range(3):
            ff1(q + 1, N_FF + 8 + 16 * q)
            if q == 0:
                ch.link(columns(3, B3, "final_b", 0))
                scale_of(2, 3, KT, "final_g").then_inc(S["mod_done"], 1)
            ff2(q, N_FF + 16 + 16 * q)
        for t in range(KT):
            n, b = N_ALL - KT + t, t % 2
            dve.wait_ge(S["bank_free"], n + 1 + 2)
            add_residual(t, b).then_inc(S["tmp_free"], 1)
            if n + 2 < N_ALL:
                lo_split(n + 2, (n + 2) % 4)
            add_square(t, 1)
        dve.wait_ge(S["rstd_done"], 3)
        dve.wait_ge(S["tmp_free"], 2 + 11 * KT)
        for f in range(KT):
            t = xp[:, f % 2, 0:T]
            if f >= 2:
                dve.wait_ge(S["yo_done"], f - 1)
            ch.link(TT(t, xT[:, f, :], rstd2[:, :], ALU.mult))
            for g, c in GR:
                last = TS_(y_fm[:, f, c], xp[:, f % 2, c], scales[:, 2, f, g:g + 1], mod[:, 3, f, g:g + 1],
                           ALU.mult, ALU.add)
            last.then_inc(S["yo_done"], 1)

    block.__exit__(None, None, None)


_INS = ["x_prompt", "x_sample", "cache_conv_a", "cache_conv_qkv", "state_delta", "c_prompt", "c_sample", "ada_w",
        "ada_b", "norm1_g", "norm2_g", "w_in", "conv_a_w", "conv_qkv_w", "a_log", "dt_bias", "out_norm_g",
        "w_a_out", "w_b_out", "w_o", "w_ff1", "w_ff2", "final_ada_w", "final_ada_b", "final_norm_g"]
_OUTS = [("y_p", (1, TP, D)), ("y_s", (1, TS, D)),
         ("ca_p", (1, 1, WA - 1, D)), ("cq_p", (1, 1, WB - 1, 3 * D)), ("s_p", (1, 1, H, P, P)),
         ("ca_s", (1, 1, WA - 1, D)), ("cq_s", (1, 1, WB - 1, 3 * D)), ("s_s", (1, 1, H, P, P))]


def kernel(**inputs):
    import numpy as _np
    import concourse.bacc as _bacc
    from concourse import mybir as _mybir
    from concourse.bass_utils import run_bass_kernel_spmd as _run

    nc = _bacc.Bacc("TRN2", target_bir_lowering=False, num_devices=1)
    arrays, t_in, t_out = {}, {}, {}
    for name in _INS:
        a = _np.ascontiguousarray(inputs[name])
        arrays[f"in_{name}"] = a
        t_in[name] = nc.dram_tensor(f"in_{name}", a.shape, _mybir.dt.from_np(a.dtype), kind="ExternalInput").ap()
    for name, shape in _OUTS:
        t_out[name] = nc.dram_tensor(f"out_{name}", shape, _mybir.dt.float32, kind="ExternalOutput").ap()
    build(nc, t_in, t_out)
    r = _run(nc, [arrays], core_ids=[0])
    return tuple(r.results[0][f"out_{name}"] for name, _ in _OUTS)
```

```python
import concourse.bass as bass
from concourse import mybir
from concourse.bass import ds

F32 = mybir.dt.float32
F32R = mybir.dt.float32r
ALU = mybir.AluOpType
ACT = mybir.ActivationFunctionType

P = 128
D = 1024
KT = D // P
TP, TS = 512, 64
T = TP + TS
HALF = T // 2
CH = 64
NCH = T // CH
H = 8
HP = H // 2
WA, WB = 3, 4
LEVELS = 6
NEXP = LEVELS - 1
EPS = 1e-6
NQKV = 24
DFF = 4096

C_PB, C_PC, C_PH, C_QKV, C_Z, C_AB, C_GA, C_GB = 0, 1024, 2048, 3072, 6144, 7168, 7184, 8208

N_QKV, N_MIX, N_TAIL, N_WA, N_WB, N_WO, N_FF = 0, 24, 56, 72, 80, 88, 96
N_ALL = 160
RAW, SLOT = 4, 2

VEC = {}
_at = 0
for _name, _n in (("conv_qkv_w", WB * NQKV), ("conv_a_w", WA * KT), ("norm1_g", KT),
                  ("cache_qkv", (WB - 1) * NQKV), ("cache_a", (WA - 1) * KT), ("norm2_g", KT), ("final_g", KT),
                  ("out_g", 1), ("c_p", KT), ("c_s", KT), ("pad", 7),
                  ("ada_b", 6 * KT), ("final_b", 2 * KT)):
    VEC[_name] = (_at, _n)
    _at += _n
NVEC = _at


class Chain:

    def __init__(self, eng, sem):
        self.eng, self.sem, self.n, self.base = eng, sem, 0, 0

    def link(self, ins):
        ins.then_inc(self.sem, 1)
        self.n += 1
        self.wait()

    def wait(self):
        self.eng.wait_ge(self.sem, self.base + self.n)

    def note(self, ins):
        ins.then_inc(self.sem, 1)
        self.n += 1

    def loop(self, i, per):
        self.base, self.start, self.per = self.base + self.n + i * per, self.base + self.n, per
        self.n = 0

    def end(self, passes):
        assert self.n == self.per, (self.n, self.per)
        self.base, self.n = self.start + passes * self.per, 0


def whole(eng, value):
    return value if isinstance(value, int) else eng.compute_val(value)


def build(nc, t_in, t_out):
    SB0 = -(-nc.sbuf_base // 32) * 32
    cur = [SB0]

    def sb(name, shape, dt=F32, at=None):
        size = 4
        for s in shape[1:]:
            size *= s
        size = -(-size // 32) * 32
        if at is None:
            at = cur[0]
            cur[0] += size
        return nc.alloc_sbuf_tensor_at(name, shape, dt, offset=at)

    def region(size):
        at = cur[0]
        cur[0] += -(-size // 32) * 32
        return at

    TILE8 = KT * T * 4

    r_x = region(TILE8)
    xT = sb("xT", [P, KT, T], at=r_x)
    a_hi = sb("a_hi", [P, KT, T], F32R)
    a_lo = sb("a_lo", [P, KT, T], F32R)
    w_raw = sb("w_raw", [P, RAW, KT, P])
    w_hi = sb("w_hi", [P, SLOT, KT, P], F32R)
    w_lo = sb("w_lo", [P, SLOT, KT, P], F32R)
    r_q, r_k, r_v, r_u = region(TILE8), region(TILE8), region(TILE8), region(TILE8)
    qkv = sb("qkv", [P, NQKV, T], at=r_q)
    Q, K, V = qkv[:, 0:8, :], qkv[:, 8:16, :], qkv[:, 16:24, :]
    U = sb("U", [P, KT, T], at=r_u)
    b_hi = sb("b_hi", [P, KT, T], F32R, at=r_u)
    b_lo = sb("b_lo", [P, KT, T], F32R, at=r_v)
    f_hi = [sb("f0_hi", [P, KT, T], F32R, at=r_q), sb("f1_hi", [P, KT, T], F32R, at=r_v)]
    f_lo = [sb("f0_lo", [P, KT, T], F32R, at=r_k), sb("f1_lo", [P, KT, T], F32R, at=r_u)]
    ada0_w = sb("ada0_w", [P, KT, 2 * D], at=r_q)
    x_back = sb("x_back", [P, KT, T], at=r_q)
    y_fm = sb("y_fm", [P, KT, T], at=r_q)
    y_tok = sb("y_tok", [P, 5, D], at=r_k)

    ident = sb("ident", [P, P])
    ones = sb("ones", [P, P])
    id64 = sb("id64", [P, CH])
    neg = sb("neg", [P, CH])
    lvl = sb("lvl", [P, LEVELS, CH])
    vecs = sb("vecs", [P, NVEC])
    mod = sb("mod", [P, 4, 16, 2])
    scales = sb("scales", [P, 3, KT, 2])
    rows = sb("rows", [P, T])
    r_rows = cur[0] - T * 4
    c_act = sb("c_act", [P, KT, 2])
    mrow_l = sb("mrow_l", [P, 512], at=r_rows)
    tokv = sb("tokv", [P, NCH, 12])
    tails = sb("tails", [P, 2, (WB - 1) * NQKV + (WA - 1) * KT])
    bias = sb("bias", [P, 8])
    o_ss = sb("o_ss", [P, 8])
    r_xp = region(2 * 584 * 4)
    xp = sb("xp", [P, 2, 584], at=r_xp)
    r_acc = region(2 * 584 * 4)
    acc = sb("acc", [P, 2, 584], at=r_acc)
    r_ds = cur[0]
    x_tok = sb("x_tok", [P, 5, D], at=r_ds)
    ab_raw = sb("ab_raw", [P, KT, CH], at=r_ds + 20480)
    ab_hi = sb("ab_hi", [P, KT, CH], F32R, at=r_ds + 22528)
    ab_lo = sb("ab_lo", [P, KT, CH], F32R, at=r_ds + 24576)
    vrows = sb("vrows", [P, 3, P], at=r_ds + 26624)
    mrow = sb("mrow", [P, 512], at=r_ds + 28160)
    rstd1 = sb("rstd1", [P, T], at=r_ds + 30208)
    ab_sb, ab_e, ab_sp, row_g, row_e, row_b, cmask = (sb(f"row{i}", [P, T], at=r_ds + i * T * 4) for i in range(7))
    sq = sb("sq", [P, 2, H, CH], at=r_ds)
    kq = sb("kq", [P, 2, H, CH], at=r_ds + 4096)
    vn = sb("vn", [P, HP, P], at=r_ds + 4096)
    vc = sb("vc", [P, H, CH], at=r_ds + 8192)
    qd = sb("qd", [P, H, CH], at=r_ds + 8192)
    decs = sb("decs", [P, 2, HP, CH], at=r_ds + 10240)
    dec, decb = decs[:, 0], decs[:, 1]
    p1 = sb("p1", [P, HP, CH], at=r_ds + 11264)
    at_ = sb("at", [P, HP, CH], at=r_ds + 12288)
    qkt = sb("qkt", [P, HP, CH], at=r_ds + 13312)
    nb = sb("nb", [P, 3, HP, CH], at=r_ds + 14336)
    mm = sb("mm", [P, 2, HP, CH], at=r_ds + 17408)
    egs = sb("egs", [P, 2, H, CH], at=r_ds + 19456)
    eg, kbe = egs[:, 0], egs[:, 1]
    kdt = sb("kdt", [P, HP, P], at=r_ds + 23552)
    vb = sb("vb", [P, HP, P], at=r_ds + 25600)
    o_tok = sb("o_tok", [P, HP, P], at=r_ds + 25600)
    o_sq = sb("o_sq", [P, P], at=r_ds + 12288)
    st = sb("st", [P, H, P], at=r_ds + 27648)
    AS = 3
    ada_w = sb("ada_w", [P, AS, 2 * D], at=r_ds)
    og = [sb("og_0", [P, T], at=r_rows), sb("og_1", [P, T], at=r_ds + 29184)]
    rstd2 = sb("rstd2", [P, T], at=r_ds + 24576)
    tail_rows = [sb(f"tail_rows{g}", [P, P], at=r_ds + 29184 + 512 * g) for g in range(2)]
    assert r_ds + 32512 <= nc.sbuf_usable_end, (r_ds + 32512, nc.sbuf_usable_end)

    norm_buf = [xp[:, 0, 0:T], xp[:, 1, 0:T], acc[:, 0, 0:T], acc[:, 1, 0:T]]
    gp = nc.alloc_psum_tensor("gp", [P, 4, 512], F32)
    dp = nc.alloc_psum_tensor("dp", [P, 4, 512], F32)
    B0, B1, B2, B3 = (dp[:, i, :] for i in range(4))

    x_spill = nc.dram_tensor("x_spill", [P, KT, T], F32, kind="Internal").ap()

    gate_e = nc.dram_tensor("gate_e", [NCH, 2, H, CH], F32, kind="Internal").ap()
    gate_g = nc.dram_tensor("gate_g", [NCH, 2, 2, HP, CH], F32, kind="Internal").ap()

    S = {}
    for group in (
            "rows_in x_in ab_in spilled x_back_in gates_spilled decs_in egs_in s_in s_out caches_out "
            "out_done consts zeros_ready pool_ready",
            "dve_own act_own pool_own",
            "vecs_t vecs_done xt_ready xt_done sq_done ss_all rstd_done t_done hi_split h_ready c_act "
            "ada0_used ada_row_sb ada_t mod_done ada_used ab_hi_done ab_split ab_ready row_a row_v ab_rows "
            "tok_t tok_done",
            "w_hi_done w_lo_done tile_done bank_free",
            "pads_done tails_done acc_free conv_done prod_done u_done prod_free pads_a u_hi u_split",
            "o_free s_done sq_ready ss_ready rkq_done kq_done vc_done dd_done dec_done decb_done kbe_done "
            "tr_ready kkqk_ready at_done tokmul_done nb_done mt_done m0_ready m0_done p1_ready p1_done "
            "x_ready m_done ks_ready rhs_done vn_ready vn_done qd_done o_ready o_rstd o_normed o_turned "
            "ds_ready",
            "tmp_free og_done og_hi og_split y_done y_hi y_split squared added f_hi_done f_split",
            "y_norm yo_done yo_done_v yt_ready yt_done yt_done_v tail_t tail_sb",
    ):
        for name in group.split():
            S[name] = nc.alloc_semaphore(name)
    raw_full = [nc.alloc_semaphore(f"w_raw_full{i}") for i in range(RAW)]
    ada_full = [nc.alloc_semaphore(f"ada_full{i}") for i in range(8)]
    late_full = [nc.alloc_semaphore(f"late_full{i}") for i in range(AS)]

    A = t_in
    w_in, w_a, w_b, w_o = A["w_in"][0], A["w_a_out"][0], A["w_b_out"][0], A["w_o"][0]
    w_ff1, w_ff2 = A["w_ff1"][0], A["w_ff2"][0]

    def wt(w, col, row=0):
        rows = slice(row, row + KT) if isinstance(row, int) else ds(row, KT)
        return w.rearrange("(k p) n -> p k n", p=P)[:, rows, ds(col, P)]

    ada_v = A["ada_w"][0].rearrange("(k p) n -> p k n", p=P)
    fin_v = A["final_ada_w"].rearrange("(k p) n -> p k n", p=P)

    def vec(name, j=0):
        return vecs[:, VEC[name][0] + j:VEC[name][0] + j + 1]

    Y_ACT = 5
    OUT = (slice(0, 256), slice(256, TP), slice(TP, T))

    block = nc.Block()
    block.__enter__()

    @block.sync
    def _(sp):
        sp.dma_start(x_tok[:, 0:4, :], A["x_prompt"][0].rearrange("(t p) d -> p t d", p=P)).then_inc(S["x_in"], 16)
        sp.dma_start(x_tok[0:TS, 4, :], A["x_sample"][0]).then_inc(S["x_in"], 16)
        def row(name, src):
            at, n = VEC[name]
            sp.dma_start(vrows[at % P:at % P + n, at // P, :], src).then_inc(S["rows_in"], 16)

        row("c_p", A["c_prompt"].rearrange("b (n p) -> (b n) p", p=P))
        row("c_s", A["c_sample"].rearrange("b (n p) -> (b n) p", p=P))
        row("conv_qkv_w", A["conv_qkv_w"][0].rearrange("j (n p) -> (j n) p", p=P))
        row("conv_a_w", A["conv_a_w"][0].rearrange("j (n p) -> (j n) p", p=P))
        row("norm1_g", A["norm1_g"].rearrange("l (n p) -> (l n) p", p=P))
        row("cache_qkv", A["cache_conv_qkv"][0, 0].rearrange("j (n p) -> (j n) p", p=P))
        row("cache_a", A["cache_conv_a"][0, 0].rearrange("j (n p) -> (j n) p", p=P))
        row("norm2_g", A["norm2_g"].rearrange("l (n p) -> (l n) p", p=P))
        row("final_g", A["final_norm_g"].rearrange("(n p) -> n p", p=P))
        row("out_g", A["out_norm_g"])
        row("pad", A["norm2_g"].rearrange("l (n p) -> (l n) p", p=P)[0:7])
        row("ada_b", A["ada_b"].rearrange("l (n p) -> (l n) p", p=P))
        row("final_b", A["final_ada_b"].rearrange("(n p) -> n p", p=P))
        sp.wait_ge(S["zeros_ready"], 1)
        v = w_in.rearrange("(k p) n -> p k n", p=P)
        with nc.allow_non_contiguous_dma(reason="16 columns"):
            sp.dma_start(ab_raw[:, :, 0:8], v[:, :, C_AB:C_AB + 8]).then_inc(S["ab_in"], 16)
            sp.dma_start(ab_raw[:, :, 32:40], v[:, :, C_AB + 8:C_AB + 16]).then_inc(S["ab_in"], 16)
            sp.dma_start(bias[0:H, 0:1], A["dt_bias"].rearrange("l h -> h l")).then_inc(S["ab_in"], 16)
            sp.dma_start(bias[0:H, 1:2], A["a_log"].rearrange("l h -> h l")).then_inc(S["ab_in"], 16)

        def load(n, group, j, src):
            if not (isinstance(group, int) and group == 0):
                value = whole(sp, n - 3)
                sp.wait_ge(S["zeros_ready"], 1)
                sp.wait_ge(S["w_lo_done"], value)
            sp.dma_start(w_raw[:, j, :, :], src).then_inc(raw_full[j], 16)

        for k in range(KT):
            sp.dma_start(ada0_w[:, k, :], ada_v[:, k, 0:2 * D]).then_inc(ada_full[k], 16)
        for j in range(4):
            load(j, 0, j, wt(w_in, C_QKV + j * P))
        sp.wait_ge(S["xt_done"], KT)
        sp.dma_start(x_spill, xT[:, :, :]).then_inc(S["spilled"], 16)
        with sp.Fori(1, NQKV // 4) as i:
            for j in range(4):
                load(4 * i + j, i, j, wt(w_in, C_QKV + j * P + i * (4 * P)))
        sp.wait_ge(S["ab_rows"], 1)
        sp.wait_ge(S["row_a"], 3)
        for e in range(2):
            for q in range(2):
                sp.dma_start(gate_g[:, e, q].rearrange("c m i -> m c i"),
                             rows[32 * q + e:32 * q + H:2, :].rearrange("p (c i) -> p c i", c=NCH))\
                    .then_inc(S["gates_spilled"], 16)
        for q, src in enumerate((row_e[0:H, :], rows[96:96 + H, :])):
            sp.dma_start(gate_e[:, q].rearrange("c h i -> h c i"), src.rearrange("p (c i) -> p c i", c=NCH))\
                .then_inc(S["gates_spilled"], 16)
        sp.wait_ge(S["gates_spilled"], 96)

        def gates(c, first=False):
            if not first:
                value = whole(sp, c * NEXP)
                sp.wait_ge(S["zeros_ready"], 1)
                sp.wait_ge(S["m_done"], value)
            for e in range(2):
                src = gate_g[ds(c, 1), e].rearrange("o q m i -> o (q m i)").to_broadcast([CH, 2 * HP * CH])
                sp.dma_start(decs[64 * e:64 * e + 64, :, :, :].rearrange("p q m i -> p (q m i)"), src)\
                    .then_inc(S["decs_in"], 16)
            value = whole(sp, c + 1)
            sp.wait_ge(S["zeros_ready"], 1)
            sp.wait_ge(S["s_done"], value)
            src = gate_e[ds(c, 1)].rearrange("o q h i -> o (q h i)").to_broadcast([P, 2 * H * CH])
            sp.dma_start(egs[:, :, :, :].rearrange("p q h i -> p (q h i)"), src).then_inc(S["egs_in"], 16)

        def mix_loads(i):
            for j, c in enumerate((C_PC, C_PH, C_PB, C_GA)):
                load(N_MIX + 4 * i + j, i + 6, j, wt(w_in, c + i * P))

        mix_loads(0)
        gates(0, True)
        with sp.Fori(1, KT) as i:
            mix_loads(i)
            gates(i)
        for j, c in enumerate((C_Z, C_GB, C_Z + P, C_GB + P)):
            load(N_TAIL + j, N_TAIL // 4, j, wt(w_in, c))
        gates(KT)
        with sp.Fori(1, KT // 2) as i:
            for j, c in enumerate((C_Z, C_GB, C_Z + P, C_GB + P)):
                load(N_TAIL + 4 * i + j, i + 14, j, wt(w_in, c + i * (2 * P)))

        def group8(n0, w, col=0, row=0):
            with sp.Fori(0, 2) as i:
                for j in range(4):
                    load(n0 + 4 * i + j, i + n0 // 4, j, wt(w, col + j * P + i * (4 * P), row))

        group8(N_WA, w_a)
        group8(N_WB, w_b)
        sp.wait_ge(S["spilled"], 16)
        sp.wait_ge(S["og_split"], 1 + KT)
        sp.dma_start(x_back[:, :, :], x_spill).then_inc(S["x_back_in"], 16)
        group8(N_WO, w_o)
        group8(N_FF, w_ff1)
        for q in range(3):
            group8(N_FF + 8 + 16 * q, w_ff1, (q + 1) * D)
            group8(N_FF + 16 + 16 * q, w_ff2, 0, q * KT)
        group8(N_ALL - 8, w_ff2, 0, 3 * KT)
        for t in range(5):
            sp.wait_ge(S[("yt_done", "yt_done_v")[t % 2]], t // 2 + 1)
            dst = t_out["y_p"][0][t * P:(t + 1) * P, :] if t < 4 else t_out["y_s"][0]
            sp.dma_start(dst, y_tok[0:P if t < 4 else TS, t, :]).then_inc(S["out_done"], 16)
        sp.wait_ge(S["out_done"], 80)
        sp.wait_ge(S["caches_out"], 64)
        sp.wait_ge(S["s_out"], 32)

    @block.gpsimd
    def _(pool):
        ch = Chain(pool, S["pool_own"])
        ch.note(pool.memset(ones[:, :], 1.0))
        ch.note(pool.memset(ident[:, :], 0.0))
        ch.note(pool.memset(id64[:, :], 0.0))
        ch.note(pool.memset(neg[:, :], 0.0))
        ch.note(pool.memset(lvl[:, :, :], 0.0))
        ch.note(pool.memset(rows[:, :], 0.0))
        ch.note(pool.memset(bias[:, :], 0.0))
        ch.link(pool.memset(ab_raw[:, :, :], 0.0))
        ch.link(pool.affine_select(out=ident[:, :], in_=ident[:, :], compare_op=ALU.not_equal, fill=1.0, base=0,
                                   pattern=[[-1, P]], channel_multiplier=1))
        pool.memset(bias[:, 2:3], EPS).then_inc(S["consts"], 1)
        pool.memset(bias[:, 3:4], -0.5 * 4.852030263919617).then_inc(S["consts"], 1)
        pool.memset(acc[:, 1, 576:584], 0.0).then_inc(S["zeros_ready"], 1)
        pool.memset(acc[:, 0, 0:1], 0.0).then_inc(S["acc_free"], 2)
        pool.memset(acc[:, 0, 1:2], 0.0).then_inc(S["tails_done"], 2)
        pool.memset(acc[:, 0, 2:3], 0.0).then_inc(S["o_free"], 1)
        pool.memset(acc[:, 0, 3:4], 0.0).then_inc(S["tmp_free"], 2)
        pool.memset(acc[:, 0, 4:5], 0.0).then_inc(S["og_split"], 1)
        pool.memset(acc[:, 0, 5:6], 0.0).then_inc(S["prod_free"], 1)
        pool.memset(acc[:, 0, 7:8], 0.0).then_inc(S["bank_free"], 2)
        pool.wait_ge(S["bank_free"], 2)
        for p in range(2):
            b, base = slice(64 * p, 64 * p + 64), 0
            ch.link(pool.affine_select(out=id64[b, :], in_=id64[b, :], compare_op=ALU.not_equal, fill=1.0,
                                       base=base, pattern=[[-1, CH]], channel_multiplier=1))
            ch.link(pool.affine_select(out=neg[b, :], in_=neg[b, :], compare_op=ALU.is_ge, fill=-1e30,
                                       base=base, pattern=[[1, CH]], channel_multiplier=-1))
        for l in range(LEVELS):
            s = 1 << l
            v = lvl[:, l, :].rearrange("p (g r) -> p g r", r=2 * s)
            ch.link(pool.memset(v[:, :, s:2 * s], -1.0))
            for p in range(2):
                b = slice(64 * p, 64 * p + 64)
                w = v[b, :, s:2 * s]
                ch.link(pool.affine_select(out=w, in_=w, compare_op=ALU.is_ge, fill=0.0, base=0,
                                           pattern=[[-2 * s, CH // (2 * s)], [0, s]], channel_multiplier=1))
                ch.link(pool.affine_select(out=w, in_=w, compare_op=ALU.is_ge, fill=0.0, base=s - 1,
                                           pattern=[[2 * s, CH // (2 * s)], [0, s]], channel_multiplier=-1))
        pool.memset(acc[:, 0, 6:7], 0.0).then_inc(S["pool_ready"], 1)

        c0, t0 = VEC["cache_qkv"][0], (WB - 1) * NQKV
        cache_v = vecs[:, c0:c0 + t0].rearrange("p (j n) -> p n j", j=WB - 1)
        tails_v = tails[:, :, 0:t0].rearrange("p g (j n) -> p g n j", j=WB - 1)
        pool.wait_ge(S["vecs_done"], 1)
        pool.wait_ge(S["h_ready"], KT)
        def conv_edges(i):
            for b in range(2):
                n = 2 * i + b
                pool.wait_ge(S["acc_free"], n + 1)
                pool.tensor_copy(xp[:, b, 515:518], cache_v[:, n, :]).then_inc(S["pads_done"], 1)
                pool.wait_ge(S["bank_free"], n + 1 + 2)
                pool.tensor_copy(tails_v[:, 0, n, :], xp[:, b, 512:515])
                pool.tensor_copy(tails_v[:, 1, n, :], xp[:, b, 579:582]).then_inc(S["tails_done"], 1)

        def chunk_squares(c):
            cols = ds(c * CH, CH) if not isinstance(c, int) else slice(c * CH, c * CH + CH)
            pool.tensor_tensor(sq[:, 0], K[:, :, cols], K[:, :, cols], ALU.mult).then_inc(S["sq_ready"], 1)
            pool.tensor_tensor(sq[:, 1], Q[:, :, cols], Q[:, :, cols], ALU.mult).then_inc(S["sq_ready"], 1)

        with pool.Fori(0, NQKV // 2 - 3) as i:
            conv_edges(i)
        pool.wait_ge(S["ab_rows"], 1)
        pool.wait_ge(S["row_a"], 3)
        pool.wait_ge(S["acc_free"], 2 * KT + 2)
        chunk_squares(0)
        with pool.Fori(NQKV // 2 - 3, NQKV // 2) as i:
            conv_edges(i)

        ca0, ta0 = VEC["cache_a"][0], (WA - 1) * KT
        cache_a = vecs[:, ca0:ca0 + ta0].rearrange("p (j n) -> p n j", j=WA - 1)
        tails_a = tails[:, :, t0:t0 + ta0].rearrange("p g (j n) -> p g n j", j=WA - 1)

        def pads(i):
            value = whole(pool, i + 1)
            pool.wait_ge(S["vecs_done"], 1)
            pool.wait_ge(S["prod_free"], value)
            pool.memset(acc[:, 0, 0:2], 0.0)
            pool.tensor_copy(acc[:, 0, 514:516], cache_a[:, i, :]).then_inc(S["pads_a"], 1)

        def tails_of(i):
            pool.wait_ge(S["prod_done"], i + 1)
            pool.tensor_copy(tails_a[:, 0, i, :], acc[:, 0, 512:514])
            pool.tensor_copy(tails_a[:, 1, i, :], acc[:, 0, 578:580]).then_inc(S["tails_done"], 1)

        def chunk_values(c):
            cols = ds(c * CH, CH) if not isinstance(c, int) else slice(c * CH, c * CH + CH)
            pool.wait_ge(S["o_free"], c + 1)
            pool.tensor_tensor(vc[:, :, :], V[:, :, cols],
                               ones[:, 0:CH].unsqueeze(1).to_broadcast([P, H, CH]), ALU.mult)\
                .then_inc(S["vc_done"], 1)

        def chunk_blocks(c):
            pool.wait_ge(S["at_done"], c + 1)
            for l in range(LEVELS):
                if l == 3:
                    pool.wait_ge(S["mt_done"], c + 1)
                elif l > 3:
                    pool.wait_ge(S["p1_ready"], c * NEXP + (l - 3))
                m = lvl[:, l, :].unsqueeze(1).to_broadcast([P, HP, CH])
                pool.tensor_tensor(nb[:, l % 3], at_[:, :, :], m, ALU.mult).then_inc(S["nb_done"], 1)

        pool.wait_ge(S["conv_done"], NQKV)
        pool.wait_ge(S["acc_free"], NQKV + 2)
        chunk_values(0)
        with pool.Fori(0, KT) as i:
            pads(i)
            chunk_blocks(i)
            pool.wait_ge(S["kq_done"], i + 1)
            chunk_squares(i + 1)
            tails_of(i)
            chunk_values(i + 1)
        pool.wait_ge(S["s_done"], KT + 1)
        pool.dma_start(t_out["s_p"][0, 0].rearrange("h k v -> k h v"), st[:, :, :]).then_inc(S["s_out"], 16)
        pool.wait_ge(S["s_out"], 16)
        pool.dma_start(st[:, :, :], A["state_delta"][0, 0].rearrange("h k v -> k h v")).then_inc(S["s_in"], 16)
        chunk_blocks(KT)
        pool.wait_ge(S["s_done"], NCH + 1)
        pool.dma_start(t_out["s_s"][0, 0].rearrange("h k v -> k h v"), st[:, :, :]).then_inc(S["s_out"], 16)
        def ada_load(m):
            if m >= AS:
                pool.wait_ge(S["ada_used"], m - AS + 1)
            r, k = 1 + m // KT, m % KT
            src = ada_v[:, k, 2 * D * r:2 * D * (r + 1)] if r < 3 else fin_v[:, k, :]
            pool.dma_start(ada_w[:, m % AS, :], src).then_inc(late_full[m % AS], 16)

        pool.wait_ge(S["o_free"], NCH + 1)
        for m in range(3 * KT):
            ada_load(m)
        pool.wait_ge(S["tail_sb"], 2)
        nb_, na_ = (WB - 1) * NQKV, (WA - 1) * KT
        for g, (cb, ca) in enumerate((("cq_p", "ca_p"), ("cq_s", "ca_s"))):
            pool.dma_start(t_out[cb][0, 0].rearrange("j (n p) -> (j n) p", p=P), tail_rows[g][0:nb_, :])\
                .then_inc(S["caches_out"], 16)
            pool.dma_start(t_out[ca][0, 0].rearrange("j (n p) -> (j n) p", p=P), tail_rows[g][nb_:nb_ + na_, :])\
                .then_inc(S["caches_out"], 16)

    @block.tensor
    def _(pe):
        T_ = nc.tensor

        def products(n, b, hi, lo, ready=None, start=0, k0=0, k1=KT):
            if k0 == 0:
                pe.wait_ge(S["w_lo_done"], n + 1)
                pe.wait_ge(S["bank_free"], n + 1)
            for k in range(k0, k1):
                if ready:
                    pe.wait_ge(S[ready], start + k + 1)
                for wp, ap in ((w_hi, hi), (w_hi, lo), (w_lo, hi)):
                    for h in range(2):
                        last = T_.matmul(gp[:, 2 * b + h, 0:HALF], wp[:, b, k, :],
                                         ap[:, k, h * HALF:(h + 1) * HALF],
                                         start=(k == 0 and wp is w_hi and ap is hi),
                                         stop=(k == KT - 1 and wp is w_lo))
            if k1 == KT:
                last.then_inc(S["tile_done"], 1)

        def two_products(n, hi, lo, ready, start, also=None):
            lag = 4
            for step in range(KT + lag):
                if step < KT:
                    pe.wait_ge(S[ready], start + step + 1)
                    if also:
                        also(step)
                for b, k in ((0, step), (1, step - lag)):
                    if not 0 <= k < KT:
                        continue
                    if k == 0:
                        pe.wait_ge(S["w_lo_done"], n + b + 1)
                        pe.wait_ge(S["bank_free"], n + b + 1)
                    for wp, ap in ((w_hi, hi), (w_hi, lo), (w_lo, hi)):
                        for h in range(2):
                            last = T_.matmul(gp[:, 2 * b + h, 0:HALF], wp[:, b, k, :],
                                             ap[:, k, h * HALF:(h + 1) * HALF],
                                             start=(k == 0 and wp is w_hi and ap is hi),
                                             stop=(k == KT - 1 and wp is w_lo))
                    if k == KT - 1:
                        last.then_inc(S["tile_done"], 1)

        def ada(r, bank, weights, wait):
            for k in range(KT):
                wait(k)
                for j in range(4):
                    last = T_.matmul(bank[32 * j:32 * j + 2, :], c_act[:, k, :],
                                     weights(k)[:, 512 * j:512 * j + 512], start=(k == 0), stop=(k == KT - 1))
                last.then_inc(S["ada0_used"], 1)

        pe.wait_ge(S["rows_in"], 16 * 13)
        pe.wait_ge(S["consts"], 1)
        for g in range(3):
            n = min(P, NVEC - g * P)
            last = T_.transpose(B0[:, g * P:g * P + n], vrows[0:n, g, :], ident[0:n, 0:n])
        last.then_inc(S["vecs_t"], 1)
        pe.wait_ge(S["x_in"], 32)
        pe.wait_ge(S["vecs_done"], 1)

        def sums(f, name, a, b, n=0):
            pe.wait_ge(S[name], n + f + 1)
            for h, bank in enumerate((a, b)):
                last = T_.matmul(bank[:, 0:HALF], ones[:, :], acc[:, f % 2, h * HALF:(h + 1) * HALF],
                                 start=(f == 0), stop=(f == KT - 1))
            last.then_inc(S["ss_all"], 1)

        for f in range(KT):
            b = f % 2
            if f >= 2:
                pe.wait_ge(S["xt_done"], f - 1)
            for t in range(4):
                T_.transpose(gp[:, 2 * b, t * P:(t + 1) * P], x_tok[:, t, f * P:(f + 1) * P], ident[:, :])
            T_.transpose(gp[:, 2 * b + 1, 0:TS], x_tok[0:TS, 4, f * P:(f + 1) * P], ident[0:TS, 0:TS])\
                .then_inc(S["xt_ready"], 1)
            if f >= 2:
                sums(f - 2, "sq_done", B0, B3)
        for f in (KT - 2, KT - 1):
            sums(f, "sq_done", B0, B3)
        pe.wait_ge(S["c_act"], 1)
        pe.wait_ge(S["ada_row_sb"], 1)
        ada(0, B1, lambda k: ada0_w[:, k, :], lambda k: pe.wait_ge(ada_full[k], 16))

        def ada_columns(bank, src, n):
            pe.wait_ge(S["ada_row_sb"], n)
            for s in range(4):
                last = T_.transpose(bank[:, s * P:(s + 1) * P], src[:, s * P:(s + 1) * P], ident[:, :])
            last.then_inc(S["ada_t"], 1)

        ada_columns(B2, mrow, 2)
        pe.wait_ge(S["ab_split"], 1)
        pe.wait_ge(S["mod_done"], 1)
        def gate_rows(k):
            for wp, ap in ((ab_hi, a_hi), (ab_hi, a_lo), (ab_lo, a_hi)):
                for h, bank in enumerate((B1, B2)):
                    last = T_.matmul(bank[0:CH, 0:HALF], wp[:, k, :], ap[:, k, h * HALF:(h + 1) * HALF],
                                     start=(k == 0 and wp is ab_hi and ap is a_hi),
                                     stop=(k == KT - 1 and wp is ab_lo))
            if k == KT - 1:
                last.then_inc(S["ab_ready"], 1)

        two_products(0, a_hi, a_lo, "h_ready", 0, gate_rows)
        for n in (2, 3):
            products(n, n % 2, a_hi, a_lo)
        with pe.Fori(1, NQKV // 4 - 1) as i:
            for j in range(4):
                products(4 * i + j, j % 2, a_hi, a_lo)

        def squares(c):
            pe.wait_ge(S["o_free"], c + 1)
            for g, bank in enumerate((B0, B1)):
                pe.wait_ge(S["sq_ready"], 2 * c + g + 1)
                last = T_.matmul(bank[:, :], ones[:, :], sq[:, g], start=True, stop=True)
            last.then_inc(S["ss_ready"], 1)

        for n in range(NQKV - 4, NQKV):
            products(n, n % 2, a_hi, a_lo)
            if n == NQKV - 4:
                squares(0)
                pe.wait_ge(S["ab_rows"], 1)
                pe.wait_ge(S["row_a"], 3)
                pe.wait_ge(S["pool_ready"], 1)
                for c in range(NCH):
                    for p in range(2):
                        sel = ident[:, :].rearrange("p (q r) -> p q r", q=4)[:, 0:3, p:H:2]
                        last = T_.matmul(B2[64 * p:64 * p + 64, 12 * c:12 * c + 12], rows[:, c * CH:(c + 1) * CH], sel,
                                         start=True, stop=True)
                last.then_inc(S["tok_t"], 1)
        pe.wait_ge(S["tok_done"], 1)


        heads = [(p, hp, 2 * hp + p, slice(64 * p, 64 * p + 64)) for hp in range(HP) for p in range(2)]

        def turn(c):
            pe.wait_ge(S["kq_done"], c + 1)
            pe.wait_ge(S["vc_done"], c + 1)
            for hp in range(HP):
                T_.transpose(B0[:, hp * P:(hp + 1) * P],
                             kq[:, 0, 2 * hp:2 * hp + 2, :].rearrange("p h i -> p (h i)"), ident[:, :])
            for hp in range(HP):
                last = T_.transpose(B1[:, hp * P:(hp + 1) * P],
                                    vc[:, 2 * hp:2 * hp + 2, :].rearrange("p h i -> p (h i)"), ident[:, :])
            last.then_inc(S["tr_ready"], 1)
            for p, hp, h, b in heads:
                last = T_.matmul(B2[b, hp * P:(hp + 1) * P], kq[:, 0, h, :], kq[:, :, h, :], start=True, stop=True)
            last.then_inc(S["kkqk_ready"], 1)

        def first_inverse(c):
            value = whole(pe, c + 1)
            pe.wait_ge(S["pool_ready"], 1)
            pe.wait_ge(S["mt_done"], value)
            for p, hp, h, b in heads:
                last = T_.matmul(B3[b, hp * CH:(hp + 1) * CH], mm[b, 1, hp, :], id64[b, :], start=True, stop=True)
            last.then_inc(S["m0_ready"], 1)

        def step_p(c, l):
            block_of = whole(pe, c * LEVELS + l + 1)
            sem, value = (S["m0_done"], c + 1) if l == 1 else (S["m_done"], c * NEXP + l - 1)
            value = whole(pe, value)
            pe.wait_ge(S["pool_ready"], 1)
            pe.wait_ge(S["nb_done"], block_of)
            pe.wait_ge(sem, value)
            for p, hp, h, b in heads:
                last = T_.matmul(B3[b, hp * CH:(hp + 1) * CH], nb[b, l % 3, hp, :], mm[b, 0, hp, :],
                                 start=True, stop=True)
            last.then_inc(S["p1_ready"], 1)

        def step_x(c, l):
            if l == 1:
                pe.wait_ge(S["at_done"], c + 1)
            value = whole(pe, c * NEXP + l)
            pe.wait_ge(S["pool_ready"], 1)
            pe.wait_ge(S["p1_done"], value)
            for p, hp, h, b in heads:
                if l < NEXP:
                    T_.matmul(B2[b, hp * CH:(hp + 1) * CH], mm[b, 1, hp, :], p1[b, hp, :], start=True, stop=True)
                last = T_.matmul(B2[b, (HP + hp) * CH:(HP + hp + 1) * CH], p1[b, hp, :], mm[b, 1, hp, :],
                                 start=True, stop=True)
            last.then_inc(S["x_ready"], 1)

        def s_product(c):
            value = whole(pe, c + 1)
            pe.wait_ge(S["pool_ready"], 1)
            pe.wait_ge(S["kbe_done"], value)
            pe.wait_ge(S["s_done"], value)
            pe.wait_ge(S["tokmul_done"], value)
            if isinstance(c, int):
                pe.wait_ge(S["s_in"], 16)
            for p, hp, h, b in heads:
                last = T_.matmul(B0[b, hp * P:(hp + 1) * P], kbe[:, h, :], st[:, h, :], start=True, stop=True)
            last.then_inc(S["ks_ready"], 1)

        def v_product(c):
            value, inverse = whole(pe, c + 1), whole(pe, (c + 1) * NEXP)
            pe.wait_ge(S["pool_ready"], 1)
            pe.wait_ge(S["m_done"], inverse)
            pe.wait_ge(S["rhs_done"], value)
            for p, hp, h, b in heads:
                last = T_.matmul(B3[b, hp * P:(hp + 1) * P], mm[b, 1, hp, :], vb[b, hp, :], start=True, stop=True)
            last.then_inc(S["vn_ready"], 1)

        def o_product(c):
            pe.wait_ge(S["vn_done"], c + 1)
            pe.wait_ge(S["qd_done"], c + 1)
            for p, hp, h, b in heads:
                T_.matmul(B0[b, hp * P:(hp + 1) * P], qd[:, h, :], st[:, h, :], start=True, stop=False)
                last = T_.matmul(B0[b, hp * P:(hp + 1) * P], qkt[b, hp, :], vn[b, hp, :], start=False, stop=True)
            last.then_inc(S["o_ready"], 1)

        def o_turn(c):
            pe.wait_ge(S["o_normed"], c + 1)
            for hp in range(HP):
                last = T_.transpose(B1[:, hp * P:(hp + 1) * P], o_tok[:, hp, :], ident[:, :])
            last.then_inc(S["o_turned"], 1)

        def s_change(c):
            for p, hp, h, b in heads:
                bank = (B2, B3)[p]
                last = T_.matmul(bank[:, hp * P:(hp + 1) * P], kdt[b, hp, :], vn[b, hp, :], start=True, stop=True)
            last.then_inc(S["ds_ready"], 1)

        def mixed(n0, c):
            def part(k0, k1):
                j = k0 // KT
                products(n0 + j, j % 2, a_hi, a_lo, k0=k0 % KT, k1=k1 - j * KT)

            sample = isinstance(c, int)
            part(0, 1)
            turn(c)
            part(1, 5)
            first_inverse(c)
            part(5, 6)
            step_p(c, 1)
            part(6, 7)
            step_x(c, 1)
            if not sample:
                s_product(c)
            part(7, 8)
            part(8, 9)
            step_p(c, 2)
            part(9, 10)
            step_x(c, 2)
            part(10, 12)
            step_p(c, 3)
            part(12, 13)
            step_x(c, 3)
            part(13, 15)
            step_p(c, 4)
            part(15, 16)
            step_x(c, 4)
            if sample:
                s_product(c)
            part(16, 18)
            step_p(c, 5)
            part(18, 19)
            step_x(c, 5)
            part(19, 21)
            v_product(c)
            part(21, 22)
            o_product(c)
            s_change(c)
            part(22, 24)
            o_turn(c)
            part(24, 26)
            if not sample:
                squares(c + 1)
            part(26, 32)

        with pe.Fori(0, KT) as i:
            mixed(N_MIX + 4 * i, i)
        mixed(N_TAIL, KT)

        def ada_late(r, k):
            m = KT * (r - 1) + k
            if k == 0:
                pe.wait_ge(S["ada_row_sb"], 2 * r + 1)
            pe.wait_ge(late_full[m % AS], 16 * (m // AS + 1))
            for j in range(4):
                last = T_.matmul(B2[32 * j:32 * j + 2, :], c_act[:, k, :], ada_w[:, m % AS, 512 * j:512 * j + 512],
                                 start=(k == 0), stop=(k == KT - 1))
            last.then_inc(S["ada_used"], 1)

        for n in range(N_TAIL + 4, N_WA):
            products(n, n % 2, a_hi, a_lo)
            if n < N_TAIL + 4 + KT:
                ada_late(1, n - N_TAIL - 4)
            elif n == N_WA - 2:
                ada_columns(B3, mrow_l, 4)

        def total(m):
            pe.wait_ge(S["added"], (m + 1) * (KT - 2))
            for b in range(2):
                if b:
                    pe.wait_ge(S["squared"], (m + 1) * KT)
                for h, bank in enumerate((B0, B1)):
                    last = T_.matmul(bank[:, 0:HALF], ones[:, :], acc[:, b, h * HALF:(h + 1) * HALF],
                                     start=(b == 0), stop=(b == 1))
            last.then_inc(S["ss_all"], 1)

        def group8(n0, hi, lo, ready=None, start=0):
            with pe.Fori(0, 2) as i:
                for j in range(4):
                    products(n0 + 4 * i + j, j % 2, hi, lo, ready, start)

        group8(N_WA, a_hi, a_lo, "u_split", 0)
        for k in range(KT):
            products(N_WB + k, k % 2, b_hi, b_lo, "og_split", 1)
            ada_late(2, k)
        for n in range(N_WO, N_WO + KT):
            products(n, n % 2, a_hi, a_lo, "y_split", 0)
            if n == N_WO + 1:
                ada_columns(B3, mrow_l, 6)
        total(0)
        two_products(N_FF, a_hi, a_lo, "h_ready", KT)
        ada_late(3, 0)
        ada_late(3, 1)
        for k in range(2, KT):
            products(N_FF + k, k % 2, a_hi, a_lo)
            ada_late(3, k)
        for q in range(3):
            group8(N_FF + 8 + 16 * q, a_hi, a_lo)
            if q == 0:
                ada_columns(B3, mrow_l, 8)
            group8(N_FF + 16 + 16 * q, f_hi[q % 2], f_lo[q % 2], "f_split", KT * q)
        for n in range(N_ALL - KT, N_ALL):
            products(n, n % 2, f_hi[1], f_lo[1], "f_split", KT * 3)
        total(1)
        nt = (WB - 1) * NQKV + (WA - 1) * KT
        pe.wait_ge(S["mod_done"], 4)
        pe.wait_ge(S["tails_done"], 2 + NQKV + KT)
        for g in range(2):
            T_.transpose(dp[0:nt, 2 + g, 0:P], tails[:, g, :], ident[:, :]).then_inc(S["tail_t"], 1)
        for t in range(5):
            rows_n = P if t < 4 else TS
            pe.wait_ge(S["yo_done"], Y_ACT * (min(t // 2, 2) + 1))
            pe.wait_ge(S["yo_done_v"], (KT - Y_ACT) * (min(t // 2, 2) + 1))
            if t >= 2:
                pe.wait_ge(S[("yt_done", "yt_done_v")[t % 2]], t // 2)
            for f in range(KT):
                last = T_.transpose(gp[0:rows_n, 2 * (t % 2) + f // 4, (f % 4) * P:(f % 4 + 1) * P],
                                    y_fm[:, f, t * P:t * P + rows_n], ident[:, :])
            last.then_inc(S["yt_ready"], 1)

    @block.scalar
    def _(act):
        AC = nc.scalar.activation
        ch = Chain(act, S["act_own"])

        def w_split(n, group, j):
            act.wait_ge(raw_full[j], 16 * (group + 1))
            AC(w_hi[:, j % 2, :, :], w_raw[:, j, :, :], ACT.Copy).then_inc(S["w_hi_done"], 1)

        def bank(b):
            return gp[:, 2 * b:2 * b + 2, 0:HALF]

        def halves(t):
            return t.rearrange("p (h c) -> p h c", h=2)

        act.wait_ge(S["vecs_done"], 1)
        for g, name in enumerate(("c_p", "c_s")):
            a0 = VEC[name][0]
            last = AC(c_act[:, :, g], vecs[:, a0:a0 + KT], ACT.Silu)
        last.then_inc(S["c_act"], 1)
        for f in range(KT):
            b = f % 2
            act.wait_ge(S["xt_done"], f + 1)
            if f >= 2:
                act.wait_ge(S["ss_all"], f - 1)
            else:
                act.wait_ge(S["pool_ready"], 1)
            AC(acc[:, b, 0:T], xT[:, f, :], ACT.Square).then_inc(S["sq_done"], 1)

        def ln_exp():
            act.preload_act_table_set("natural_log_exp_and_others")

        def rstd(out, banks, name, n, scale):
            act.wait_ge(S[name], n)
            for h, bk in enumerate(banks):
                ch.note(AC(out[:, h * HALF:(h + 1) * HALF], bk[:, 0:HALF], ACT.Ln, bias=bias[:, 2:3], scale=scale))
            ch.wait()
            return AC(out[:, :], out[:, :], ACT.Exp, scale=-0.5)

        act.wait_ge(S["ab_in"], 64)
        AC(ab_hi[:, :, :], ab_raw[:, :, :], ACT.Copy).then_inc(S["ab_hi_done"], 1)
        ln_exp()
        rstd(rstd1[:, :], (B0, B3), "ss_all", KT, 1.0 / D).then_inc(S["rstd_done"], 1)

        def ada_rows(bk, dst, n, r):
            act.wait_ge(S["ada0_used"] if r == 0 else S["ada_used"], n)
            AC(dst[:, :], bk[:, :], ACT.Copy).then_inc(S["ada_row_sb"], 1)

        ada_rows(B1, mrow, KT, 0)
        for j in range(2):
            w_split(j, 0, j)

        def modulated(k, r, b0):
            act.wait_ge(S["mod_done"], (1, 3)[k])
            for f in range(KT):
                act.wait_ge(S["t_done"], k * KT + f + 1)
                t = norm_buf[f % 4]
                ch.link(AC(t[:, 0:TP], t[:, 0:TP], ACT.Identity, scale=scales[:, k, f, 0:1],
                           bias=mod[:, r, b0 + f, 0:1]))
                AC(a_hi[:, f, :], t, ACT.Copy).then_inc(S["hi_split"], 1)

        modulated(0, 0, 0)
        def gates(part):
            if part == 0:
                act.wait_ge(S["ab_ready"], 1)
                ch.note(AC(ab_sb[0:CH, 0:HALF], B1[0:CH, 0:HALF], ACT.Copy))
                ch.link(AC(ab_sb[0:CH, HALF:T], B2[0:CH, 0:HALF], ACT.Copy))
                ch.note(AC(ab_sb[0:32, :], ab_sb[0:32, :], ACT.Identity, bias=bias[0:32, 0:1]))
                ch.link(AC(ab_sb[32:CH, :], ab_sb[32:CH, :], ACT.Copy, scale=-1.0))
            elif part == 1:
                ln_exp()
                ch.note(AC(bias[0:H, 4:5], bias[0:H, 1:2], ACT.Exp))
                ch.link(AC(ab_e[0:CH, :], ab_sb[0:CH, :], ACT.Abs))
                ch.link(AC(ab_e[0:CH, :], ab_e[0:CH, :], ACT.Exp, scale=-1.0))
                AC(ab_e[0:CH, :], ab_e[0:CH, :], ACT.Ln, bias=ones[0:CH, 0:1])
                AC(bias[0:H, 5:6], bias[0:H, 4:5], ACT.Copy, scale=-1.0).then_inc(S["row_a"], 1)
            elif part == 2:
                act.wait_ge(S["row_v"], 1)
                AC(rows[32:32 + H, :], ab_sp[32:32 + H, :], ACT.Exp, scale=-1.0)
                AC(row_b[0:H, :], ab_sp[32:32 + H, :], ACT.Exp, scale=-1.0)
                act.wait_ge(S["row_v"], 2)
                AC(row_e[0:H, :], rows[0:H, :], ACT.Exp).then_inc(S["row_a"], 1)
                AC(rows[64:64 + H, :], row_g[0:H, :], ACT.Exp).then_inc(S["row_a"], 1)

        def qkv_in(n, group, j):
            b = j % 2
            act.wait_ge(S["tile_done"], n + 1)
            act.wait_ge(S["tails_done"], n + 1)
            AC(xp[:, b, 3:3 + HALF], gp[:, 2 * b, 0:HALF], ACT.Copy)
            AC(xp[:, b, 3 + HALF:3 + TP], gp[:, 2 * b + 1, 0:TP - HALF], ACT.Copy)
            AC(xp[:, b, 6 + TP:6 + T], gp[:, 2 * b + 1, TP - HALF:HALF], ACT.Copy).then_inc(S["bank_free"], 1)
            w_split(n + 2, group + (j + 2) // 4, (j + 2) % 4)

        def qkv_out(n, b):
            act.wait_ge(S["conv_done"], n + 1)
            AC(qkv[:, n, 0:TP], acc[:, b, 0:TP], ACT.Silu)
            AC(qkv[:, n, TP:T], acc[:, b, TP + 3:T + 3], ACT.Silu).then_inc(S["acc_free"], 1)

        for n in range(4):
            qkv_in(n, 0, n)
            if n:
                qkv_out(n - 1, (n - 1) % 2)
            gates(n)
        def chunk_norms(c):
            act.wait_ge(S["ss_ready"], c + 1)
            for g, bk in enumerate((B0, B1)):
                ch.note(AC(sq[:, g], bk.rearrange("p (h i) -> p h i", h=H), ACT.Ln, bias=bias[:, 2:3]))
            ch.wait()
            AC(sq[:, 0], sq[:, 0], ACT.Exp, scale=-0.5)
            AC(sq[:, 1], sq[:, 1], ACT.Exp, scale=-0.5, bias=bias[:, 3:4]).then_inc(S["rkq_done"], 1)

        with act.Fori(1, NQKV // 4 - 1) as i:
            for j in range(4):
                qkv_in(4 * i + j, i, j)
                qkv_out(4 * i + j - 1, (j - 1) % 2)
        for j in range(4):
            n = NQKV - 4 + j
            qkv_in(n, n // 4, j)
            qkv_out(n - 1, (j - 1) % 2)
            if j == 1:
                ln_exp()
                chunk_norms(0)
        qkv_out(NQKV - 1, 1)

        def free(n, group, j):
            w_split(n + 2, group + (j + 2) // 4, (j + 2) % 4)

        def evac(n, b, out, func=ACT.Copy, scale=1.0, also=None, value=0):
            act.wait_ge(S["tile_done"], n + 1)
            if also:
                act.wait_ge(S[also], value)
            AC(halves(out), bank(b), func, scale=scale).then_inc(S["bank_free"], 1)

        def chunk_decay(c):
            act.wait_ge(S["dd_done"], c + 1)
            AC(dec, dec, ACT.Exp).then_inc(S["dec_done"], 1)

        def step_copy(c, l):
            act.wait_ge(S["p1_ready"], c * NEXP + l)
            AC(p1[:, :, :], B3[:, 0:HP * CH].rearrange("p (h i) -> p h i", h=HP), ACT.Copy).then_inc(S["p1_done"], 1)

        def chunk_out(c):
            act.wait_ge(S["vn_ready"], c + 1)
            AC(vn[:, :, :], B3.rearrange("p (h v) -> p h v", h=HP), ACT.Copy).then_inc(S["vn_done"], 1)
            act.wait_ge(S["o_ready"], c + 1)
            for hp in range(HP):
                ch.link(AC(o_sq[:, :], B0[:, hp * P:(hp + 1) * P], ACT.Square, accum_out=o_ss[:, hp:hp + 1]))
            ch.link(AC(o_ss[:, HP:2 * HP], o_ss[:, 0:HP], ACT.Ln, bias=bias[:, 2:3], scale=1.0 / P))
            AC(o_ss[:, HP:2 * HP], o_ss[:, HP:2 * HP], ACT.Exp, scale=-0.5).then_inc(S["o_rstd"], 1)
            act.wait_ge(S["o_turned"], c + 1)
            AC(Q[:, :, ds(c * CH, CH)], B1.rearrange("p (h i) -> p h i", h=H), ACT.Copy).then_inc(S["o_free"], 1)

        ln_exp()
        act.wait_ge(S["spilled"], 16)
        act.wait_ge(S["tails_done"], NQKV + 2)
        chunk_decay(0)
        with act.Fori(0, KT) as i:
            n0 = N_MIX + 4 * i
            ch.loop(i, 7)
            step_copy(i, 1)
            step_copy(i, 2)
            evac(n0, 0, xp[:, 0, 0:T], also="u_done", value=i + 1)
            free(n0, 6 + i, 0)
            step_copy(i, 3)
            step_copy(i, 4)
            evac(n0 + 1, 1, xp[:, 1, 0:T])
            free(n0 + 1, 6 + i, 1)
            step_copy(i, 5)
            chunk_out(i)
            evac(n0 + 2, 0, xp[:, 0, 0:T], also="prod_done", value=i + 1)
            free(n0 + 2, 6 + i, 2)
            chunk_norms(i + 1)
            chunk_decay(i + 1)
            evac(n0 + 3, 1, xT[:, i, :])
            free(n0 + 3, 6 + i, 3)
            ch.end(KT)

        act.wait_ge(S["kq_done"], NCH)
        act.wait_ge(S["vc_done"], NCH)
        for j, steps in enumerate(((1, 2), (3, 4), (5,), ())):
            n, t = N_TAIL + j, j // 2
            for l in steps:
                step_copy(KT, l)
            if j == 2:
                chunk_out(KT)
            evac(n, j % 2, (V, K)[j % 2][:, t, :])
            free(n, 14, j)
        for t in range(2):
            act.wait_ge(S["bank_free"], N_TAIL + 4 + 2)
            AC(V[:, t, :], V[:, t, :], ACT.Silu)
            AC(K[:, t, :], K[:, t, :], ACT.Tanh, scale=0.5)
            AC(xT[:, t, :], xT[:, t, :], ACT.Tanh, scale=0.5)
        def tail4(i, last=False):
            for j in range(4):
                n, t = N_TAIL + 4 * i + j, 2 * i + j // 2
                if j % 2 == 0:
                    evac(n, 0, V[:, t, :], ACT.Silu)
                    free(n, 14 + i, j)
                    AC(xT[:, t, :], xT[:, t, :], ACT.Tanh, scale=0.5)
                else:
                    evac(n, 1, K[:, t, :], ACT.Tanh, scale=0.5)
                    if not (last and j == 3):
                        free(n, 14 + i, j)

        with act.Fori(1, KT // 2 - 1) as i:
            tail4(i)
        ada_rows(B2, mrow_l, KT, 1)
        tail4(KT // 2 - 1, True)
        act.wait_ge(S["tile_done"], N_WA)
        act.wait_ge(S["u_done"], KT + 1)
        for t in range(KT):
            AC(a_hi[:, t, :], U[:, t, :], ACT.Copy).then_inc(S["u_hi"], 1)
            if t == 2:
                free(N_WA - 1, N_WA // 4 - 1, 3)

        def og_hi(t, e):
            act.wait_ge(S["og_done"], t + 1)
            AC(b_hi[:, t, :], og[e][:, :], ACT.Copy).then_inc(S["og_hi"], 1)

        ln_exp()
        act.wait_ge(S["u_split"], KT)
        with act.Fori(0, 2) as i:
            for j in range(4):
                n, b = N_WA + 4 * i + j, j % 2
                evac(n, b, xp[:, b, 0:T], scale=0.5, also="tmp_free", value=4 * i + j + 1)
                free(n, 18 + i, j)
                if j % 2 == 1:
                    og_hi(4 * i + j - 1, 0)
                    og_hi(4 * i + j, 1)
        with act.Fori(0, 2) as i:
            for j in range(4):
                n, b = N_WB + 4 * i + j, j % 2
                evac(n, b, xp[:, b, 0:T], scale=0.5, also="tmp_free", value=8 + 4 * i + j + 1)
                free(n, 20 + i, j)
                act.wait_ge(S["y_done"], 4 * i + j + 1)
                AC(a_hi[:, 4 * i + j, :], acc[:, b, 0:T], ACT.Copy).then_inc(S["y_hi"], 1)
        ada_rows(B2, mrow_l, 2 * KT, 2)

        def squared(t, n, m):
            act.wait_ge(S["tmp_free"], n - N_WA + 3)
            if t >= 2:
                act.wait_ge(S["added"], m * (KT - 2) + t - 1)
            AC(acc[:, min(t, 1), 0:T], xT[:, t, :], ACT.Square).then_inc(S["squared"], 1)

        act.wait_ge(S["y_split"], KT)
        for t in range(KT):
            n, b = N_WO + t, t % 2
            evac(n, b, xp[:, b, 0:T], also="tmp_free", value=16 + t + 1)
            squared(t, n, 0)
            free(n, 22 + t // 4, t % 4)
        rstd(rstd2[:, :], (B0, B1), "ss_all", KT + 1, 1.0 / D).then_inc(S["rstd_done"], 1)
        modulated(1, 1, KT)

        def ff1(q, n0):
            with act.Fori(0, 2) as i:
                for j in range(4):
                    n, b, t = n0 + 4 * i + j, j % 2, 4 * i + j
                    evac(n, b, xp[:, b, 0:T], also="tmp_free", value=n - N_WA + 1)
                    free(n, n0 // 4 + i, j)
                    act.wait_ge(S["tmp_free"], n - N_WA + 3)
                    AC(f_hi[q % 2][:, t, :], acc[:, b, 0:T], ACT.Copy).then_inc(S["f_hi_done"], 1)

        def ff2(q, n0):
            with act.Fori(0, 2) as i:
                for j in range(4):
                    n, b = n0 + 4 * i + j, j % 2
                    evac(n, b, xp[:, b, 0:T], also="tmp_free", value=n - N_WA + 1)
                    free(n, n0 // 4 + i, j)

        ff1(0, N_FF)
        ada_rows(B2, mrow_l, 3 * KT, 3)
        for q in range(3):
            ff1(q + 1, N_FF + 8 + 16 * q)
            ff2(q, N_FF + 16 + 16 * q)
        for t in range(KT):
            n, b = N_ALL - KT + t, t % 2
            evac(n, b, xp[:, b, 0:T], also="tmp_free", value=n - N_WA + 1)
            squared(t, n, 1)
            if n + 2 < N_ALL:
                free(n, n // 4, n % 4)
        rstd(rstd2[:, :], (B0, B1), "ss_all", KT + 2, 1.0 / D).then_inc(S["rstd_done"], 1)
        for g in range(2):
            nt = (WB - 1) * NQKV + (WA - 1) * KT
            act.wait_ge(S["tail_t"], g + 1)
            AC(tail_rows[g][0:nt, :], dp[0:nt, 2 + g, 0:P], ACT.Copy).then_inc(S["tail_sb"], 1)
        def y_affine(g, c):
            for f in range(Y_ACT):
                if f % 4 == 0:
                    act.wait_ge(S["y_norm"], 2 * g + f // 4 + 1)
                s_ = int(c.start >= TP)
                AC(y_fm[:, f, c], y_fm[:, f, c], ACT.Identity, scale=scales[:, 2, f, s_:s_ + 1],
                   bias=mod[:, 3, f, s_:s_ + 1]).then_inc(S["yo_done"], 1)

        y_affine(0, OUT[0])
        y_affine(1, OUT[1])
        for t in range(0, 5, 2):
            if t == 2:
                y_affine(2, OUT[2])
            rn = P if t < 4 else TS
            act.wait_ge(S["yt_ready"], t + 1)
            AC(y_tok[0:rn, t, :].rearrange("p (h c) -> p h c", h=2),
               gp[0:rn, 2 * (t % 2):2 * (t % 2) + 2, :], ACT.Copy)\
                .then_inc(S["yt_done"], 1)

    @block.vector
    def _(dve):
        V_ = nc.vector
        TT, TS_, STT = V_.tensor_tensor, V_.tensor_scalar, V_.scalar_tensor_tensor
        ch = Chain(dve, S["dve_own"])
        GR = ((0, slice(0, TP)), (1, slice(TP, T)))

        def lo_split(n, j):
            dve.wait_ge(S["w_hi_done"], n + 1)
            TT(w_lo[:, j % 2, :, :], w_raw[:, j, :, :], w_hi[:, j % 2, :, :].bitcast(F32), ALU.subtract)\
                .then_inc(S["w_lo_done"], 1)

        dve.wait_ge(S["vecs_t"], 1)
        V_.tensor_copy(vecs[:, :], B0[:, 0:NVEC]).then_inc(S["vecs_done"], 1)
        dve.wait_ge(S["vecs_done"], 1)
        V_.memset(B1, 0.0).then_inc(S["ada_row_sb"], 1)
        for f in range(KT):
            b = f % 2
            dve.wait_ge(S["xt_ready"], f + 1)
            V_.tensor_copy(xT[:, f, 0:TP], gp[:, 2 * b, 0:TP])
            V_.tensor_copy(xT[:, f, TP:T], gp[:, 2 * b + 1, 0:TS]).then_inc(S["xt_done"], 1)

        def columns(r, bk, bias_name, b0):
            dve.wait_ge(S["ada_t"], r + 1)
            a0 = VEC[bias_name][0] + b0
            src = bk.rearrange("p (s j q) -> p j s q", s=4, j=4)[:, :, :, 0:2]
            bs = vecs[:, a0:a0 + 16].rearrange("p (j s) -> p j s", j=4).unsqueeze(3).to_broadcast([P, 4, 4, 2])
            return TT(mod[:, r].rearrange("p (j s) g -> p j s g", j=4), src, bs, ALU.add)

        def scale_of(k, r, b0, gname):
            a0 = VEC[gname][0]
            g = vecs[:, a0:a0 + KT].unsqueeze(2).to_broadcast([P, KT, 2])
            ch.link(TS_(scales[:, k], mod[:, r, b0:b0 + KT, :], 1.0, None, ALU.add))
            return TT(scales[:, k], scales[:, k], g, ALU.mult)

        dve.wait_ge(S["ab_hi_done"], 1)
        TT(ab_lo[:, :, :], ab_raw[:, :, :], ab_hi[:, :, :].bitcast(F32), ALU.subtract).then_inc(S["ab_split"], 1)
        def scaled(rstd, k, f):
            if f >= 4:
                dve.wait_ge(S["h_ready"], k * KT + f - 3)
            ch.link(TT(norm_buf[f % 4], xT[:, f, :], rstd[:, :], ALU.mult))

        def sample(k, f):
            r, b0 = ((0, 0), (1, KT))[k]
            t = norm_buf[f % 4][:, TP:T]
            TS_(t, t, scales[:, k, f, 1:2], mod[:, r, b0 + f, 1:2], ALU.mult, ALU.add).then_inc(S["t_done"], 1)

        def norm(rstd, k):
            for f in range(KT):
                if f + 2 < KT:
                    scaled(rstd, k, f + 2)
                    sample(k, f + 2)
                dve.wait_ge(S["hi_split"], k * KT + f + 1)
                TT(a_lo[:, f, :], norm_buf[f % 4], a_hi[:, f, :].bitcast(F32), ALU.subtract)\
                    .then_inc(S["h_ready"], 1)
                if k == 0 and f < 2:
                    lo_split(f, f)

        dve.wait_ge(S["rstd_done"], 1)
        for f in range(2):
            scaled(rstd1, 0, f)
        ch.link(columns(0, B2, "ada_b", 0))
        scale_of(0, 0, KT, "norm1_g").then_inc(S["mod_done"], 1)
        dve.wait_ge(S["mod_done"], 1)
        for f in range(2):
            sample(0, f)
        norm(rstd1, 0)
        dve.wait_ge(S["h_ready"], KT)
        ch.link(V_.memset(xp[:, :, 0:3], 0.0))
        def gates(part):
            if part == 1:
                dve.wait_ge(S["row_a"], 1)
                ch.note(V_.memset(cmask[0:H, :], 1.0))
                ch.link(STT(ab_sp[0:CH, :], ab_sb[0:CH, :], 0.0, ab_e[0:CH, :], ALU.max, ALU.add))
                ch.note(V_.memset(cmask[0:H, :].rearrange("p (c i) -> p c i", i=CH)[:, :, 0:1], 0.0))
                TS_(row_g[0:H, :], ab_sp[0:H, :], bias[0:H, 5:6], None, ALU.mult).then_inc(S["row_v"], 1)
                dve.wait_ge(S["row_v"], 1)
                ch.wait()
                ch.link(V_.tensor_tensor_scan(rows[0:H, :], cmask[0:H, :], row_g[0:H, :], 0.0, ALU.mult, ALU.add))
                rv = rows[0:H, :].rearrange("p (c i) -> p c i", i=CH)
                TT(row_g[0:H, :].rearrange("p (c i) -> p c i", i=CH), rv[:, :, CH - 1:CH].to_broadcast([H, NCH, CH]),
                   rv, ALU.subtract).then_inc(S["row_v"], 1)
            elif part == 2:
                dve.wait_ge(S["row_a"], 2)
                TT(rows[96:96 + H, :], row_e[0:H, :], row_b[0:H, :], ALU.mult).then_inc(S["ab_rows"], 1)

        c0 = VEC["conv_qkv_w"][0]
        cw = vecs[:, c0:c0 + WB * NQKV].rearrange("p (j n) -> p j n", j=WB)
        W = TP + 3 + TS

        def conv(n, j, last=False):
            b = j % 2
            dve.wait_ge(S["bank_free"], n + 1 + 2)
            if not last:
                lo_split(n + 2, (j + 2) % 4)
            dve.wait_ge(S["pads_done"], n + 1)
            dve.wait_ge(S["acc_free"], n + 1)
            ch.link(TS_(acc[:, b, 0:W], xp[:, b, 0:W], cw[:, 0, ds(n, 1)], None, ALU.mult))
            for tap in range(1, WB):
                ins = STT(acc[:, b, 0:W], xp[:, b, tap:tap + W], cw[:, tap, ds(n, 1)], acc[:, b, 0:W],
                          ALU.mult, ALU.add)
                if tap < WB - 1:
                    ch.link(ins)
                else:
                    ins.then_inc(S["conv_done"], 1)
            if last:
                lo_split(n + 2, (j + 2) % 4)

        for n in range(4):
            conv(n, n)
            gates(n)
        V_.memset(st[:, :, :], 0.0).then_inc(S["s_done"], 1)
        with dve.Fori(1, NQKV // 4 - 1) as i:
            ch.loop(i - 1, 12)
            for j in range(4):
                conv(4 * i + j, j)
            ch.end(NQKV // 4 - 2)

        def chunk_scaled(c):
            dve.wait_ge(S["rkq_done"], c + 1)
            cols = ds(c * CH, CH) if not isinstance(c, int) else slice(c * CH, c * CH + CH)
            TT(kq[:, 0], K[:, :, cols], sq[:, 0], ALU.mult)
            TT(kq[:, 1], Q[:, :, cols], sq[:, 1], ALU.mult).then_inc(S["kq_done"], 1)

        for j in range(4):
            conv(NQKV - 4 + j, j, j == 3)
            if j == 1:
                dve.wait_ge(S["tok_t"], 1)
                V_.tensor_copy(tokv[:, :, :], B2[:, 0:NCH * 12].rearrange("p (c q) -> p c q", q=12))\
                    .then_inc(S["tok_done"], 1)
                chunk_scaled(0)
        dve.wait_ge(S["ab_rows"], 1)
        dve.wait_ge(S["row_a"], 3)
        dve.wait_ge(S["tok_done"], 1)
        V_.memset(bias[:, 7:8], 0.0).then_inc(S["u_done"], 1)

        def tok(c, q, n):
            return tokv[:, c, 4 * q:4 * q + 4].unsqueeze(2).to_broadcast([P, HP, n])

        def chunk_decay(c):
            dve.wait_ge(S["decs_in"], 32 * (c + 1))
            ch.link(TT(dec, dec, tok(c, 0, CH), ALU.subtract))
            TT(dec, dec, neg[:, :].unsqueeze(1).to_broadcast([P, HP, CH]), ALU.add)\
                .then_inc(S["dd_done"], 1)

        def chunk_beta(c):
            dve.wait_ge(S["dec_done"], c + 1)
            TT(decb, dec, decb, ALU.mult).then_inc(S["decb_done"], 1)
            dve.wait_ge(S["kq_done"], c + 1)
            dve.wait_ge(S["egs_in"], 16 * (c + 1))
            TT(kbe, kq[:, 0], kbe, ALU.mult).then_inc(S["kbe_done"], 1)

        def chunk_tokens(c):
            dve.wait_ge(S["tr_ready"], c + 1)
            TT(qd[:, :, :], kq[:, 1], eg, ALU.mult).then_inc(S["qd_done"], 1)
            dve.wait_ge(S["kkqk_ready"], c + 1)
            v = B2.rearrange("p (h e i) -> p h e i", h=HP, e=2)
            dve.wait_ge(S["decb_done"], c + 1)
            TT(at_[:, :, :], v[:, :, 0, :], decb, ALU.mult)
            TT(qkt[:, :, :], v[:, :, 1, :], dec, ALU.mult).then_inc(S["at_done"], 1)
            k_v, v_v = (x.rearrange("p (h d) -> p h d", h=HP) for x in (B0, B1))
            TT(kdt[:, :, :], k_v, tok(c, 2, P), ALU.mult)
            dve.wait_ge(S["nb_done"], c * LEVELS + 1)
            TT(mm[:, 1], nb[:, 0], id64[:, :].unsqueeze(1).to_broadcast([P, HP, CH]), ALU.add).then_inc(S["mt_done"], 1)
            TT(vb[:, :, :], v_v, tok(c, 1, P), ALU.mult).then_inc(S["tokmul_done"], 1)
            dve.wait_ge(S["m0_ready"], c + 1)
            V_.tensor_copy(mm[:, 0], B3[:, 0:HP * CH].rearrange("p (h i) -> p h i", h=HP)).then_inc(S["m0_done"], 1)
            dve.wait_ge(S["mt_done"], c + 1)
            dve.wait_ge(S["m0_done"], c + 1)

        def rhs(c):
            dve.wait_ge(S["ks_ready"], c + 1)
            TT(vb[:, :, :], vb[:, :, :], B0.rearrange("p (h d) -> p h d", h=HP), ALU.subtract)\
                .then_inc(S["rhs_done"], 1)

        def step_add(c, l):
            dve.wait_ge(S["x_ready"], c * NEXP + l)
            g = 0 if l < NEXP else 1
            TT(mm[:, g:2], mm[:, g:2], B2[:, g * HP * CH:].rearrange("p (g h i) -> p g h i", h=HP, i=CH), ALU.add)\
                .then_inc(S["m_done"], 1)
            dve.wait_ge(S["m_done"], c * NEXP + l)

        def o_scaled(c):
            dve.wait_ge(S["o_rstd"], c + 1)
            TT(o_tok[:, :, :], B0.rearrange("p (h v) -> p h v", h=HP),
               o_ss[:, HP:2 * HP].unsqueeze(2).to_broadcast([P, HP, P]), ALU.mult).then_inc(S["o_normed"], 1)

        def state(c):
            dve.wait_ge(S["ds_ready"], c + 1)
            for h in range(H):
                hp, bk = h // 2, (B2, B3)[h % 2]
                last = STT(st[:, h, :], st[:, h, :], eg[:, h, CH - 1:CH], bk[:, hp * P:(hp + 1) * P], ALU.mult, ALU.add)
            last.then_inc(S["s_done"], 1)
            dve.wait_ge(S["s_done"], c + 2)

        c0 = VEC["conv_a_w"][0]
        caw = vecs[:, c0:c0 + WA * KT].rearrange("p (j n) -> p j n", j=WA)
        WM = TP + 2 + TS
        chunk_decay(0)
        chunk_beta(0)
        with dve.Fori(0, KT) as i:
            n0 = N_MIX + 4 * i
            ch.loop(i, 3)
            chunk_tokens(i)
            step_add(i, 1)
            rhs(i)
            step_add(i, 2)
            lo_split(n0 + 2, 2)
            step_add(i, 3)
            dve.wait_ge(S["bank_free"], n0 + 1 + 3)
            dve.wait_ge(S["pads_a"], i + 1)
            dve.wait_ge(S["tails_done"], 2 + NQKV + i)
            TT(acc[:, 0, 2:2 + TP], xp[:, 0, 0:TP], xp[:, 1, 0:TP], ALU.mult)
            TT(acc[:, 0, 4 + TP:4 + T], xp[:, 0, TP:T], xp[:, 1, TP:T], ALU.mult).then_inc(S["prod_done"], 1)
            step_add(i, 4)
            lo_split(n0 + 3, 3)
            step_add(i, 5)
            dve.wait_ge(S["prod_done"], i + 1)
            ch.link(TS_(acc[:, 1, 0:WM], acc[:, 0, 0:WM], caw[:, 0, ds(i, 1)], None, ALU.mult))
            ch.link(STT(acc[:, 1, 0:WM], acc[:, 0, 1:1 + WM], caw[:, 1, ds(i, 1)], acc[:, 1, 0:WM], ALU.mult, ALU.add))
            STT(acc[:, 1, 0:WM], acc[:, 0, 2:2 + WM], caw[:, 2, ds(i, 1)], acc[:, 1, 0:WM], ALU.mult, ALU.add)\
                .then_inc(S["prod_free"], 1)
            o_scaled(i)
            state(i)
            chunk_decay(i + 1)
            lo_split(n0 + 4, 0)
            dve.wait_ge(S["bank_free"], n0 + 2 + 3)
            dve.wait_ge(S["prod_free"], i + 2)
            TT(U[:, i, 0:TP], acc[:, 1, 0:TP], xp[:, 0, 0:TP], ALU.mult)
            TT(U[:, i, TP:T], acc[:, 1, TP + 2:T + 2], xp[:, 0, TP:T], ALU.mult).then_inc(S["u_done"], 1)
            chunk_scaled(i + 1)
            chunk_beta(i + 1)
            lo_split(n0 + 5, 1)
            ch.end(KT)

        chunk_tokens(KT)
        step_add(KT, 1)
        step_add(KT, 2)
        lo_split(N_TAIL + 2, 2)
        step_add(KT, 3)
        step_add(KT, 4)
        lo_split(N_TAIL + 3, 3)
        dve.wait_ge(S["s_in"], 16)
        rhs(KT)
        step_add(KT, 5)
        o_scaled(KT)
        state(KT)
        lo_split(N_TAIL + 4, 0)
        lo_split(N_TAIL + 5, 1)
        V_.memset(B2, 0.0).then_inc(S["ada_row_sb"], 1)
        with dve.Fori(1, KT // 2 - 1) as i:
            for j in range(4):
                lo_split(N_TAIL + 4 * i + j + 2, (j + 2) % 4)
        for j in range(3):
            lo_split(N_WA - 4 + j + 2, (j + 2) % 4)
            if j == 2:
                columns(1, B3, "ada_b", 16).then_inc(S["mod_done"], 1)
        for t in range(KT):
            dve.wait_ge(S["u_hi"], t + 1)
            TT(a_lo[:, t, :], U[:, t, :], a_hi[:, t, :].bitcast(F32), ALU.subtract).then_inc(S["u_split"], 1)
            if t == 2:
                lo_split(N_WA + 1, 1)

        og_g = vec("out_g")
        dve.wait_ge(S["s_out"], 32)
        dve.wait_ge(S["o_free"], NCH + 1)
        with dve.Fori(0, 2) as i:
            for j in range(4):
                t, b = 4 * i + j, j % 2
                n = N_WA + t
                dve.wait_ge(S["bank_free"], n + 1 + 2)
                STT(xT[:, t, :], xT[:, t, :], 1.0, xp[:, b, 0:T], ALU.add, ALU.mult).then_inc(S["tmp_free"], 1)
                lo_split(n + 2, (j + 2) % 4)
                if j % 2 == 0:
                    dve.wait_ge(S["og_split"], t + 1)
                    for e in range(2):
                        STT(og[e][:, :], Q[:, t + e, :], og_g, V[:, t + e, :], ALU.mult, ALU.mult)\
                            .then_inc(S["og_done"], 1)
                else:
                    for e in range(2):
                        dve.wait_ge(S["og_hi"], t + e)
                        TT(b_lo[:, t - 1 + e, :], og[e][:, :], b_hi[:, t - 1 + e, :].bitcast(F32), ALU.subtract)\
                            .then_inc(S["og_split"], 1)

        V_.memset(B2, 0.0).then_inc(S["ada_row_sb"], 1)
        with dve.Fori(0, 2) as i:
            for j in range(4):
                t, b = 4 * i + j, j % 2
                n = N_WB + t
                dve.wait_ge(S["bank_free"], n + 1 + 2)
                ins = STT(acc[:, b, 0:T], K[:, t, :], 1.0, xp[:, b, 0:T], ALU.add, ALU.mult)
                ins.then_inc(S["tmp_free"], 1)
                dve.wait_ge(S["tmp_free"], 2 + KT + t + 1)
                TT(acc[:, b, 0:T], acc[:, b, 0:T], xT[:, t, :], ALU.add).then_inc(S["y_done"], 1)
                lo_split(n + 2, (j + 2) % 4)
                dve.wait_ge(S["y_hi"], t + 1)
                TT(a_lo[:, t, :], acc[:, b, 0:T], a_hi[:, t, :].bitcast(F32), ALU.subtract).then_inc(S["y_split"], 1)
        dve.wait_ge(S["mod_done"], 2)
        dve.wait_ge(S["x_back_in"], 16)

        def add_square(t, m):
            if 0 < t < KT - 1:
                dve.wait_ge(S["squared"], KT * m + t + 1)
                TT(acc[:, 0, 0:T], acc[:, 0, 0:T], acc[:, 1, 0:T], ALU.add).then_inc(S["added"], 1)
                dve.wait_ge(S["added"], m * (KT - 2) + t)

        for t in range(KT):
            n, b = N_WO + t, t % 2
            dve.wait_ge(S["bank_free"], n + 1 + 2)
            for g, c in GR:
                last = STT(xT[:, t, c], xp[:, b, c], mod[:, 1, t, g:g + 1], x_back[:, t, c], ALU.mult, ALU.add)
            last.then_inc(S["tmp_free"], 1)
            add_square(t, 0)
            lo_split(n + 2, (n + 2) % 4)
            if t == 2:
                ch.link(columns(2, B3, "ada_b", 32))
                scale_of(1, 2, 0, "norm2_g").then_inc(S["mod_done"], 1)
                dve.wait_ge(S["mod_done"], 3)
                V_.memset(B2, 0.0).then_inc(S["ada_row_sb"], 1)
        dve.wait_ge(S["rstd_done"], 2)
        dve.wait_ge(S["tmp_free"], 2 + 3 * KT)
        for f in range(2):
            scaled(rstd2, 1, f)
            sample(1, f)
        norm(rstd2, 1)

        def ff1(q, n0):
            with dve.Fori(0, 2) as i:
                for j in range(4):
                    n, b, t = n0 + 4 * i + j, j % 2, 4 * i + j
                    dve.wait_ge(S["bank_free"], n + 1 + 2)
                    STT(acc[:, b, 0:T], xp[:, b, 0:T], 0.0, xp[:, b, 0:T], ALU.max, ALU.mult).then_inc(S["tmp_free"], 1)
                    lo_split(n + 2, (j + 2) % 4)
                    dve.wait_ge(S["f_hi_done"], KT * q + t + 1)
                    TT(f_lo[q % 2][:, t, :], acc[:, b, 0:T], f_hi[q % 2][:, t, :].bitcast(F32), ALU.subtract)\
                        .then_inc(S["f_split"], 1)

        def add_residual(t, b):
            for g, c in GR:
                last = STT(xT[:, t, c], xp[:, b, c], mod_c(t, g), xT[:, t, c], ALU.mult, ALU.add)
            return last

        def mod_c(t, g):
            return mod[:, 2, ds(t + KT, 1), g] if not isinstance(t, int) else mod[:, 2, t + KT:t + KT + 1, g]

        def ff2(q, n0):
            with dve.Fori(0, 2) as i:
                for j in range(4):
                    n, b, t = n0 + 4 * i + j, j % 2, 4 * i + j
                    dve.wait_ge(S["bank_free"], n + 1 + 2)
                    add_residual(t, b).then_inc(S["tmp_free"], 1)
                    lo_split(n + 2, (j + 2) % 4)

        ff1(0, N_FF)
        for q in range(3):
            ff1(q + 1, N_FF + 8 + 16 * q)
            if q == 0:
                ch.link(columns(3, B3, "final_b", 0))
                scale_of(2, 3, KT, "final_g").then_inc(S["mod_done"], 1)
            ff2(q, N_FF + 16 + 16 * q)
        for t in range(KT):
            n, b = N_ALL - KT + t, t % 2
            dve.wait_ge(S["bank_free"], n + 1 + 2)
            add_residual(t, b).then_inc(S["tmp_free"], 1)
            add_square(t, 1)
            if n + 2 < N_ALL:
                lo_split(n + 2, (n + 2) % 4)
        dve.wait_ge(S["rstd_done"], 3)
        dve.wait_ge(S["tmp_free"], 2 + 11 * KT)
        for g, c in enumerate(OUT):
            for q in range(2):
                f = slice(4 * q, 4 * q + 4)
                w = c.stop - c.start
                TT(y_fm[:, f, c], xT[:, f, c], rstd2[:, c].unsqueeze(1).to_broadcast([P, 4, w]), ALU.mult)\
                    .then_inc(S["y_norm"], 1)
            dve.wait_ge(S["y_norm"], 2 * g + 2)
            s_ = int(c.start >= TP)
            for f in range(Y_ACT, KT):
                TS_(y_fm[:, f, c], y_fm[:, f, c], scales[:, 2, f, s_:s_ + 1], mod[:, 3, f, s_:s_ + 1],
                    ALU.mult, ALU.add).then_inc(S["yo_done_v"], 1)
        for t in range(1, 5, 2):
            dve.wait_ge(S["yt_ready"], t + 1)
            V_.tensor_copy(y_tok[:, t, :].rearrange("p (h c) -> p h c", h=2), gp[:, 2:4, :])\
                .then_inc(S["yt_done_v"], 1)

    block.__exit__(None, None, None)


_INS = ["x_prompt", "x_sample", "cache_conv_a", "cache_conv_qkv", "state_delta", "c_prompt", "c_sample", "ada_w",
        "ada_b", "norm1_g", "norm2_g", "w_in", "conv_a_w", "conv_qkv_w", "a_log", "dt_bias", "out_norm_g",
        "w_a_out", "w_b_out", "w_o", "w_ff1", "w_ff2", "final_ada_w", "final_ada_b", "final_norm_g"]
_OUTS = [("y_p", (1, TP, D)), ("y_s", (1, TS, D)),
         ("ca_p", (1, 1, WA - 1, D)), ("cq_p", (1, 1, WB - 1, 3 * D)), ("s_p", (1, 1, H, P, P)),
         ("ca_s", (1, 1, WA - 1, D)), ("cq_s", (1, 1, WB - 1, 3 * D)), ("s_s", (1, 1, H, P, P))]


def kernel(**inputs):
    import numpy as _np
    import concourse.bacc as _bacc
    from concourse import mybir as _mybir
    from concourse.bass_utils import run_bass_kernel_spmd as _run

    nc = _bacc.Bacc("TRN2", target_bir_lowering=False, num_devices=1)
    arrays, t_in, t_out = {}, {}, {}
    for name in _INS:
        a = _np.ascontiguousarray(inputs[name])
        arrays[f"in_{name}"] = a
        t_in[name] = nc.dram_tensor(f"in_{name}", a.shape, _mybir.dt.from_np(a.dtype), kind="ExternalInput").ap()
    for name, shape in _OUTS:
        t_out[name] = nc.dram_tensor(f"out_{name}", shape, _mybir.dt.float32, kind="ExternalOutput").ap()
    build(nc, t_in, t_out)
    r = _run(nc, [arrays], core_ids=[0])
    return tuple(r.results[0][f"out_{name}"] for name, _ in _OUTS)
```
